# Optimizing a Trainium2 kernel written in Bass

```python
import numpy as np
import jax
import jax.numpy as jnp
from jax import lax

D_MODEL = 1024
BATCH = 1
SEQ = 256
DEPTH = 2

HEAD_DIM = 64
ROT_DIM = HEAD_DIM // 4
ROPE_THETA = 500000.0
Q_BLOCK = 128
NEG = -1e30
EPS = 1e-6

NSA_HEADS = 8
NSA_GROUPS = 2
NSA_REP = NSA_HEADS // NSA_GROUPS
CMP_LEN = 32
CMP_STRIDE = 16
CMP_HIDDEN = 256
SEL_LEN = 64
SEL_BLOCKS = 16
WINDOW = 512

DSA_HEADS = 8
IDX_HEADS = 8
IDX_DIM = 64
DSA_TOPK = 256

PEER_HEADS = 8
PEER_QDIM = 256
N_KEYS = 128
N_EXPERTS = N_KEYS * N_KEYS
PEER_HALF_TOPK = 16
PEER_TOPK = 16
PEER_TOKEN_BLOCK = 128

PLE_DIM = 256

MIX_A = NSA_HEADS * HEAD_DIM
MIX_B = DSA_HEADS * HEAD_DIM
IN_SIZES = (
    MIX_A,
    6 * NSA_GROUPS * HEAD_DIM,
    3 * NSA_HEADS,
    MIX_B,
    2 * HEAD_DIM,
    IDX_HEADS * IDX_DIM,
    IDX_DIM,
    IDX_HEADS,
    2 * D_MODEL,
)
IN_COLS = sum(IN_SIZES)

kernel_name = 'hybrid_nsa_dsa_peer_ple'

def _rms(x):
    xf = x.astype(jnp.float32)
    return xf * lax.rsqrt(jnp.mean(xf * xf, axis=-1, keepdims=True) + EPS)

def rms_norm(x, g):
    return (_rms(x) * g.astype(jnp.float32)).astype(x.dtype)

def rope(x, pos):
    half = ROT_DIM // 2
    inv = ROPE_THETA ** (-jnp.arange(half, dtype=jnp.float32) / half)
    ang = pos.astype(jnp.float32)[..., None] * inv
    cos = jnp.cos(ang)[:, :, None, :]
    sin = jnp.sin(ang)[:, :, None, :]
    xf = x.astype(jnp.float32)
    x1, x2, rest = xf[..., :half], xf[..., half:ROT_DIM], xf[..., ROT_DIM:]
    return jnp.concatenate([x1 * cos - x2 * sin, x2 * cos + x1 * sin, rest], axis=-1).astype(x.dtype)

def masked_softmax(s, mask):
    p = jax.nn.softmax(jnp.where(mask, s, NEG), axis=-1)
    return jnp.where(mask, p, 0.0)

def compress(t, pos_emb, w1, w2):
    b, s, g, d = t.shape
    r = CMP_LEN // CMP_STRIDE
    n_chunk = s // CMP_STRIDE
    n_cmp = n_chunk - r + 1
    c = t.reshape(b, n_chunk, CMP_STRIDE, g, d)
    blocks = jnp.concatenate([c[:, j:j + n_cmp] for j in range(r)], axis=2)
    blocks = blocks + pos_emb[None, None, :, None, :].astype(t.dtype)
    flat = blocks.transpose(0, 1, 3, 2, 4).reshape(b, n_cmp, g, CMP_LEN * d)
    return jax.nn.gelu(flat @ w1) @ w2

def nsa_attention(q, kc, vc, ks, vs, kw, vw, gates):
    b, s = q.shape[0], q.shape[1]
    n_cmp = kc.shape[1]
    n_sel_blocks = s // SEL_LEN
    n_top = min(SEL_BLOCKS, n_sel_blocks)
    scale = HEAD_DIM ** -0.5
    dt = q.dtype
    cmp_end = jnp.asarray(np.arange(n_cmp) * CMP_STRIDE + CMP_LEN - 1)
    ci = np.arange(n_cmp)[:, None] * CMP_STRIDE
    sj = np.arange(n_sel_blocks)[None, :] * SEL_LEN
    overlap = jnp.asarray(((ci < sj + SEL_LEN) & (ci + CMP_LEN > sj)).astype(np.float32))
    ks_blk = ks.reshape(b, n_sel_blocks, SEL_LEN, NSA_GROUPS, HEAD_DIM).transpose(0, 3, 1, 2, 4)
    vs_blk = vs.reshape(b, n_sel_blocks, SEL_LEN, NSA_GROUPS, HEAD_DIM).transpose(0, 3, 1, 2, 4)
    kw_pad = jnp.pad(kw, ((0, 0), (WINDOW, 0), (0, 0), (0, 0)))
    vw_pad = jnp.pad(vw, ((0, 0), (WINDOW, 0), (0, 0), (0, 0)))
    bix = jnp.arange(b)[:, None, None, None]
    gix = jnp.arange(NSA_GROUPS)[None, :, None, None]
    blk_ids = jnp.arange(n_sel_blocks)
    in_blk = jnp.arange(SEL_LEN)
    win_off = jnp.arange(WINDOW + Q_BLOCK) - WINDOW

    def block(bi):
        q0 = bi * Q_BLOCK
        t = q0 + jnp.arange(Q_BLOCK)
        qg = lax.dynamic_slice_in_dim(q, q0, Q_BLOCK, 1).reshape(b, Q_BLOCK, NSA_GROUPS, NSA_REP, HEAD_DIM)
        s_c = jnp.einsum('bqgrd,bngd->bgrqn', qg, kc).astype(jnp.float32) * scale
        p_c = masked_softmax(s_c, cmp_end[None, :] <= t[:, None])
        o_c = jnp.einsum('bgrqn,bngd->bqgrd', p_c.astype(dt), vc)
        imp = jnp.einsum('bgrqn,nj->bgqj', p_c, overlap)
        cur = (t // SEL_LEN)[:, None]
        forced = (blk_ids[None] == 0) | (blk_ids[None] == cur) | (blk_ids[None] == cur - 1)
        imp = jnp.where(forced, jnp.inf, imp)
        imp = jnp.where(blk_ids[None] * SEL_LEN <= t[:, None], imp, -jnp.inf)
        _, sel = lax.top_k(imp, n_top)
        k_g = ks_blk[bix, gix, sel].reshape(b, NSA_GROUPS, Q_BLOCK, n_top * SEL_LEN, HEAD_DIM)
        v_g = vs_blk[bix, gix, sel].reshape(b, NSA_GROUPS, Q_BLOCK, n_top * SEL_LEN, HEAD_DIM)
        key_pos = (sel[..., None] * SEL_LEN + in_blk).reshape(b, NSA_GROUPS, 1, Q_BLOCK, n_top * SEL_LEN)
        s_s = jnp.einsum('bqgrd,bgqmd->bgrqm', qg, k_g).astype(jnp.float32) * scale
        p_s = masked_softmax(s_s, key_pos <= t[:, None])
        o_s = jnp.einsum('bgrqm,bgqmd->bqgrd', p_s.astype(dt), v_g)
        k_w = lax.dynamic_slice_in_dim(kw_pad, q0, WINDOW + Q_BLOCK, 1)
        v_w = lax.dynamic_slice_in_dim(vw_pad, q0, WINDOW + Q_BLOCK, 1)
        kpos = q0 + win_off
        diff = t[:, None] - kpos[None, :]
        mask_w = (kpos[None, :] >= 0) & (diff >= 0) & (diff < WINDOW)
        s_w = jnp.einsum('bqgrd,bkgd->bgrqk', qg, k_w).astype(jnp.float32) * scale
        p_w = masked_softmax(s_w, mask_w)
        o_w = jnp.einsum('bgrqk,bkgd->bqgrd', p_w.astype(dt), v_w)
        g = lax.dynamic_slice_in_dim(gates, q0, Q_BLOCK, 1)[..., None]
        o = g[:, :, 0] * o_c + g[:, :, 1] * o_s + g[:, :, 2] * o_w
        return o.reshape(b, Q_BLOCK, MIX_A)

    out = lax.map(block, jnp.arange(s // Q_BLOCK))
    return out.transpose(1, 0, 2, 3).reshape(b, s, MIX_A)

def dsa_attention(q, k, v, iq, ik, iw):
    b, s = q.shape[0], q.shape[1]
    n_keep = min(DSA_TOPK, s // 4)
    scale = HEAD_DIM ** -0.5
    dt = q.dtype
    key_pos = jnp.arange(s)
    bix = jnp.arange(b)[:, None, None]

    def block(bi):
        q0 = bi * Q_BLOCK
        t = q0 + jnp.arange(Q_BLOCK)
        qb = lax.dynamic_slice_in_dim(q, q0, Q_BLOCK, 1)
        iqb = lax.dynamic_slice_in_dim(iq, q0, Q_BLOCK, 1)
        iwb = lax.dynamic_slice_in_dim(iw, q0, Q_BLOCK, 1).astype(jnp.float32) * IDX_HEADS ** -0.5
        logits = jnp.einsum('bqhd,bsd->bqhs', iqb, ik).astype(jnp.float32) * IDX_DIM ** -0.5
        score = jnp.einsum('bqhs,bqh->bqs', jax.nn.relu(logits), iwb)
        score = jnp.where(key_pos[None, None, :] <= t[None, :, None], score, -jnp.inf)
        _, sel = lax.top_k(score, n_keep)
        k_g = k[bix, sel]
        v_g = v[bix, sel]
        att = jnp.einsum('bqhd,bqkd->bhqk', qb, k_g).astype(jnp.float32) * scale
        p = masked_softmax(att, (sel <= t[None, :, None])[:, None])
        o = jnp.einsum('bhqk,bqkd->bqhd', p.astype(dt), v_g)
        return o.reshape(b, Q_BLOCK, MIX_B)

    out = lax.map(block, jnp.arange(s // Q_BLOCK))
    return out.transpose(1, 0, 2, 3).reshape(b, s, MIX_B)

def peer(h, wq, sub_keys, u, v):
    b, s, d = h.shape
    dt = h.dtype
    tok = h.reshape(b * s // PEER_TOKEN_BLOCK, PEER_TOKEN_BLOCK, d)

    def block(xb):
        q = (xb @ wq).reshape(PEER_TOKEN_BLOCK, PEER_HEADS, 2, PEER_QDIM // 2)
        s1 = jnp.einsum('thd,kd->thk', q[:, :, 0], sub_keys[0]).astype(jnp.float32)
        s2 = jnp.einsum('thd,kd->thk', q[:, :, 1], sub_keys[1]).astype(jnp.float32)
        v1, i1 = lax.top_k(s1, PEER_HALF_TOPK)
        v2, i2 = lax.top_k(s2, PEER_HALF_TOPK)
        cand = (v1[..., :, None] + v2[..., None, :]).reshape(PEER_TOKEN_BLOCK, PEER_HEADS, -1)
        cidx = (i1[..., :, None] * N_KEYS + i2[..., None, :]).reshape(PEER_TOKEN_BLOCK, PEER_HEADS, -1)
        top, pos = lax.top_k(cand, PEER_TOPK)
        eidx = jnp.take_along_axis(cidx, pos, axis=-1)
        gate = jax.nn.softmax(top, axis=-1)
        act = jax.nn.gelu(jnp.einsum('td,thkd->thk', xb, u[eidx]).astype(jnp.float32))
        return jnp.einsum('thk,thkd->td', (gate * act).astype(dt), v[eidx])

    return lax.map(block, tok).reshape(b, s, d)

def hybrid_layer(x, p_i, positions, attn_norm, w_in, nsa_qk_gain, cmp_pos, cmp_w1, cmp_w2,
                 dsa_qk_gain, w_branch_a, w_branch_b, w_out, ffn_norm, peer_wq, peer_sub_keys,
                 peer_u, peer_v, ple_w, ple_gate_w, ple_norm):
    b, s, _ = x.shape
    h = rms_norm(x, attn_norm)
    proj = h @ w_in
    cuts = np.cumsum(IN_SIZES)[:-1].tolist()
    nq, nkv, ngate, dq, dkv, iq, ik, iw, mg = jnp.split(proj, cuts, axis=-1)

    qa = rope(rms_norm(nq.reshape(b, s, NSA_HEADS, HEAD_DIM), nsa_qk_gain[0]), positions)
    kv = nkv.reshape(b, s, 6, NSA_GROUPS, HEAD_DIM)
    kc = compress(kv[:, :, 0], cmp_pos[0], cmp_w1[0], cmp_w2[0])
    vc = compress(kv[:, :, 1], cmp_pos[1], cmp_w1[1], cmp_w2[1])
    n_cmp = kc.shape[1]
    cmp_pos_ids = positions[:, CMP_LEN - 1::CMP_STRIDE][:, :n_cmp]
    kc = rope(rms_norm(kc, nsa_qk_gain[1]), cmp_pos_ids)
    ks = rope(rms_norm(kv[:, :, 2], nsa_qk_gain[2]), positions)
    kw = rope(rms_norm(kv[:, :, 4], nsa_qk_gain[3]), positions)
    gates = jax.nn.sigmoid(ngate).reshape(b, s, 3, NSA_GROUPS, NSA_REP)
    ya = nsa_attention(qa, kc, vc, ks, kv[:, :, 3], kw, kv[:, :, 5], gates)

    qb = rope(rms_norm(dq.reshape(b, s, DSA_HEADS, HEAD_DIM), dsa_qk_gain[0]), positions)
    dkv = dkv.reshape(b, s, 2, HEAD_DIM)
    kb = rope(rms_norm(dkv[:, :, :1], dsa_qk_gain[1]), positions)[:, :, 0]
    vb = dkv[:, :, 1]
    iq = rope(iq.reshape(b, s, IDX_HEADS, IDX_DIM), positions)
    ik = rope(ik[:, :, None], positions)[:, :, 0]
    yb = dsa_attention(qb, kb, vb, iq, ik, iw)

    ga, gb = jnp.split(jax.nn.sigmoid(mg), 2, axis=-1)
    x = x + (ga * (ya @ w_branch_a) + gb * (yb @ w_branch_b)) @ w_out

    x = x + peer(rms_norm(x, ffn_norm), peer_wq, peer_sub_keys, peer_u, peer_v)

    gate = jax.nn.sigmoid(_rms(x).astype(x.dtype) @ ple_gate_w)
    return x + gate * rms_norm(p_i @ ple_w, ple_norm)

def setup_inputs(seed: int = 0) -> dict:
    key = jax.random.key(seed)
    ks = jax.random.split(key, 24)
    f32 = jnp.float32
    L = DEPTH

    def nrm(k, shape, scale):
        return jax.random.normal(k, shape, f32) * scale

    def gain(k, shape):
        return 1.0 + 0.05 * jax.random.normal(k, shape, f32)

    offset = jax.random.randint(ks[2], (BATCH, 1), 0, 1024, dtype=jnp.int32)
    positions = offset + jnp.arange(SEQ, dtype=jnp.int32)[None, :]
    return {
        'x': nrm(ks[0], (BATCH, SEQ, D_MODEL), 1.0),
        'p': nrm(ks[1], (DEPTH, BATCH, SEQ, PLE_DIM), 1.0),
        'positions': positions,
        'attn_norm': gain(ks[3], (L, D_MODEL)),
        'w_in': nrm(ks[4], (L, D_MODEL, IN_COLS), D_MODEL ** -0.5),
        'nsa_qk_gain': gain(ks[5], (L, 4, HEAD_DIM)),
        'cmp_pos': nrm(ks[6], (L, 2, CMP_LEN, HEAD_DIM), 0.1),
        'cmp_w1': nrm(ks[7], (L, 2, CMP_LEN * HEAD_DIM, CMP_HIDDEN), (CMP_LEN * HEAD_DIM) ** -0.5),
        'cmp_w2': nrm(ks[8], (L, 2, CMP_HIDDEN, HEAD_DIM), CMP_HIDDEN ** -0.5),
        'dsa_qk_gain': gain(ks[9], (L, 2, HEAD_DIM)),
        'w_branch_a': nrm(ks[10], (L, MIX_A, D_MODEL), MIX_A ** -0.5),
        'w_branch_b': nrm(ks[11], (L, MIX_B, D_MODEL), MIX_B ** -0.5),
        'w_out': nrm(ks[12], (L, D_MODEL, D_MODEL), 0.5 * D_MODEL ** -0.5),
        'ffn_norm': gain(ks[13], (L, D_MODEL)),
        'peer_wq': nrm(ks[14], (L, D_MODEL, PEER_HEADS * PEER_QDIM), D_MODEL ** -0.5),
        'peer_sub_keys': nrm(ks[15], (L, 2, N_KEYS, PEER_QDIM // 2), (PEER_QDIM // 2) ** -0.5),
        'peer_u': nrm(ks[16], (L, N_EXPERTS, D_MODEL), D_MODEL ** -0.5),
        'peer_v': nrm(ks[17], (L, N_EXPERTS, D_MODEL), PEER_HEADS ** -0.5),
        'ple_w': nrm(ks[18], (L, PLE_DIM, D_MODEL), PLE_DIM ** -0.5),
        'ple_gate_w': nrm(ks[19], (L, D_MODEL, D_MODEL), D_MODEL ** -0.5),
        'ple_norm': gain(ks[20], (L, D_MODEL)),
    }

def reference(x, p, positions, attn_norm, w_in, nsa_qk_gain, cmp_pos, cmp_w1, cmp_w2,
              dsa_qk_gain, w_branch_a, w_branch_b, w_out, ffn_norm, peer_wq, peer_sub_keys,
              peer_u, peer_v, ple_w, ple_gate_w, ple_norm):
    for i in range(DEPTH):
        x = hybrid_layer(x, p[i], positions, attn_norm[i], w_in[i], nsa_qk_gain[i], cmp_pos[i],
                         cmp_w1[i], cmp_w2[i], dsa_qk_gain[i], w_branch_a[i], w_branch_b[i],
                         w_out[i], ffn_norm[i], peer_wq[i], peer_sub_keys[i], peer_u[i],
                         peer_v[i], ple_w[i], ple_gate_w[i], ple_norm[i])
    return x


_drawn_inputs = setup_inputs


def setup_inputs(seed=0):
    import zlib

    import numpy as np

    out = dict(_drawn_inputs(seed))
    spreads = {}
    factors = {'nsa_qk_gain': 3.166, 'dsa_qk_gain': 2.887}
    for name, (base, spread) in spreads.items():
        noise = np.random.default_rng([zlib.crc32(name.encode()), seed]).standard_normal(out[name].shape)
        drawn = base * np.exp(spread * noise) if base else spread * noise
        out[name] = jnp.asarray(drawn.astype(out[name].dtype))
    for name, factor in factors.items():
        out[name] = (out[name] * factor).astype(out[name].dtype)
    return out
```

```python
from contextlib import ExitStack

import concourse.bass as bass
from concourse import mybir

F32 = mybir.dt.float32
BF16 = mybir.dt.bfloat16
I32 = mybir.dt.int32
U32 = mybir.dt.uint32
ALU = mybir.AluOpType
ACT = mybir.ActivationFunctionType
AX = mybir.AxisListType

P = 128
DEPTH, SEQ, D = 2, 256, 1024
NT = SEQ // P
NK = D // P
HD = 64
HEADS = 8
ROT2 = HD // 8
EPS = 1e-6
NEG = -1e30
GONE = -3e38
SCALE = HD ** -0.5
CMP_STRIDE, CMP_LEN, NCMP = 16, 32, 15
CP = 16
TOPK_ROUNDS = 64 // 8
PICKS = 16
NKEYS = 128
PLE = 256

C_NQ, C_KS, C_KW, C_DQ, C_KB, C_IQ, C_IK = 0, 512, 640, 768, 1280, 1344, 1856
C_VS, C_VW, C_CK, C_CV, C_VB, C_NG, C_IW = 1920, 2048, 2176, 2304, 2432, 2496, 2520
ROW = 2528
ROPE_SLOTS, NORM_SLOTS = 30, 21
ROW_BLOCKS = [(b * 512, min(512, ROW - b * 512)) for b in range((ROW + 511) // 512)]

BLK = 1024
B_ROW = 0
B_GATE = B_ROW + 4 * len(ROW_BLOCKS)
B_W1 = B_GATE + 16
B_BR = B_W1 + 8
B_OUT = B_BR + 8
B_WQ = B_OUT + 8
B_EXP = B_WQ + 16
NCHUNK = 128
B_PLEW = B_EXP + 2 * NCHUNK
B_PLEG = B_PLEW + 2
RING = 4
PAIRS = -(-(B_PLEG + 8) // 2)
PAIRS += -PAIRS % RING
BODY = RING

Q_GA, Q_GF, Q_GAIN, Q_CGAIN = 0, 8, 16, 16 + NORM_SLOTS * HD
Q_POS = Q_CGAIN + HD
Q_W2 = Q_POS + 32
Q_SUB = Q_W2 + 4 * HD
Q_PT = Q_SUB + 2 * NKEYS
Q_PLEN = Q_PT + 2 * SEQ
NPARAM = Q_PLEN + D

T_NQ, T_DQ, T_IQ, T_KS, T_KW, T_KB, T_IK = 0, 4, 8, 12, 14, 16, 17
T_SRC = [c + 128 * j for c in (C_NQ, C_DQ, C_IQ) for j in range(4)]

ITEMS = [(b, t, hf) for b in range(3) for t in range(NT) for hf in range(2)]


def build(nc, x_in, stream, params, positions, inv_freq, out):
    ctx = ExitStack()
    with ctx:
        def sb(name, shape, dt=F32):
            return ctx.enter_context(nc.sbuf_tensor(name, shape, dt))

        layer_sems = []

        def sem(name, cleared=True):
            s = ctx.enter_context(nc.semaphore(name))
            if cleared:
                layer_sems.append(s)
            return s

        ps = ctx.enter_context(nc.psum_tensor("ps", [P, 8, 512], F32))

        x = sb("x", [P, NT, D])
        hT = sb("hT", [P, NK, SEQ])
        ring = sb("ring", [P, RING, 2, BLK])
        par = sb("par", [P, NPARAM])
        ident = sb("ident", [P, P])
        iota = sb("iota", [P, P])
        causal = sb("causal", [P, SEQ])
        cmask = sb("cmask", [P, NT, CP])
        cneg = sb("cneg", [P, NT, CP])
        headmask = sb("headmask", [P, HEADS])
        minus_half = sb("minus_half", [P, NT * NORM_SLOTS])
        zero16 = sb("zero16", [P, 512], BF16)
        cos = sb("cos", [P, NT + 1, ROT2])
        sin = sb("sin", [P, NT + 1, ROT2])
        small = sb("small", [P, 512])
        pickT = sb("pickT", [P, 3, SEQ])
        onehot1 = sb("onehot1", [P, 2, 4, P])
        onehot2 = sb("onehot2", [P, 2, 4, P])
        act = onehot1[:, 0, :, :].rearrange("p a b -> p (a b)").rearrange("p (b t) -> p b t", b=2)
        wgt = onehot1[:, 1, :, :].rearrange("p a b -> p (a b)").rearrange("p (b t) -> p b t", b=2)

        big = sb("big", [P, SEQ * NKEYS])
        G = big[:, :].rearrange("p (t i) -> p t i", t=SEQ)
        used = [0]

        def carve(n, *dims, **kw):
            a = big[:, used[0]:used[0] + n]
            used[0] += n
            assert used[0] <= SEQ * NKEYS
            return a.rearrange(*dims, **kw) if dims else a

        xn = carve(NT * D, "p (t d) -> p t d", t=NT)
        rows = carve(NT * ROW, "p (t c) -> p t c", t=NT)
        tmp = carve(NT * NORM_SLOTS * HD)
        qkT = carve(18 * SEQ, "p (s t) -> p s t", s=18)
        gateT = carve(16 * SEQ, "p (m t) -> p m t", m=16)
        Z = carve(2 * 16 * 2 * CP, "p (v j g n) -> p v j g n", v=2, j=16, g=2)
        hidT = carve(2 * 2 * CP, "p (f c) -> p f c", f=2)
        hidv = carve(2 * P, "p (f c) -> p f c", f=2)
        kcdup = carve(P)
        vcblk = carve(HEADS * HD, "p (h d) -> p h d", h=HEADS)
        kc = carve(HD)
        kcT = carve(2 * CP)
        relu = carve(HEADS * SEQ, "p (h s) -> p h s", h=HEADS)
        score = carve(NT * SEQ, "p (t s) -> p t s", t=NT)
        dmask = carve(NT * SEQ, "p (t s) -> p t s", t=NT)
        over = used[0]
        cdup = carve(NT * 4 * P, "p (t s c) -> p t s c", t=NT, s=4)
        kdup = carve(NT * 6 * P, "p (t s c) -> p t s c", t=NT, s=6)
        used[0] = over
        sm = carve(2 * 4 * SEQ, "p (i h s) -> p i h s", i=2, h=4)
        prob = carve(2 * 4 * SEQ, "p (i h s) -> p i h s", i=2, h=4)
        probT = carve(2 * 2 * 512, "p (i b c) -> p i b c", i=2, b=2)
        pc = carve(NT * P, "p (t c) -> p t c", t=NT)
        y = carve(2 * NT * 512, "p (m t c) -> p m t c", m=2, t=NT)
        o_tmp = carve(512)
        peak_attention = used[0]
        used[0] = NT * D
        yT = carve(2 * 4 * SEQ, "p (m k t) -> p m k t", m=2, k=4)
        mergedT = carve(NK * SEQ, "p (k t) -> p k t", k=NK)
        gate_prod = carve(2 * SEQ)
        assert used[0] <= NT * D + NT * ROW + NT * NORM_SLOTS * HD
        used[0] = NT * D
        qPT = carve(16 * SEQ, "p (c t) -> p c t", c=16)
        keyscore = carve(NT * 16 * NKEYS, "p (t c n) -> p t c n", t=NT, c=16)
        keyrest = carve(NT * 16 * NKEYS, "p (t c n) -> p t c n", t=NT, c=16)
        top1 = carve(NT * 16 * PICKS, "p (t c k) -> p t c k", t=NT, c=16)
        idx1 = carve(NT * 16 * PICKS, "p (t c k) -> p t c k", t=NT, c=16)
        cand = carve(NT * HEADS * 256, "p (t h c) -> p t h c", t=NT, h=HEADS)
        candrest = carve(NT * HEADS * 256, "p (t h c) -> p t h c", t=NT, h=HEADS)
        top2 = carve(NT * 128, "p (t h k) -> p t h k", t=NT, h=HEADS)
        pos2 = carve(NT * 128, "p (t h k) -> p t h k", t=NT, h=HEADS)
        which = carve(2 * NT * 128, "p (v t h k) -> p v t h k", v=2, t=NT, h=HEADS)
        whichf = carve(2 * NT * 128, "p (v t h k) -> p v t h k", v=2, t=NT, h=HEADS)
        picks = carve(3 * NT * 128, "p (v t h k) -> p v t h k", v=3, t=NT, h=HEADS)
        expo = carve(NT * 128, "p (t h k) -> p t h k", t=NT, h=HEADS)
        used[0] = NT * D
        pw = carve(NT * D, "p (t d) -> p t d", t=NT)
        gate = carve(NT * D, "p (t d) -> p t d", t=NT)
        junk = carve(D)

        idx1u = idx1.bitcast(U32)
        pos2u = pos2.bitcast(U32)
        whichu = which.bitcast(U32)

        ss = small[:, 0:2]
        rstd = small[:, 2:4]
        psq = small[:, 4:6]
        prstd = small[:, 6:8]
        ms = small[:, 8:50].rearrange("p (t s) -> p t s", t=NT)
        msr = small[:, 50:92].rearrange("p (t s) -> p t s", t=NT)
        sg = small[:, 92:140].rearrange("p (t s) -> p t s", t=NT)
        iwb = small[:, 140:156].rearrange("p (t s) -> p t s", t=NT)
        cms = small[:, 156:158]
        maxes = small[:, 160:208].rearrange("p (i h) -> p i h", h=4)
        nmax = small[:, 208:256].rearrange("p (i h) -> p i h", h=4)
        sums = small[:, 256:304].rearrange("p (i h) -> p i h", h=4)
        coef = small[:, 304:352].rearrange("p (i h) -> p i h", h=4)
        csum = small[:, 352:368].rearrange("p (t h) -> p t h", t=NT)
        ccoef = small[:, 368:384].rearrange("p (t h) -> p t h", t=NT)
        cmax = small[:, 384:400].rearrange("p (t h) -> p t h", t=NT)
        gsum = small[:, 400:416].rearrange("p (t h) -> p t h", t=NT)
        top8 = small[:, 416:432].rearrange("p (t k) -> p t k", t=NT)
        gmax = small[:, 432:448].rearrange("p (t h) -> p t h", t=NT)
        grec = small[:, 448:464].rearrange("p (t h) -> p t h", t=NT)

        rms_steps = [rstd, msr, cms[0:2 * CP, 1:2], rstd, prstd, rstd]

        def bank(b, lo=0, hi=512):
            return ps[:, b, lo:hi]

        in_dma = sem("in_dma", False)
        consts_pool = sem("consts_pool", False)
        consts_dve = sem("consts_dve", False)
        consts_act = sem("consts_act", False)
        angle_done = sem("angle_done", False)
        pair_full = [sem(f"pair_full{s}", False) for s in range(RING)]
        pair_free = sem("pair_free", False)
        out_dma = sem("out_dma", False)
        layer_done = sem("layer_done", False)
        layer_over = sem("layer_over", False)
        layer_go = sem("layer_go", False)
        params_in = sem("params_in")
        squares = sem("squares")
        rms_in = sem("rms_in")
        rms_out = sem("rms_out")
        xn_ready = sem("xn_ready")
        xT_ps = sem("xT_ps")
        hT_ready = sem("hT_ready")
        row_ps = sem("row_ps")
        row_ready = sem("row_ready")
        mg_ps = sem("mg_ps")
        mg_ready = sem("mg_ready")
        cdup_ready = sem("cdup_ready")
        sg_ready = sem("sg_ready")
        rope_done = sem("rope_done")
        qk_ps = sem("qk_ps")
        qk_ready = sem("qk_ready")
        cmp_ps = sem("cmp_ps")
        z_ready = sem("z_ready")
        hid_ready = sem("hid_ready")
        kc_ready = sem("kc_ready")
        kcT_ready = sem("kcT_ready")
        idx_ps = sem("idx_ps")
        relu_ready = sem("relu_ready")
        relu_used = sem("relu_used")
        cs_ps = sem("cs_ps")
        cs_sub = sem("cs_sub")
        cs_exp = sem("cs_exp")
        pc_ready = sem("pc_ready")
        pcT_ps = sem("pcT_ps")
        pcT_ready = sem("pcT_ready")
        oc_ps = sem("oc_ps")
        s_ps = sem("s_ps")
        sm_ready = sem("sm_ready")
        prob_ready = sem("prob_ready")
        pT_ps = sem("pT_ps")
        pT_ready = sem("pT_ready")
        o_ps = sem("o_ps")
        y_added = sem("y_added")
        yT_ps = sem("yT_ps")
        yT_ready = sem("yT_ready")
        br_ps = sem("br_ps")
        br_ready = sem("br_ready")
        wo_ps = sem("wo_ps")
        q_ps = sem("q_ps")
        q_ready = sem("q_ready")
        ks_ps = sem("ks_ps")
        ks_ready = sem("ks_ready")
        picks_ready = sem("picks_ready")
        gexp_in = sem("gexp_in")
        gexp_out = sem("gexp_out")
        pickT_ps = sem("pickT_ps")
        pickT_ready = sem("pickT_ready")
        hot_ready = sem("hot_ready")
        g_ps = sem("g_ps")
        g_ready = sem("g_ready")
        act_ps = sem("act_ps")
        act_ready = sem("act_ready")
        wgt_ready = sem("wgt_ready")
        wgt_used = sem("wgt_used")
        pw_ps = sem("pw_ps")
        pw_ready = sem("pw_ready")
        pg_ps = sem("pg_ps")
        pg_ready = sem("pg_ready")
        ENGINES = 4

        block = ctx.enter_context(nc.Block())

        @block.sync
        def _(sp):
            sp.dma_start(x[:, :, :], x_in.rearrange("o (t p) d -> p (o t) d", p=P)).then_inc(in_dma, 16)
            sp.dma_start(small[:, 0:8], inv_freq).then_inc(in_dma, 16)
            sp.dma_start(small[:, 8:11].bitcast(I32), positions).then_inc(in_dma, 16)
            for s in range(RING):
                sp.dma_start(ring[:, s, :, :], stream[s]).then_inc(pair_full[s], 16)
            with sp.Fori(1, DEPTH * PAIRS // RING) as turn:
                for s in range(RING):
                    need = sp.snap(turn * RING + (s + 1 - RING))
                    src = sp.snap(turn * RING + s)
                    sp.wait_ge(pair_free, need)
                    sp.dma_start(ring[:, s, :, :],
                                 stream[bass.ds(src, 1)].rearrange("o p b c -> p (o b) c")).then_inc(pair_full[s], 16)
            sp.wait_ge(layer_go, DEPTH)
            sp.dma_start(out.rearrange("o (t p) d -> p (o t) d", p=P), x[:, :, :]).then_inc(out_dma, 16)
            sp.wait_ge(out_dma, 16)

        @block.gpsimd
        def _(g):
            g.memset(ident[:, :], 0.0)
            g.memset(causal[:, :], 0.0)
            g.memset(minus_half[:, :], -0.5)
            g.memset(cmask[:, :, :], 1.0)
            g.memset(cneg[:, :, :], 0.0)
            g.memset(headmask[:, :], 1.0)
            g.iota(iota[:, :], pattern=[[1, P]], base=0, channel_multiplier=0, allow_small_or_imprecise_dtypes=True)
            g.drain()
            g.affine_select(out=ident[:, :], in_=ident[:, :], compare_op=ALU.not_equal, fill=1.0,
                            base=0, pattern=[[-1, P]], channel_multiplier=1)
            g.affine_select(out=causal[:, :], in_=causal[:, :], compare_op=ALU.is_ge, fill=NEG,
                            base=P, pattern=[[-1, SEQ]], channel_multiplier=1)
            g.affine_select(out=cmask[:, :, :], in_=cmask[:, :, :], compare_op=ALU.is_ge, fill=0.0,
                            base=-(CMP_LEN - 1), pattern=[[P, NT], [-CMP_STRIDE, CP]], channel_multiplier=1)
            g.affine_select(out=cneg[:, :, :], in_=cneg[:, :, :], compare_op=ALU.is_ge, fill=NEG,
                            base=-(CMP_LEN - 1), pattern=[[P, NT], [-CMP_STRIDE, CP]], channel_multiplier=1)
            g.affine_select(out=headmask[:, :], in_=headmask[:, :], compare_op=ALU.is_ge, fill=0.0,
                            base=0, pattern=[[-CP, HEADS]], channel_multiplier=1)
            g.drain()
            g.affine_select(out=headmask[:, :], in_=headmask[:, :], compare_op=ALU.is_ge, fill=0.0,
                            base=CP - 1, pattern=[[CP, HEADS]], channel_multiplier=-1)
            g.drain().then_inc(consts_pool, 1)
            with g.Fori(0, DEPTH) as layer:
                for n, v in enumerate(rms_steps):
                    g.wait_ge(rms_in, n + 1)
                    flat = v if len(v.shape) == 2 else v.rearrange("p a b -> p (a b)")
                    g.tensor_tensor(flat, flat, minus_half[0:v.shape[0], 0:flat.shape[1]], ALU.pow).then_inc(rms_out, 1)
                g.drain().then_inc(layer_done, 1)
                g.wait_ge(layer_done, layer * ENGINES + ENGINES)
                g.sem_inc(layer_over, 1)
                for s in layer_sems:
                    g.sem_clear(s)
                g.sem_inc(layer_go, 1)

        @block.scalar
        def _(a):
            a.wait_ge(angle_done, 1)
            a.activation(sin[:, :, :], sin[:, :, :], ACT.Sin)
            a.activation(cos[:, :, :], cos[:, :, :], ACT.Sin)
            a.drain().then_inc(consts_act, 1)
            a.wait_ge(in_dma, 3 * 16)

            def norm_squares():
                for t in range(NT):
                    a.activation(junk, x[:, t, :], ACT.Square, accum_out=ss[:, t:t + 1])
                    a.drain()
                a.drain().then_inc(squares, 1)

            def norm_hT(m, b0, gain):
                for j in range(4):
                    a.wait_ge(xT_ps, 4 * m + j + 1)
                    for k in (2 * j, 2 * j + 1):
                        src = bank(b0 + j, (k % 2) * SEQ, (k % 2 + 1) * SEQ)
                        ins = a.activation(hT[:, k, :], src, ACT.Copy,
                                           scale=1.0 if gain is None else par[:, gain + k:gain + k + 1])
                    ins.then_inc(hT_ready, 1)

            with a.Fori(0, DEPTH) as layer:
                a.dma_start(par[:, :], params[bass.ds(layer, 1)].rearrange("o p c -> p (o c)")).then_inc(params_in, 16)
                norm_squares()
                a.wait_ge(params_in, 16)
                norm_hT(0, 4, Q_GA)

                for n, (c0, w) in enumerate([(c0, w) for c0, w in ROW_BLOCKS for t in range(NT)]):
                    a.wait_ge(row_ps, n + 1)
                    a.activation(rows[:, n % NT, c0:c0 + w], bank(n % 4, 0, w), ACT.Copy).then_inc(row_ready, 1)
                a.drain()
                for t in range(NT):
                    ins = a.activation(cdup[:, t, :, :].rearrange("p s (e d) -> p s e d", e=2),
                                       rows[:, t, C_CK:C_CK + 4 * HD].rearrange("p (s d) -> p s d", d=HD).unsqueeze(2)
                                       .broadcast_to([P, 4, 2, HD]), ACT.Copy)
                ins.then_inc(cdup_ready, 1)
                a.activation(sg[:, :, :], rows[:, :, C_NG:C_NG + 24], ACT.Sigmoid).then_inc(sg_ready, 1)

                for n in range(8):
                    a.wait_ge(mg_ps, n + 1)
                    a.activation(gateT[:, 2 * n:2 * n + 2, :], bank(4 + n % 2).rearrange("p (m t) -> p m t", m=2),
                                 ACT.Sigmoid).then_inc(mg_ready, 1)

                a.wait_ge(cmp_ps, 2)
                a.activation(hidT[:, :, :], bank(2, 0, 64).rearrange("p (f c) -> p f c", f=2),
                             ACT.Gelu_apprx_tanh).then_inc(hid_ready, 1)
                a.wait_ge(cmp_ps, 3)
                for half in range(2):
                    ins = a.activation(hidv[:, half, :].rearrange("p (g r n) -> p g r n", g=2, r=4),
                                       bank(3, 32 * half, 32 * half + 32).rearrange("p (g n) -> p g n", g=2)
                                       .unsqueeze(2).broadcast_to([P, 2, 4, CP]), ACT.Gelu_apprx_tanh)
                ins.then_inc(hid_ready, 1)
                for n in range(9):
                    a.wait_ge(qk_ps, n + 1)
                    a.activation(qkT[:, 2 * n:2 * n + 2, :], bank(4 + n % 4).rearrange("p (s t) -> p s t", s=2),
                                 ACT.Copy).then_inc(qk_ready, 1)
                for t in range(NT):
                    keys = (t + 1) * P
                    a.wait_ge(idx_ps, t + 1)
                    if t:
                        a.wait_ge(relu_used, t)
                    per = 512 // keys
                    for j in range(HEADS // per):
                        ins = a.activation(relu[:, j * per:(j + 1) * per, 0:keys],
                                           bank(2 * t + j).rearrange("p (h s) -> p h s", h=per), ACT.Relu, scale=SCALE)
                    ins.then_inc(relu_ready, 1)
                for t in range(NT):
                    a.wait_ge(cs_sub, t + 1)
                    a.activation(pc[:, t, :], pc[:, t, :], ACT.Exp, scale=SCALE).then_inc(cs_exp, 1)
                a.wait_ge(pcT_ps, 1)
                a.activation(relu[:, 0:1, :], bank(6, 0, 256).rearrange("p (h s) -> p h s", h=1),
                             ACT.Copy).then_inc(pcT_ready, 1)
                def exps(i):
                    _, t, _ = ITEMS[i]
                    a.wait_ge(sm_ready, i + 1)
                    if i >= 2:
                        a.wait_ge(pT_ps, i - 1)
                    for h in range(4):
                        ins = a.activation(prob[:, i % 2, h, 0:(t + 1) * P], sm[:, i % 2, h, 0:(t + 1) * P], ACT.Exp,
                                           scale=SCALE, bias=nmax[:, i, h:h + 1], accum_out=sums[:, i, h:h + 1])
                    a.drain().then_inc(prob_ready, 1)

                def copies(i):
                    _, t, _ = ITEMS[i]
                    a.wait_ge(pT_ps, i + 1)
                    if i >= 2:
                        a.wait_ge(o_ps, i - 1)
                    for b in range(t + 1):
                        ins = a.activation(probT[:, i % 2, b, :], bank(4 + b), ACT.Copy)
                    ins.then_inc(pT_ready, 1)

                for i in range(len(ITEMS)):
                    exps(i)
                    if i:
                        copies(i - 1)
                copies(len(ITEMS) - 1)
                for n in range(4):
                    a.wait_ge(yT_ps, n + 1)
                    a.activation(yT[:, n // 2, 2 * (n % 2):2 * (n % 2) + 2, :],
                                 bank(n).rearrange("p (k t) -> p k t", k=2), ACT.Copy).then_inc(yT_ready, 1)

                a.wait_ge(xn_ready, 2)
                norm_squares()
                norm_hT(1, 4, Q_GF)
                for n in range(8):
                    a.wait_ge(q_ps, n + 1)
                    a.activation(qPT[:, 2 * n:2 * n + 2, :], bank(n % 2).rearrange("p (c t) -> p c t", c=2),
                                 ACT.Copy).then_inc(q_ready, 1)
                    if n % 2:
                        for t in range(NT):
                            a.wait_ge(ks_ps, (n // 2) * 2 + t + 1)
                            a.activation(keyscore[:, t, 2 * n - 2:2 * n + 2, :],
                                         bank(2 + t).rearrange("p (c n) -> p c n", c=4), ACT.Copy).then_inc(ks_ready, 1)
                a.wait_ge(gexp_in, 1)
                a.activation(expo[:, :, :, :], expo[:, :, :, :], ACT.Exp).then_inc(gexp_out, 1)
                a.wait_ge(pickT_ps, 1)
                a.activation(pickT[:, 0:2, :], bank(6).rearrange("p (v t) -> p v t", v=2), ACT.Copy).then_inc(pickT_ready, 1)
                a.activation(pickT[:, 2, :], bank(7, 0, SEQ), ACT.Copy).then_inc(pickT_ready, 1)
                a.sem_inc(g_ready, 2)
                with a.Fori(0, SEQ // 8) as i:
                    for b in range(2):
                        a.wait_ge(g_ps, i * 2 + (b + 3))
                        a.activation(big[:, bass.ds(i * (8 * P) + b * 4 * P, 4 * P)], bank(4 + b),
                                     ACT.Copy).then_inc(g_ready, 1)
                with a.Fori(0, NCHUNK // 2) as i:
                    for b in range(2):
                        a.wait_ge(act_ps, i * 2 + (b + 1))
                        a.wait_ge(wgt_ready, i * 2 + (b + 1))
                        a.activation(act[:, b, :], bank(4 + b, 0, SEQ), ACT.Gelu_apprx_tanh).then_inc(act_ready, 1)

                a.wait_ge(pw_ps, 1)
                for n in range(4):
                    a.activation(pw[:, n // 2, (n % 2) * 512:(n % 2) * 512 + 512], bank(4 + n), ACT.Copy)
                a.drain()
                for t in range(NT):
                    a.activation(junk, pw[:, t, :], ACT.Square, accum_out=psq[:, t:t + 1])
                    a.drain()
                a.drain().then_inc(pw_ready, 1)
                a.wait_ge(xn_ready, 4)
                norm_squares()
                norm_hT(2, 0, None)
                a.wait_ge(pg_ps, 1)
                for n in range(4):
                    a.activation(gate[:, n // 2, (n % 2) * 512:(n % 2) * 512 + 512], bank(4 + n),
                                 ACT.Sigmoid).then_inc(pg_ready, 1)
                a.drain().then_inc(layer_done, 1)
                a.wait_ge(layer_go, layer + 1)

        @block.vector
        def _(v):
            v.memset(zero16[:, :], 0.0)
            v.memset(sin[:, :, :], 0.0)
            v.drain().then_inc(consts_dve, 1)
            v.wait_ge(in_dma, 3 * 16)
            v.tensor_copy(small[:, 16:19], small[:, 8:11].bitcast(I32))
            v.drain()
            ang = small[:, 32:56].rearrange("p (t f) -> p t f", f=ROT2)
            v.tensor_tensor(ang, small[:, 16:19].unsqueeze(2).broadcast_to([P, 3, ROT2]),
                            small[:, 0:8].unsqueeze(1).broadcast_to([P, 3, ROT2]), ALU.mult)
            v.drain()
            v.tensor_scalar(small[:, 64:88], small[:, 32:56], 0.15915494309189535, None, ALU.mult)
            v.drain()
            v.tensor_copy(small[:, 96:120].bitcast(I32), small[:, 64:88])
            v.drain()
            v.tensor_copy(small[:, 64:88], small[:, 96:120].bitcast(I32))
            v.drain()
            v.scalar_tensor_tensor(small[:, 128:152], small[:, 64:88], -6.28125, small[:, 32:56], ALU.mult, ALU.add)
            v.drain()
            v.scalar_tensor_tensor(small[:, 160:184], small[:, 64:88], -0.0019353071795864769, small[:, 128:152],
                                   ALU.mult, ALU.add)
            v.drain()
            v.tensor_scalar(sin[:, :, :], small[:, 160:184].rearrange("p (t f) -> p t f", f=ROT2),
                            3.141592, -3.141592, ALU.min, ALU.max)
            v.drain()
            v.scalar_tensor_tensor(cos[:, :, :], sin[:, :, :], -1.0, sin[:, :, :], ALU.mult, ALU.max)
            v.drain()
            v.tensor_scalar(cos[:, :, :], cos[:, :, :], -1.0, 1.5707963267948966, ALU.mult, ALU.add)
            v.drain().then_inc(angle_done, 1)
            v.wait_ge(consts_act, 1)
            v.wait_ge(consts_pool, 1)

            def rsqrt_mean(step, src, n):
                v.tensor_scalar(rms_steps[step], src, 1.0 / n, EPS, ALU.mult, ALU.add).then_inc(rms_in, 1)
                v.wait_ge(rms_out, step + 1)

            def norm_x(m):
                v.wait_ge(squares, m + 1)
                rsqrt_mean((0, 3, 5)[m], ss[:, :], D)
                for t in range(NT):
                    ins = v.tensor_scalar(xn[:, t, :], x[:, t, :], rstd[:, t:t + 1], None, ALU.mult)
                ins.then_inc(xn_ready, 1)

            def rope(lo, hi, c, s, shape):
                n = 1
                for d in shape[1:]:
                    n *= d
                np_ = shape[0]
                parts = []
                for j in range(4):
                    a = tmp[0:np_, j * n:(j + 1) * n]
                    if len(shape) == 4:
                        a = a.rearrange("p (t s f) -> p t s f", t=shape[1], s=shape[2])
                    parts.append(a)
                v.tensor_tensor(parts[0], lo, c, ALU.mult)
                v.tensor_tensor(parts[1], hi, s, ALU.mult)
                v.tensor_tensor(parts[2], hi, c, ALU.mult)
                v.tensor_tensor(parts[3], lo, s, ALU.mult)
                v.drain()
                v.tensor_tensor(lo, parts[0], parts[1], ALU.subtract)
                return v.tensor_tensor(hi, parts[2], parts[3], ALU.add)

            with v.Fori(0, DEPTH) as layer:
                norm_x(0)

                v.wait_ge(row_ready, 2 * len(ROW_BLOCKS))
                v.wait_ge(params_in, 16)
                nrows = rows[:, :, 0:NORM_SLOTS * HD]
                nslots = nrows.rearrange("p t (s d) -> p t s d", d=HD)
                tslots = tmp.rearrange("p (t s d) -> p t s d", t=NT, d=HD)
                v.tensor_tensor(tmp.rearrange("p (t c) -> p t c", t=NT), nrows, nrows, ALU.mult)
                v.drain()
                v.tensor_reduce(ms[:, :, :], tslots, AX.X, ALU.add)
                v.drain()
                rsqrt_mean(1, ms[:, :, :], HD)
                v.tensor_tensor(nslots, nslots, msr[:, :, :].unsqueeze(3).broadcast_to([P, NT, NORM_SLOTS, HD]), ALU.mult)
                v.drain()
                v.tensor_tensor(nrows, nrows, par[:, Q_GAIN:Q_GAIN + NORM_SLOTS * HD].unsqueeze(1)
                                .broadcast_to([P, NT, NORM_SLOTS * HD]), ALU.mult)
                v.drain()
                rslots = rows[:, :, 0:ROPE_SLOTS * HD].rearrange("p t (s d) -> p t s d", d=HD)
                shape = [P, NT, ROPE_SLOTS, ROT2]
                rope(rslots[:, :, :, 0:ROT2], rslots[:, :, :, ROT2:2 * ROT2],
                     cos[:, 0:NT, :].unsqueeze(2).broadcast_to(shape), sin[:, 0:NT, :].unsqueeze(2).broadcast_to(shape),
                     shape)
                v.drain()
                for t in range(NT):
                    v.tensor_copy(kdup[:, t, 0:4, :].rearrange("p s (e d) -> p s e d", e=2),
                                  rows[:, t, C_KS:C_KS + 4 * HD].rearrange("p (s d) -> p s d", d=HD).unsqueeze(2)
                                  .broadcast_to([P, 4, 2, HD]))
                    for s, col in ((4, C_KB), (5, C_IK)):
                        ins = v.tensor_copy(kdup[:, t, s, :].rearrange("p (e d) -> p e d", e=2),
                                            rows[:, t, col:col + HD].unsqueeze(1).broadcast_to([P, 2, HD]))
                ins.then_inc(rope_done, 1)
                v.tensor_scalar(iwb[:, :, :], rows[:, :, C_IW:C_IW + 8], HEADS ** -0.5, None, ALU.mult)
                v.memset(Z[:, :, :, :, :], 0.0)
                v.drain()

                v.wait_ge(cmp_ps, 1)
                for kv in range(2):
                    for gr in range(2):
                        for par_ in range(2):
                            lo = par_ * HD
                            src = ps[lo:lo + HD, kv, gr * SEQ:(gr + 1) * SEQ].rearrange(
                                "p (n j e) -> p e j n", j=8, e=2)[:, par_]
                            for half in range(2):
                                ins = v.tensor_tensor(
                                    Z[lo:lo + HD, kv, 8 * half:8 * half + 8, gr, 0:NCMP],
                                    src[:, :, half:half + NCMP],
                                    par[lo:lo + HD, Q_POS + 16 * kv + 8 * half:Q_POS + 16 * kv + 8 * half + 8]
                                    .unsqueeze(2).broadcast_to([HD, 8, NCMP]), ALU.add)
                v.drain().then_inc(z_ready, 1)
                v.wait_ge(cmp_ps, 4)
                kcp = ps[0:2 * CP, 3, 0:HD]
                kcs = kc[0:2 * CP, :]
                v.tensor_copy(kcs, kcp)
                v.drain()
                v.tensor_tensor(tmp[0:2 * CP, 0:HD], kcs, kcs, ALU.mult)
                v.drain()
                v.tensor_reduce(cms[0:2 * CP, 0:1], tmp[0:2 * CP, 0:HD], AX.X, ALU.add)
                v.drain()
                rsqrt_mean(2, cms[0:2 * CP, 0:1], HD)
                v.scalar_tensor_tensor(kcs, kcs, cms[0:2 * CP, 1:2], par[0:2 * CP, Q_CGAIN:Q_CGAIN + HD],
                                       ALU.mult, ALU.mult)
                v.drain()
                rope(kc[0:2 * CP, 0:ROT2], kc[0:2 * CP, ROT2:2 * ROT2], cos[0:2 * CP, NT, :], sin[0:2 * CP, NT, :],
                     [2 * CP, ROT2])
                v.drain()
                v.tensor_copy(kcdup[0:2 * CP, :].rearrange("p (e d) -> p e d", e=2),
                              kcs.unsqueeze(1).broadcast_to([2 * CP, 2, HD]))
                v.tensor_tensor(vcblk[:, :, :], bank(3, 64, 128).unsqueeze(1).broadcast_to([P, HEADS, HD]),
                                headmask[:, :].unsqueeze(2).broadcast_to([P, HEADS, HD]), ALU.mult)
                v.drain().then_inc(kc_ready, 1)
                v.wait_ge(cmp_ps, 5)
                v.tensor_copy(kcT, bank(3, 128, 128 + 2 * CP)).then_inc(kcT_ready, 1)

                for t in range(NT):
                    keys = (t + 1) * P
                    sc = score[:, t, 0:keys]
                    cm = causal[:, SEQ - keys:SEQ]
                    v.wait_ge(relu_ready, t + 1)
                    for h in range(HEADS):
                        v.scalar_tensor_tensor(sc, relu[:, h % 2 * 4 + h // 2, 0:keys], iwb[:, t, h:h + 1], cm if h == 0 else sc,
                                               ALU.mult, ALU.add)
                        v.drain()
                    v.drain().then_inc(relu_used, 1)
                for r in range(TOPK_ROUNDS):
                    for t in range(NT):
                        v.max(top8[:, t, :], score[:, t, 0:(t + 1) * P])
                    v.drain()
                    for t in range(NT):
                        v.match_replace(score[:, t, 0:(t + 1) * P], top8[:, t, :], score[:, t, 0:(t + 1) * P], GONE)
                    v.drain()
                for t in range(NT):
                    keys = (t + 1) * P
                    v.tensor_scalar(dmask[:, t, 0:keys], score[:, t, 0:keys], 0.5 * GONE, NEG, ALU.is_gt, ALU.mult)
                v.drain()
                for t in range(NT):
                    keys = (t + 1) * P
                    v.tensor_tensor(dmask[:, t, 0:keys], dmask[:, t, 0:keys], causal[:, SEQ - keys:SEQ], ALU.add)
                v.drain()

                v.wait_ge(cs_ps, 1)
                for t in range(NT):
                    pcv = pc[:, t, :].rearrange("p (h n) -> p h n", h=HEADS)
                    for e in range(2):
                        v.tensor_tensor(pcv.rearrange("p (h e) n -> p e h n", e=2)[:, e],
                                        bank(6 + e, t * HD, (t + 1) * HD).rearrange("p (h n) -> p h n", h=4),
                                        cneg[:, t, :].unsqueeze(1).broadcast_to([P, 4, CP]), ALU.add)
                    v.drain()
                    v.tensor_reduce(cmax[:, t, :], pcv, AX.X, ALU.max)
                    v.drain()
                    v.tensor_tensor(pcv, pcv, cmax[:, t, :].unsqueeze(2).broadcast_to([P, HEADS, CP]), ALU.subtract)
                    v.drain().then_inc(cs_sub, 1)
                for t in range(NT):
                    pcv = pc[:, t, :].rearrange("p (h n) -> p h n", h=HEADS)
                    v.wait_ge(cs_exp, t + 1)
                    v.tensor_reduce(csum[:, t, :], pcv, AX.X, ALU.add)
                    v.drain()
                    v.reciprocal(ccoef[:, t, :], csum[:, t, :])
                    v.tensor_tensor(pcv, pcv, cmask[:, t, :].unsqueeze(1).broadcast_to([P, HEADS, CP]), ALU.mult)
                    v.drain()
                v.wait_ge(sg_ready, 1)
                v.tensor_tensor(ccoef[:, :, :], ccoef[:, :, :], sg[:, :, 0:8], ALU.mult)
                v.drain().then_inc(pc_ready, 1)
                for t in range(NT):
                    v.wait_ge(oc_ps, t + 1)
                    v.tensor_tensor(y[:, 0, t, :].rearrange("p (h d) -> p h d", h=HEADS),
                                    bank(t).rearrange("p (h d) -> p h d", h=HEADS),
                                    ccoef[:, t, :].unsqueeze(2).broadcast_to([P, HEADS, HD]), ALU.mult)
                v.drain().then_inc(y_added, 1)

                def masked(i):
                    b, t, _ = ITEMS[i]
                    keys = (t + 1) * P
                    mk = dmask[:, t, 0:keys] if b == 2 else causal[:, SEQ - keys:SEQ]
                    v.wait_ge(s_ps, i + 1)
                    if i >= 2:
                        v.wait_ge(prob_ready, i - 1)
                    for h in range(4):
                        src = bank(2 * (i % 2) + h % 2, (h // 2) * keys, (h // 2 + 1) * keys)
                        v.tensor_tensor_reduce(out=sm[:, i % 2, h, 0:keys], in0=src, in1=mk, scale=1.0, scalar=GONE,
                                               op0=ALU.add, op1=ALU.max, accum_out=maxes[:, i, h:h + 1])
                    v.drain()
                    v.tensor_scalar(nmax[:, i, :], maxes[:, i, :], -SCALE, None, ALU.mult)
                    v.drain().then_inc(sm_ready, 1)

                def weighted(i):
                    b, t, hf = ITEMS[i]
                    v.wait_ge(prob_ready, i + 1)
                    v.reciprocal(coef[:, i, :], sums[:, i, :])
                    v.drain()
                    if b < 2:
                        v.tensor_tensor(coef[:, i, :], coef[:, i, :],
                                        sg[:, t, 8 * (b + 1) + 4 * hf:8 * (b + 1) + 4 * hf + 4], ALU.mult)
                        v.drain()
                    v.wait_ge(o_ps, i + 1)
                    cf = coef[:, i, :].unsqueeze(2).broadcast_to([P, 4, HD])
                    src = bank(6 + i % 2, 0, 256).rearrange("p (h d) -> p h d", h=4)
                    if b == 2:
                        v.tensor_tensor(y[:, 1, t, 256 * hf:256 * hf + 256].rearrange("p (h d) -> p h d", h=4),
                                        src, cf, ALU.mult)
                    else:
                        v.tensor_tensor(o_tmp[:, 0:256].rearrange("p (h d) -> p h d", h=4), src, cf, ALU.mult)
                        v.drain()
                        v.tensor_tensor(y[:, 0, t, 256 * hf:256 * hf + 256], y[:, 0, t, 256 * hf:256 * hf + 256],
                                        o_tmp[:, 0:256], ALU.add)
                    v.drain().then_inc(y_added, 1)

                for i in range(len(ITEMS)):
                    masked(i)
                    if i >= 2:
                        weighted(i - 2)
                weighted(len(ITEMS) - 2)
                weighted(len(ITEMS) - 1)

                v.wait_ge(mg_ready, 8)
                for m in range(NK):
                    v.wait_ge(br_ps, m + 1)
                    v.tensor_tensor(gate_prod[:, 0:SEQ], bank(4 + m % 4, 0, SEQ), gateT[:, m, :], ALU.mult)
                    v.tensor_tensor(gate_prod[:, SEQ:2 * SEQ], bank(4 + m % 4, SEQ, 2 * SEQ), gateT[:, NK + m, :], ALU.mult)
                    v.drain()
                    v.tensor_tensor(mergedT[:, m, :], gate_prod[:, 0:SEQ], gate_prod[:, SEQ:2 * SEQ],
                                    ALU.add)
                    v.drain().then_inc(br_ready, 1)
                v.wait_ge(wo_ps, 1)
                for n in range(4):
                    xs = x[:, n // 2, (n % 2) * 512:(n % 2) * 512 + 512]
                    v.tensor_tensor(xs, bank(n), xs, ALU.add)
                v.drain().then_inc(xn_ready, 1)

                norm_x(1)
                v.wait_ge(ks_ready, 8)
                both = [(t, c) for t in range(NT) for c in range(16)]
                for t, c in both:
                    v.max(top1[:, t, c, 0:8], keyscore[:, t, c, :])
                v.drain()
                for t, c in both:
                    v.max_index(idx1u[:, t, c, 0:8], top1[:, t, c, 0:8], keyscore[:, t, c, :])
                    v.match_replace(keyrest[:, t, c, :], top1[:, t, c, 0:8], keyscore[:, t, c, :], GONE)
                v.drain()
                for t, c in both:
                    v.max(top1[:, t, c, 8:16], keyrest[:, t, c, :])
                v.drain()
                for t, c in both:
                    v.max_index(idx1u[:, t, c, 8:16], top1[:, t, c, 8:16], keyrest[:, t, c, :])
                v.drain()
                for t in range(NT):
                    tv = top1[:, t, :, :].rearrange("p (h s) k -> p h s k", s=2)
                    v.tensor_tensor(cand[:, t, :, :].rearrange("p h (a b) -> p h a b", a=PICKS),
                                    tv[:, :, 0, :].unsqueeze(3).broadcast_to([P, HEADS, PICKS, PICKS]),
                                    tv[:, :, 1, :].unsqueeze(2).broadcast_to([P, HEADS, PICKS, PICKS]), ALU.add)
                v.drain()
                heads = [(t, h) for t in range(NT) for h in range(HEADS)]
                for t, h in heads:
                    v.max(top2[:, t, h, 0:8], cand[:, t, h, :])
                v.drain()
                for t, h in heads:
                    v.max_index(pos2u[:, t, h, 0:8], top2[:, t, h, 0:8], cand[:, t, h, :])
                    v.match_replace(candrest[:, t, h, :], top2[:, t, h, 0:8], cand[:, t, h, :], GONE)
                v.drain()
                for t, h in heads:
                    v.max(top2[:, t, h, 8:16], candrest[:, t, h, :])
                v.drain()
                for t in range(NT):
                    v.tensor_tensor(expo[:, t, :, :], top2[:, t, :, :],
                                    top2[:, t, :, 0:1].broadcast_to([P, HEADS, PICKS]), ALU.subtract)
                v.drain().then_inc(gexp_in, 1)
                for t, h in heads:
                    v.max_index(pos2u[:, t, h, 8:16], top2[:, t, h, 8:16], candrest[:, t, h, :])
                v.drain()
                v.tensor_scalar(whichu[:, 0], pos2u[:, :, :, :], 4, None, ALU.logical_shift_right)
                v.tensor_scalar(whichu[:, 1], pos2u[:, :, :, :], PICKS - 1, None, ALU.bitwise_and)
                v.tensor_copy(top1[:, :, :, :], idx1u[:, :, :, :])
                v.drain()
                v.tensor_copy(whichf[:, :, :, :, :], whichu[:, :, :, :, :])
                v.drain()
                for t in range(NT):
                    for s in range(2):
                        shape = [P, HEADS, PICKS, PICKS]
                        eq = (cand if s == 0 else candrest)[:, t, :, :].rearrange("p h (k j) -> p h k j", k=PICKS)
                        v.tensor_tensor(eq, iota[:, 0:PICKS].unsqueeze(1).unsqueeze(1).broadcast_to(shape),
                                        whichf[:, s, t, :, :].unsqueeze(3).broadcast_to(shape), ALU.is_equal)
                v.drain()
                for t in range(NT):
                    for s in range(2):
                        eq = (cand if s == 0 else candrest)[:, t, :, :].rearrange("p h (k j) -> p h k j", k=PICKS)
                        tv = top1[:, t, :, :].rearrange("p (h s) k -> p h s k", s=2)
                        v.tensor_tensor(eq, eq, tv[:, :, s, :].unsqueeze(2).broadcast_to(shape), ALU.mult)
                v.drain()
                for t in range(NT):
                    for s in range(2):
                        eq = (cand if s == 0 else candrest)[:, t, :, :].rearrange("p h (k j) -> p h k j", k=PICKS)
                        v.tensor_reduce(picks[:, s, t, :, :], eq, AX.X, ALU.add)
                v.wait_ge(gexp_out, 1)
                v.tensor_reduce(gsum[:, :, :], expo[:, :, :, :], AX.X, ALU.add)
                v.drain()
                v.reciprocal(grec[:, :, :], gsum[:, :, :])
                v.drain()
                v.tensor_tensor(picks[:, 2], expo[:, :, :, :],
                                grec[:, :, :].unsqueeze(3).broadcast_to([P, NT, HEADS, PICKS]), ALU.mult)
                v.drain().then_inc(picks_ready, 1)

                v.wait_ge(pickT_ready, 2)
                with v.Fori(0, SEQ // 8) as i:
                    for b in range(2):
                        v.wait_ge(g_ps, i * 2 + (b + 1))
                        for j in range(4):
                            tok = bass.ds(i * 8 + (4 * b + j), 1)
                            v.tensor_scalar(onehot1[:, b, j, :], iota[:, :], pickT[:, 0, tok], None, ALU.is_equal)
                            ins = v.tensor_scalar(onehot2[:, b, j, :], iota[:, :], pickT[:, 1, tok], pickT[:, 2, tok],
                                                  ALU.is_equal, ALU.mult)
                        ins.then_inc(hot_ready, 1)
                v.wait_ge(g_ready, SEQ // 4 + 2)
                v.sem_inc(wgt_ready, 2)
                with v.Fori(0, NCHUNK // 2) as i:
                    for b in range(2):
                        v.wait_ge(act_ready, i * 2 + (b + 1))
                        v.wait_ge(wgt_used, i * 2 + (b + 1))
                        v.tensor_tensor(wgt[:, b, :], act[:, b, :], G[:, :, bass.ds(i * 2 + b, 1)].squeeze(2),
                                        ALU.mult).then_inc(wgt_ready, 1)
                v.wait_ge(wgt_used, NCHUNK + 2)
                for n in range(4):
                    xs = x[:, n // 2, (n % 2) * 512:(n % 2) * 512 + 512]
                    v.tensor_tensor(xs, bank(n), xs, ALU.add)
                v.drain().then_inc(xn_ready, 1)

                v.wait_ge(pw_ready, 1)
                rsqrt_mean(4, psq[:, :], D)
                norm_x(2)
                for t in range(NT):
                    v.scalar_tensor_tensor(pw[:, t, :], pw[:, t, :], prstd[:, t:t + 1], par[:, Q_PLEN:Q_PLEN + D],
                                           ALU.mult, ALU.mult)
                v.drain()
                v.wait_ge(pg_ready, 4)
                for t in range(NT):
                    v.tensor_tensor(pw[:, t, :], pw[:, t, :], gate[:, t, :], ALU.mult)
                v.drain()
                for t in range(NT):
                    v.tensor_tensor(x[:, t, :], x[:, t, :], pw[:, t, :], ALU.add)
                v.drain().then_inc(layer_done, 1)
                v.wait_ge(layer_go, layer + 1)

        @block.tensor
        def _(pe):
            pe.wait_ge(consts_pool, 1)
            pe.wait_ge(consts_dve, 1)
            with pe.Fori(0, DEPTH) as layer:
                turns = PAIRS // RING * 16

                def block_of(n):
                    return ring[:, (n // 2) % RING, n % 2, :]

                def arrive(n):
                    if n % 2 == 0:
                        p = n // 2
                        pe.wait_ge(pair_full[p % RING], layer * turns + 16 * (p // RING + 1))

                owed = [0]

                def settle(ins):
                    if owed[0]:
                        ins.then_inc(pair_free, owed[0])
                        owed[0] = 0

                def norm_T(m, b0):
                    pe.wait_ge(xn_ready, [1, 3, 5][m])
                    for j in range(4):
                        for k in (2 * j, 2 * j + 1):
                            for t in range(NT):
                                ins = pe.transpose(bank(b0 + j, (k % 2) * SEQ + t * P, (k % 2) * SEQ + t * P + P),
                                                   xn[:, t, k * P:(k + 1) * P], ident[:, :])
                                settle(ins)
                        ins.then_inc(xT_ps, 1)
                    pe.wait_ge(hT_ready, 4 * (m + 1))

                norm_T(0, 4)
                for cb, (c0, w) in enumerate(ROW_BLOCKS):
                    for t in range(NT):
                        n = cb * NT + t
                        if n >= 4:
                            pe.wait_ge(row_ready, n - 3)
                        for k in range(NK):
                            blk = B_ROW + 4 * cb + k // 2
                            if t == 0 and k % 2 == 0:
                                arrive(blk)
                            wv = block_of(blk).rearrange("p (k c) -> p k c", k=2)
                            ins = pe.matmul(bank(n % 4, 0, w), hT[:, k, t * P:(t + 1) * P], wv[:, k % 2, 0:w],
                                            start=(k == 0), stop=(k == NK - 1))
                            settle(ins)
                            if t == NT - 1 and k == 3:
                                ins.then_inc(pair_free, 1)
                        owed[0] += t == NT - 1
                        ins.then_inc(row_ps, 1)
                for c in range(16):
                    blk = B_GATE + c
                    arrive(blk)
                    if c % 2 == 0 and c >= 4:
                        pe.wait_ge(mg_ready, c // 2 - 1)
                    wv = block_of(blk).rearrange("p (k c) -> p k c", k=NK)
                    for k in range(NK):
                        ins = pe.matmul(bank(4 + (c // 2) % 2, (c % 2) * SEQ, (c % 2 + 1) * SEQ), wv[:, k, :],
                                        hT[:, k, :], start=(k == 0), stop=(k == NK - 1))
                        settle(ins)
                    if c % 2:
                        ins.then_inc(mg_ps, 1)
                        owed[0] += 1

                pe.wait_ge(cdup_ready, 1)
                for kv in range(2):
                    for gr in range(2):
                        for t in range(NT):
                            ins = pe.transpose(bank(kv, gr * SEQ + t * P, gr * SEQ + t * P + P),
                                               cdup[:, t, 2 * kv + gr, :], ident[:, :])
                            settle(ins)
                ins.then_inc(cmp_ps, 1)
                pe.wait_ge(rope_done, 1)

                def transposes(n):
                    if n >= 4:
                        pe.wait_ge(qk_ready, n - 3)
                    for s in (2 * n, 2 * n + 1):
                        for t in range(NT):
                            src = rows[:, t, T_SRC[s]:T_SRC[s] + P] if s < T_KS else kdup[:, t, s - T_KS, :]
                            ins = pe.transpose(bank(4 + n % 4, (s % 2) * SEQ + t * P, (s % 2) * SEQ + t * P + P),
                                               src, ident[:, :])
                            settle(ins)
                    ins.then_inc(qk_ps, 1)

                pe.wait_ge(mg_ready, 8)
                pe.wait_ge(z_ready, 1)
                for kv in range(2):
                    for b in range(4):
                        blk = B_W1 + 4 * kv + b
                        arrive(blk)
                    for half in range(2):
                        for j in range(16):
                            wv = block_of(B_W1 + 4 * kv + j // 4).rearrange("p (j c) -> p j c", j=4)
                            ins = pe.matmul(bank(2 + kv, half * 32, half * 32 + 32),
                                            wv[:, j % 4, half * P:(half + 1) * P],
                                            Z[:, kv, j, :, :].rearrange("p g n -> p (g n)"),
                                            start=(j == 0), stop=(j == 15))
                            settle(ins)
                            if half == 1 and j == 7:
                                ins.then_inc(pair_free, 1)
                    owed[0] += 1
                    ins.then_inc(cmp_ps, 1)
                for n in range(9):
                    transposes(n)
                pe.wait_ge(hid_ready, 2)
                w2 = par[:, Q_W2:Q_W2 + 4 * HD].rearrange("p (v f d) -> p v f d", v=2, f=2)
                for half in range(2):
                    pe.matmul(ps[0:2 * CP, 3, 0:HD], hidT[:, half, :], w2[:, 0, half, :],
                              start=(half == 0), stop=(half == 1))
                for half in range(2):
                    ins = pe.matmul(bank(3, 64, 128), hidv[:, half, :], w2[:, 1, half, :], start=(half == 0), stop=(half == 1))
                ins.then_inc(cmp_ps, 1)
                pe.wait_ge(kc_ready, 1)
                pe.transpose(bank(3, 128, 128 + 2 * CP), kcdup[0:2 * CP, :],
                             ident[0:2 * CP, 0:2 * CP]).then_inc(cmp_ps, 1)

                def side(h):
                    return (h % 2) * HD

                pe.wait_ge(qk_ready, 9)
                pe.wait_ge(kcT_ready, 1)
                for t in range(NT):
                    keys = (t + 1) * P
                    per = 512 // keys
                    for h in range(HEADS):
                        lo = side(h)
                        at = h % 2 * 4 + h // 2
                        ins = pe.matmul(bank(2 * t + at // per, (at % per) * keys, (at % per + 1) * keys),
                                        qkT[lo:lo + HD, T_IQ + h // 2, t * P:(t + 1) * P],
                                        qkT[lo:lo + HD, T_IK, 0:keys], start=True, stop=True)
                    ins.then_inc(idx_ps, 1)
                for t in range(NT):
                    for h in range(HEADS):
                        lo = side(h)
                        gr = h // 4
                        ins = pe.matmul(bank(6 + h % 2, t * HD + h // 2 * CP, t * HD + (h // 2 + 1) * CP),
                                        qkT[lo:lo + HD, T_NQ + h // 2, t * P:(t + 1) * P],
                                        kcT[lo:lo + HD, gr * CP:(gr + 1) * CP], start=True, stop=True)
                ins.then_inc(cs_ps, 1)
                pe.wait_ge(pc_ready, 1)
                for t in range(NT):
                    ins = pe.transpose(bank(6, t * P, t * P + P), pc[:, t, :], ident[:, :])
                ins.then_inc(pcT_ps, 1)
                pe.wait_ge(pcT_ready, 1)
                pe.wait_ge(relu_ready, 2)
                for t in range(NT):
                    pe.matmul(bank(t), relu[:, 0, t * P:(t + 1) * P], vcblk[:, :, :].rearrange("p h d -> p (h d)"),
                              start=True, stop=True).then_inc(oc_ps, 1)
                pe.wait_ge(y_added, 1)

                def scores(i):
                    b, t, hf = ITEMS[i]
                    keys = (t + 1) * P
                    if i >= 2:
                        pe.wait_ge(sm_ready, i - 1)
                    for j in range(4):
                        h = 4 * hf + j
                        lo = side(h)
                        q = (T_DQ if b == 2 else T_NQ) + h // 2
                        k = (T_KS + h // 4, T_KW + h // 4, T_KB)[b]
                        ins = pe.matmul(bank(2 * (i % 2) + j % 2, (j // 2) * keys, (j // 2 + 1) * keys),
                                        qkT[lo:lo + HD, q, t * P:(t + 1) * P], qkT[lo:lo + HD, k, 0:keys],
                                        start=True, stop=True)
                    ins.then_inc(s_ps, 1)

                def prob_T(i):
                    _, t, _ = ITEMS[i]
                    pe.wait_ge(prob_ready, i + 1)
                    if i >= 1:
                        pe.wait_ge(pT_ready, i)
                    for b in range(t + 1):
                        for j in range(4):
                            ins = pe.transpose(bank(4 + b, j * P, (j + 1) * P), prob[:, i % 2, j, b * P:(b + 1) * P],
                                               ident[:, :])
                    ins.then_inc(pT_ps, 1)

                def outputs(i):
                    b, t, hf = ITEMS[i]
                    pe.wait_ge(pT_ready, i + 1)
                    if i >= 2:
                        pe.wait_ge(y_added, i)
                    for j in range(4):
                        col = (C_VS + (4 * hf + j) // 4 * HD, C_VW + (4 * hf + j) // 4 * HD, C_VB)[b]
                        for kb in range(t + 1):
                            ins = pe.matmul(bank(6 + i % 2, j * HD, (j + 1) * HD),
                                            probT[:, i % 2, kb, j * P:(j + 1) * P], rows[:, kb, col:col + HD],
                                            start=(kb == 0), stop=(kb == t))
                    ins.then_inc(o_ps, 1)

                n_items = len(ITEMS)
                scores(0)
                for i in range(n_items):
                    if i + 1 < n_items:
                        scores(i + 1)
                    prob_T(i)
                    if i:
                        outputs(i - 1)
                outputs(n_items - 1)
                pe.wait_ge(y_added, n_items + 1)
                for n in range(4):
                    m = n // 2
                    for k in (2 * (n % 2), 2 * (n % 2) + 1):
                        for t in range(NT):
                            ins = pe.transpose(bank(n, (k % 2) * SEQ + t * P, (k % 2) * SEQ + t * P + P),
                                               y[:, m, t, k * P:(k + 1) * P], ident[:, :])
                    ins.then_inc(yT_ps, 1)
                pe.wait_ge(yT_ready, 4)
                for m in range(NK):
                    if m >= 4:
                        pe.wait_ge(br_ready, m - 3)
                    for br in range(2):
                        blk = B_BR + 2 * (m // 2) + br
                        if m % 2 == 0:
                            arrive(blk)
                        wv = block_of(blk).rearrange("p (k c) -> p k c", k=4)
                        for k in range(4):
                            ins = pe.matmul(bank(4 + m % 4, br * SEQ, (br + 1) * SEQ),
                                            wv[:, k, (m % 2) * P:(m % 2 + 1) * P], yT[:, br, k, :],
                                            start=(k == 0), stop=(k == 3))
                            settle(ins)
                    ins.then_inc(br_ps, 1)
                    owed[0] += m % 2

                def streamed(blk, b0, left, nk):
                    for k in range(nk):
                        arrive(blk + k)
                        for n in range(4):
                            t = n // 2
                            ins = pe.matmul(bank(b0 + n), left[:, k, t * P:(t + 1) * P],
                                            block_of(blk + k)[:, (n % 2) * 512:(n % 2) * 512 + 512],
                                            start=(k == 0), stop=(k == nk - 1))
                            settle(ins)
                        if k % 2 and k < nk - 1:
                            ins.then_inc(pair_free, 1)
                    owed[0] += 1
                    return ins

                pe.wait_ge(br_ready, NK)
                streamed(B_OUT, 0, mergedT, NK).then_inc(wo_ps, 1)

                norm_T(1, 4)
                sub = par[:, Q_SUB:Q_SUB + 2 * NKEYS].rearrange("p (s n) -> p s n", s=2)
                for c in range(16):
                    blk = B_WQ + c
                    arrive(blk)
                    if c % 2 == 0 and c >= 4:
                        pe.wait_ge(q_ready, c // 2 - 1)
                    wv = block_of(blk).rearrange("p (k c) -> p k c", k=NK)
                    for k in range(NK):
                        ins = pe.matmul(bank((c // 2) % 2, (c % 2) * SEQ, (c % 2 + 1) * SEQ), wv[:, k, :],
                                        hT[:, k, :], start=(k == 0), stop=(k == NK - 1))
                        settle(ins)
                    if c % 2:
                        ins.then_inc(q_ps, 1)
                        owed[0] += 1
                    if c % 4 == 3:
                        pe.wait_ge(q_ready, (c + 1) // 2)
                        for t in range(NT):
                            if c >= 7:
                                pe.wait_ge(ks_ready, (c // 4 - 1) * 2 + t + 1)
                            for j in range(4):
                                cc = c - 3 + j
                                ins = pe.matmul(bank(2 + t, j * P, (j + 1) * P), qPT[:, cc, t * P:(t + 1) * P],
                                                sub[:, cc % 2, :], start=True, stop=True)
                                settle(ins)
                            ins.then_inc(ks_ps, 1)
                pe.wait_ge(picks_ready, 1)
                for w in range(3):
                    for t in range(NT):
                        ins = pe.transpose(bank(6 + w // 2, (w % 2) * SEQ + t * P, (w % 2) * SEQ + t * P + P),
                                           picks[:, w, t, :, :].rearrange("p h k -> p (h k)"), ident[:, :])
                ins.then_inc(pickT_ps, 1)
                pe.wait_ge(pickT_ready, 2)
                pe.sem_inc(g_ps, 2)
                with pe.Fori(0, SEQ // 8) as i:
                    for b in range(2):
                        pe.wait_ge(hot_ready, i * 2 + (b + 1))
                        pe.wait_ge(g_ready, i * 2 + (b + 1))
                        for j in range(4):
                            ins = pe.matmul(bank(4 + b, j * P, (j + 1) * P), onehot2[:, b, j, :], onehot1[:, b, j, :],
                                            start=True, stop=True)
                        ins.then_inc(g_ps, 1)

                for n in range(4):
                    pe.matmul(bank(n), zero16[:, 0:P], zero16[:, :], start=True, stop=False, skip_group_check=True)
                pe.wait_ge(g_ready, SEQ // 4 + 2)
                pe.sem_inc(wgt_used, 2)

                arrive(B_EXP)
                for c in range(2):
                    wv = block_of(B_EXP + c).rearrange("p (k c) -> p k c", k=NK)
                    for k in range(NK):
                        ins = pe.matmul(bank(4 + c, 0, SEQ), wv[:, k, :], hT[:, k, :],
                                        start=(k == 0), stop=(k == NK - 1))
                    ins.then_inc(act_ps, 1)

                def chunk(j, i, first_pair, with_act):
                    slot = (first_pair + j) % RING
                    step = (first_pair + j) // RING
                    c = i * BODY + j
                    pe.wait_ge(pair_full[slot], layer * turns + (i * 16 + 16 * (step + 1)))
                    pe.wait_ge(wgt_ready, c + 3)
                    for n in range(4):
                        t = n // 2
                        ins = pe.matmul(bank(n), wgt[:, j % 2, t * P:(t + 1) * P],
                                        ring[:, slot, 0, (n % 2) * 512:(n % 2) * 512 + 512],
                                        start=False, stop=False, skip_group_check=True)
                        if n == 0:
                            ins.then_inc(pair_free, 1)
                    ins.then_inc(wgt_used, 1)
                    if with_act:
                        wv = ring[:, slot, 1, :].rearrange("p (k c) -> p k c", k=NK)
                        for k in range(NK):
                            ins = pe.matmul(bank(4 + j % 2, 0, SEQ), wv[:, k, :], hT[:, k, :],
                                            start=(k == 0), stop=(k == NK - 1))
                        ins.then_inc(act_ps, 1)

                first_pair = B_EXP // 2 + 1
                with pe.Fori(0, NCHUNK // BODY - 1) as i:
                    for j in range(BODY):
                        chunk(j, i, first_pair, True)
                last = NCHUNK // BODY - 1
                for j in range(BODY - 2):
                    chunk(j, last, first_pair, True)
                p = B_EXP // 2 + NCHUNK - 1
                pe.wait_ge(pair_full[p % RING], layer * turns + 16 * (p // RING + 1))
                for b in range(2):
                    pe.wait_ge(wgt_ready, NCHUNK - 2 + b + 3)
                    for n in range(4):
                        t = n // 2
                        ins = pe.matmul(bank(n), wgt[:, b, t * P:(t + 1) * P],
                                        ring[:, p % RING, b, (n % 2) * 512:(n % 2) * 512 + 512],
                                        start=False, stop=(b == 1), skip_group_check=True)
                        if b == 0 and n == 0:
                            ins.then_inc(pair_free, 1)
                    ins.then_inc(wgt_used, 1)
                owed[0] += 1

                streamed(B_PLEW, 4, par[:, Q_PT:Q_PT + 2 * SEQ].rearrange("p (k t) -> p k t", k=2), 2).then_inc(pw_ps, 1)
                norm_T(2, 0)
                pe.wait_ge(pw_ready, 1)
                streamed(B_PLEG, 4, hT, NK).then_inc(pg_ps, 1)
                for p in range((B_PLEG + 8) // 2, PAIRS):
                    pe.wait_ge(pair_full[p % RING], layer * turns + 16 * (p // RING + 1))
                    owed[0] += 1
                pe.drain().then_inc(pair_free, owed[0])
                pe.drain().then_inc(layer_done, 1)
                pe.wait_ge(layer_go, layer + 1)


def _stream(i):
    import numpy as np

    blocks = np.zeros((DEPTH, PAIRS * 2, P, BLK), np.float32)
    w_in = i["w_in"]
    cuts = [(0, 512), (512 + 256, 512 + 384), (512 + 512, 512 + 640), (1304, 1816), (1816, 1880), (1944, 2456),
            (2456, 2520), (512 + 384, 512 + 512), (512 + 640, 512 + 768), (512, 640), (640, 768), (1880, 1944),
            (1280, 1304), (2520, 2528)]
    for l in range(DEPTH):
        b = blocks[l]
        rows = np.concatenate([w_in[l][:, lo:hi] for lo, hi in cuts], axis=1).reshape(4, 2, P, ROW)
        for cb, (c0, w) in enumerate(ROW_BLOCKS):
            v = b[B_ROW + 4 * cb:B_ROW + 4 * cb + 4].reshape(4, P, 2, 512)
            v[:, :, :, :w] = rows[:, :, :, c0:c0 + w].transpose(0, 2, 1, 3)

        def columns(w):
            return w.reshape(NK, P, -1, P).transpose(2, 1, 0, 3).reshape(-1, P, BLK)

        b[B_GATE:B_GATE + 16] = columns(w_in[l][:, 2528:])
        for v in range(2):
            b[B_W1 + 4 * v:B_W1 + 4 * v + 4] = i["cmp_w1"][l][v].reshape(4, 4, P, 256).transpose(0, 2, 1, 3).reshape(4, P, BLK)
        for m, name in enumerate(("w_branch_a", "w_branch_b")):
            b[B_BR + m:B_BR + 8:2] = i[name][l].reshape(4, P, 4, 256).transpose(2, 1, 0, 3).reshape(4, P, BLK)
        b[B_OUT:B_OUT + 8] = i["w_out"][l].reshape(8, P, D)
        b[B_WQ:B_WQ + 16] = columns(i["peer_wq"][l])
        u = i["peer_u"][l].reshape(NCHUNK, P, NK, P).transpose(0, 3, 2, 1).reshape(NCHUNK, P, BLK)
        v = i["peer_v"][l].reshape(NCHUNK, P, D)
        e = b[B_EXP:B_EXP + 2 * NCHUNK]
        e[0:2] = u[0:2]
        e[2:254:2], e[3:254:2] = v[0:126], u[2:128]
        e[254:256] = v[126:128]
        b[B_PLEW:B_PLEW + 2] = i["ple_w"][l].reshape(2, P, D)
        b[B_PLEG:B_PLEG + 8] = i["ple_gate_w"][l].reshape(8, P, D)
    return np.ascontiguousarray(blocks.reshape(DEPTH * PAIRS, 2, P, BLK).transpose(0, 2, 1, 3))


def _params(i):
    import numpy as np

    par = np.zeros((DEPTH, P, NPARAM), np.float32)
    for l in range(DEPTH):
        q = par[l]
        q[:, Q_GA:Q_GA + NK] = i["attn_norm"][l].reshape(NK, P).T
        q[:, Q_GF:Q_GF + NK] = i["ffn_norm"][l].reshape(NK, P).T
        ga, gd = i["nsa_qk_gain"][l], i["dsa_qk_gain"][l]
        gains = [ga[0]] * 8 + [ga[2]] * 2 + [ga[3]] * 2 + [gd[0]] * 8 + [gd[1]]
        q[:, Q_GAIN:Q_GAIN + NORM_SLOTS * HD] = np.concatenate(gains)[None]
        q[:, Q_CGAIN:Q_CGAIN + HD] = ga[1][None]
        q[:, Q_POS:Q_POS + 32] = i["cmp_pos"][l].reshape(2, 16, 2, HD).transpose(2, 3, 0, 1).reshape(P, 32)
        q[:, Q_W2:Q_W2 + 4 * HD] = i["cmp_w2"][l].reshape(2, 2, P, HD).transpose(2, 0, 1, 3).reshape(P, 4 * HD)
        q[:, Q_SUB:Q_SUB + 2 * NKEYS] = i["peer_sub_keys"][l].transpose(2, 0, 1).reshape(P, 2 * NKEYS)
        q[:, Q_PT:Q_PT + 2 * SEQ] = i["p"][l, 0].T.reshape(2, P, SEQ).transpose(1, 0, 2).reshape(P, 2 * SEQ)
        q[:, Q_PLEN:Q_PLEN + D] = i["ple_norm"][l][None]
    return par


def kernel(**inputs):
    import numpy as np
    import concourse.bacc as bacc
    from concourse.bass_utils import run_bass_kernel_spmd as run

    i = {k: np.asarray(v) for k, v in inputs.items()}
    pos = np.ascontiguousarray(i["positions"])
    posl = np.zeros((P, 3), pos.dtype)
    posl[:, 0:2] = pos[0].reshape(2, P).T
    for gr in range(2):
        posl[gr * CP:gr * CP + NCMP, 2] = pos[0, CMP_LEN - 1::CMP_STRIDE][:NCMP]
    inv = (np.float32(500000.0) ** (-np.arange(ROT2, dtype=np.float32) / ROT2)).astype(np.float32)
    arrays = {
        "in_x": np.ascontiguousarray(i["x"]),
        "in_stream": _stream(i),
        "in_params": _params(i),
        "in_positions": posl,
        "in_inv_freq": np.ascontiguousarray(np.broadcast_to(inv, (P, ROT2))),
    }
    nc = bacc.Bacc("TRN2", target_bir_lowering=False, num_devices=1)
    args = [nc.dram_tensor(n, a.shape, mybir.dt.from_np(a.dtype), kind="ExternalInput").ap() for n, a in arrays.items()]
    o = nc.dram_tensor("out_0", (1, SEQ, D), F32, kind="ExternalOutput").ap()
    build(nc, *args, o)
    r = run(nc, [arrays], core_ids=[0])
    return r.results[0]["out_0"]
```

```python
from contextlib import ExitStack

import concourse.bass as bass
from concourse import mybir

F32 = mybir.dt.float32
F32R = mybir.dt.float32r
BF16 = mybir.dt.bfloat16
I32 = mybir.dt.int32
U32 = mybir.dt.uint32
ALU = mybir.AluOpType
ACT = mybir.ActivationFunctionType
AX = mybir.AxisListType

P = 128
DEPTH, SEQ, D = 2, 256, 1024
NT = SEQ // P
NK = D // P
HD = 64
HEADS = 8
ROT2 = HD // 8
EPS = 1e-6
NEG = -1e30
GONE = -3e38
SCALE = HD ** -0.5
CMP_STRIDE, CMP_LEN, NCMP = 16, 32, 15
CP = 16
TOPK_ROUNDS = 64 // 8
PICKS = 16
NKEYS = 128
PLE = 256

C_NQ, C_KS, C_KW, C_DQ, C_KB, C_IQ, C_IK = 0, 512, 640, 768, 1280, 1344, 1856
C_VS, C_VW, C_CK, C_CV, C_VB, C_NG, C_IW = 1920, 2048, 2176, 2304, 2432, 2496, 2520
ROW = 2528
ROPE_SLOTS, NORM_SLOTS = 30, 21
ROW_BLOCKS = [(b * 512, min(512, ROW - b * 512)) for b in range((ROW + 511) // 512)]

BLK = 1024
B_ROW = 0
B_GATE = B_ROW + 4 * len(ROW_BLOCKS)
B_W1 = B_GATE + 16
B_BR = B_W1 + 8
B_OUT = B_BR + 8
B_WQ = B_OUT + 8
B_EXP = B_WQ + 16
NCHUNK = 128
B_PLEW = B_EXP + 2 * NCHUNK
B_PLEG = B_PLEW + 2
RING = 2
PAIRS = -(-(B_PLEG + 8) // 2)
PAIRS += -PAIRS % RING
ACT_HOTS = (1, 1)
BODY = 2

Q_GA, Q_GF, Q_GAIN, Q_CGAIN = 0, 8, 16, 16 + NORM_SLOTS * HD
Q_POS = Q_CGAIN + HD
Q_W2 = Q_POS + 32
Q_SUB = Q_W2 + 4 * HD
Q_END = Q_SUB + 2 * NKEYS
Q_PT = Q_END
Q_PLEN = Q_PT + 2 * SEQ
NPARAM = Q_PLEN + D

T_NQ, T_DQ, T_IQ, T_KS, T_KW, T_KB, T_IK = 0, 4, 8, 12, 14, 16, 17
T_SRC = [c + 128 * j for c in (C_NQ, C_DQ, C_IQ) for j in range(4)]

ITEMS = [(b, t, hf) for b in range(3) for t in range(NT) for hf in range(2)]


def build(nc, x_in, stream, params, positions, inv_freq, out):
    ctx = ExitStack()
    with ctx:
        def sb(name, shape, dt=F32):
            return ctx.enter_context(nc.sbuf_tensor(name, shape, dt))

        layer_sems = []

        def sem(name, cleared=True):
            s = ctx.enter_context(nc.semaphore(name))
            if cleared:
                layer_sems.append(s)
            return s

        ps = ctx.enter_context(nc.psum_tensor("ps", [P, 8, 512], F32))

        x = sb("x", [P, NT, D])
        hT = sb("hT", [P, NK, SEQ])
        hs = sb("hs", [P, 2, NK * SEQ], F32R)
        split = sb("split", [P, 2, 2, 2, BLK], F32R)
        wgt = sb("wgt", [P, 2, 2, SEQ], F32R)
        ring = sb("ring", [P, RING, 2, BLK])
        pT = sb("pT", [P, 2 * SEQ])
        ident = sb("ident", [P, P])
        iota = sb("iota", [P, P])
        causal = sb("causal", [P, SEQ])
        cmask = sb("cmask", [P, NT, CP])
        cneg = sb("cneg", [P, NT, CP])
        headmask = sb("headmask", [P, HEADS])
        minus_half = sb("minus_half", [P, NT * NORM_SLOTS])
        zero16 = sb("zero16", [P, 512], BF16)
        cos = sb("cos", [P, NT + 1, ROT2])
        sin = sb("sin", [P, NT + 1, ROT2])
        small = sb("small", [P, 480])
        pickT = sb("pickT", [P, 3, SEQ])
        neg2 = sb("neg2", [P, SEQ])
        rest = hT[:, :, :].rearrange("p k t -> p (k t)")
        onehot1 = rest[:, 0:1024].rearrange("p (b j i) -> p b j i", b=2, j=4)
        onehot2 = rest[:, 1024:2048].rearrange("p (b j i) -> p b j i", b=2, j=4)
        act = rest[:, 0:2 * SEQ].rearrange("p (b t) -> p b t", b=2)

        big = sb("big", [P, SEQ * NKEYS])
        G = big[:, :].rearrange("p (t i) -> p t i", t=SEQ)
        used = [0]

        def carve(n, *dims, **kw):
            a = big[:, used[0]:used[0] + n]
            used[0] += n
            assert used[0] <= SEQ * NKEYS
            return a.rearrange(*dims, **kw) if dims else a

        xn = carve(NT * D, "p (t d) -> p t d", t=NT)
        par = carve(Q_END)
        rows = carve(NT * ROW, "p (t c) -> p t c", t=NT)
        tmp = carve(NT * NORM_SLOTS * HD)
        qkT = carve(18 * SEQ, "p (s t) -> p s t", s=18)
        gateT = carve(16 * SEQ, "p (m t) -> p m t", m=16)
        Z = carve(2 * 16 * 2 * CP, "p (v j g n) -> p v j g n", v=2, j=16, g=2)
        hidT = carve(2 * 2 * CP, "p (f c) -> p f c", f=2)
        hidv = carve(2 * P, "p (f c) -> p f c", f=2)
        kcdup = carve(P)
        vcblk = carve(HEADS * HD, "p (h d) -> p h d", h=HEADS)
        kc = carve(HD)
        kcT = carve(2 * CP)
        relu = carve(HEADS * SEQ, "p (h s) -> p h s", h=HEADS)
        score = carve(NT * SEQ, "p (t s) -> p t s", t=NT)
        dmask = carve(NT * SEQ, "p (t s) -> p t s", t=NT)
        over = used[0]
        cdup = carve(NT * 4 * P, "p (t s c) -> p t s c", t=NT, s=4)
        kdup = carve(NT * 6 * P, "p (t s c) -> p t s c", t=NT, s=6)
        used[0] = over
        sm = carve(2 * 4 * SEQ, "p (i h s) -> p i h s", i=2, h=4)
        prob = carve(2 * 4 * SEQ, "p (i h s) -> p i h s", i=2, h=4)
        probT = carve(2 * 2 * 512, "p (i b c) -> p i b c", i=2, b=2)
        pc = carve(NT * P, "p (t c) -> p t c", t=NT)
        y = big[:, 0:NT * D].rearrange("p (m t c) -> p m t c", m=2, t=NT)
        o_tmp = carve(512)
        used[0] = NT * D + Q_END
        yT = carve(2 * 4 * SEQ, "p (m k t) -> p m k t", m=2, k=4)
        mergedT = carve(NK * SEQ, "p (k t) -> p k t", k=NK)
        gate_prod = carve(2 * SEQ)
        assert used[0] <= NT * D + Q_END + NT * ROW + NT * NORM_SLOTS * HD
        used[0] = NT * D + Q_END
        qPT = carve(16 * SEQ, "p (c t) -> p c t", c=16)
        keyscore = carve(NT * 16 * NKEYS, "p (t c n) -> p t c n", t=NT, c=16)
        keyrest = carve(NT * 16 * NKEYS, "p (t c n) -> p t c n", t=NT, c=16)
        top1 = carve(NT * 16 * PICKS, "p (t c k) -> p t c k", t=NT, c=16)
        idx1 = carve(NT * 16 * PICKS, "p (t c k) -> p t c k", t=NT, c=16)
        cand = carve(NT * HEADS * 256, "p (t h c) -> p t h c", t=NT, h=HEADS)
        candrest = carve(NT * HEADS * 256, "p (t h c) -> p t h c", t=NT, h=HEADS)
        top2 = carve(NT * 128, "p (t h k) -> p t h k", t=NT, h=HEADS)
        pos2 = carve(NT * 128, "p (t h k) -> p t h k", t=NT, h=HEADS)
        which = carve(2 * NT * 128, "p (v t h k) -> p v t h k", v=2, t=NT, h=HEADS)
        whichf = carve(2 * NT * 128, "p (v t h k) -> p v t h k", v=2, t=NT, h=HEADS)
        picks = carve(3 * NT * 128, "p (v t h k) -> p v t h k", v=3, t=NT, h=HEADS)
        expo = carve(NT * 128, "p (t h k) -> p t h k", t=NT, h=HEADS)
        used[0] = NT * D
        pw = carve(NT * D, "p (t d) -> p t d", t=NT)
        gate = carve(NT * D, "p (t d) -> p t d", t=NT)
        plen = carve(D)

        junk = big[:, SEQ * NKEYS - D:SEQ * NKEYS]
        idx1u = idx1.bitcast(U32)
        pos2u = pos2.bitcast(U32)
        whichu = which.bitcast(U32)

        ss = small[:, 0:2]
        rstd = small[:, 2:4]
        psq = small[:, 4:6]
        prstd = small[:, 6:8]
        ms = small[:, 8:50].rearrange("p (t s) -> p t s", t=NT)
        msr = small[:, 50:92].rearrange("p (t s) -> p t s", t=NT)
        sg = small[:, 92:140].rearrange("p (t s) -> p t s", t=NT)
        iwb = small[:, 140:156].rearrange("p (t s) -> p t s", t=NT)
        cms = small[:, 156:158]
        maxes = small[:, 160:208].rearrange("p (i h) -> p i h", h=4)
        nmax = small[:, 208:256].rearrange("p (i h) -> p i h", h=4)
        sums = small[:, 256:304].rearrange("p (i h) -> p i h", h=4)
        coef = small[:, 304:352].rearrange("p (i h) -> p i h", h=4)
        csum = small[:, 352:368].rearrange("p (t h) -> p t h", t=NT)
        ccoef = small[:, 368:384].rearrange("p (t h) -> p t h", t=NT)
        cmax = small[:, 384:400].rearrange("p (t h) -> p t h", t=NT)
        gsum = small[:, 400:416].rearrange("p (t h) -> p t h", t=NT)
        top8 = small[:, 416:432].rearrange("p (t k) -> p t k", t=NT)
        gmax = small[:, 432:448].rearrange("p (t h) -> p t h", t=NT)
        grec = small[:, 448:464].rearrange("p (t h) -> p t h", t=NT)

        rms_steps = [rstd, msr, cms[0:2 * CP, 1:2], rstd, prstd, rstd]

        def bank(b, lo=0, hi=512):
            return ps[:, b, lo:hi]

        in_dma = sem("in_dma", False)
        consts_pool = sem("consts_pool", False)
        consts_dve = sem("consts_dve", False)
        consts_act = sem("consts_act", False)
        angle_done = sem("angle_done", False)
        pair_full = [sem(f"pair_full{s}", False) for s in range(RING)]
        pair_free = sem("pair_free", False)
        out_dma = sem("out_dma", False)
        layer_done = sem("layer_done", False)
        layer_over = sem("layer_over", False)
        layer_go = sem("layer_go", False)
        params_in = sem("params_in")
        squares = sem("squares")
        rms_in = sem("rms_in")
        rms_out = sem("rms_out")
        xn_ready = sem("xn_ready")
        xT_ps = sem("xT_ps")
        hT_ready = sem("hT_ready")
        row_ps = sem("row_ps")
        row_ready = sem("row_ready")
        mg_ps = sem("mg_ps")
        mg_ready = sem("mg_ready")
        cdup_ready = sem("cdup_ready")
        sg_ready = sem("sg_ready")
        rope_done = sem("rope_done")
        qk_ps = sem("qk_ps")
        qk_ready = sem("qk_ready")
        cmp_ps = sem("cmp_ps")
        z_ready = sem("z_ready")
        hid_ready = sem("hid_ready")
        kc_ready = sem("kc_ready")
        kcT_ready = sem("kcT_ready")
        idx_ps = sem("idx_ps")
        relu_ready = sem("relu_ready")
        relu_used = sem("relu_used")
        cs_ps = sem("cs_ps")
        cs_sub = sem("cs_sub")
        cs_exp = sem("cs_exp")
        pc_ready = sem("pc_ready")
        pcT_ps = sem("pcT_ps")
        pcT_ready = sem("pcT_ready")
        oc_ps = sem("oc_ps")
        s_ps = sem("s_ps")
        sm_ready = sem("sm_ready")
        prob_ready = sem("prob_ready")
        pT_ps = sem("pT_ps")
        pT_ready = sem("pT_ready")
        o_ps = sem("o_ps")
        y_added = sem("y_added")
        yT_ps = sem("yT_ps")
        yT_ready = sem("yT_ready")
        br_ps = sem("br_ps")
        br_ready = sem("br_ready")
        wo_ps = sem("wo_ps")
        q_ps = sem("q_ps")
        q_ready = sem("q_ready")
        ks_ps = sem("ks_ps")
        ks_ready = sem("ks_ready")
        picks_ready = sem("picks_ready")
        gexp_in = sem("gexp_in")
        gexp_out = sem("gexp_out")
        pickT_ps = sem("pickT_ps")
        pickT_ready = sem("pickT_ready")
        hot_ready = sem("hot_ready")
        act_hot_ready = sem("act_hot_ready")
        g_ps = sem("g_ps")
        g_ready = sem("g_ready")
        hs_ready = sem("hs_ready")
        hi_ready = sem("hi_ready")
        lo_ready = sem("lo_ready")
        plen_in = sem("plen_in")
        act_ps = sem("act_ps")
        act_ready = sem("act_ready")
        wgt_ready = sem("wgt_ready")
        wgt_used = sem("wgt_used")
        pw_ps = sem("pw_ps")
        pw_ready = sem("pw_ready")
        pg_ps = sem("pg_ps")
        pg_ready = sem("pg_ready")
        ENGINES = 4

        block = ctx.enter_context(nc.Block())

        @block.sync
        def _(sp):
            sp.dma_start(x[:, :, :], x_in.rearrange("o (t p) d -> p (o t) d", p=P)).then_inc(in_dma, 16)
            sp.dma_start(small[:, 0:8], inv_freq).then_inc(in_dma, 16)
            sp.dma_start(small[:, 8:11].bitcast(I32), positions).then_inc(in_dma, 16)
            for s in range(RING):
                sp.dma_start(ring[:, s, :, :], stream[s]).then_inc(pair_full[s], 16)
            with sp.Fori(1, DEPTH * PAIRS // RING) as turn:
                for s in range(RING):
                    need = sp.snap(turn * RING + (s + 1 - RING))
                    src = sp.snap(turn * RING + s)
                    sp.wait_ge(pair_free, need)
                    sp.dma_start(ring[:, s, :, :],
                                 stream[bass.ds(src, 1)].rearrange("o p b c -> p (o b) c")).then_inc(pair_full[s], 16)
            sp.wait_ge(layer_go, DEPTH)
            sp.dma_start(out.rearrange("o (t p) d -> p (o t) d", p=P), x[:, :, :]).then_inc(out_dma, 16)
            sp.wait_ge(out_dma, 16)

        @block.gpsimd
        def _(g):
            g.memset(ident[:, :], 0.0)
            g.memset(causal[:, :], 0.0)
            g.memset(minus_half[:, :], -0.5)
            g.memset(cmask[:, :, :], 1.0)
            g.memset(cneg[:, :, :], 0.0)
            g.memset(headmask[:, :], 1.0)
            g.iota(iota[:, :], pattern=[[1, P]], base=0, channel_multiplier=0, allow_small_or_imprecise_dtypes=True)
            g.drain()
            g.affine_select(out=ident[:, :], in_=ident[:, :], compare_op=ALU.not_equal, fill=1.0,
                            base=0, pattern=[[-1, P]], channel_multiplier=1)
            g.affine_select(out=causal[:, :], in_=causal[:, :], compare_op=ALU.is_ge, fill=NEG,
                            base=P, pattern=[[-1, SEQ]], channel_multiplier=1)
            g.affine_select(out=cmask[:, :, :], in_=cmask[:, :, :], compare_op=ALU.is_ge, fill=0.0,
                            base=-(CMP_LEN - 1), pattern=[[P, NT], [-CMP_STRIDE, CP]], channel_multiplier=1)
            g.affine_select(out=cneg[:, :, :], in_=cneg[:, :, :], compare_op=ALU.is_ge, fill=NEG,
                            base=-(CMP_LEN - 1), pattern=[[P, NT], [-CMP_STRIDE, CP]], channel_multiplier=1)
            g.affine_select(out=headmask[:, :], in_=headmask[:, :], compare_op=ALU.is_ge, fill=0.0,
                            base=0, pattern=[[-CP, HEADS]], channel_multiplier=1)
            g.drain()
            g.affine_select(out=headmask[:, :], in_=headmask[:, :], compare_op=ALU.is_ge, fill=0.0,
                            base=CP - 1, pattern=[[CP, HEADS]], channel_multiplier=-1)
            g.drain().then_inc(consts_pool, 1)
            with g.Fori(0, DEPTH) as layer:
                for n, v in enumerate(rms_steps):
                    g.wait_ge(rms_in, n + 1)
                    flat = v if len(v.shape) == 2 else v.rearrange("p a b -> p (a b)")
                    g.tensor_tensor(flat, flat, minus_half[0:v.shape[0], 0:flat.shape[1]], ALU.pow).then_inc(rms_out, 1)
                g.drain().then_inc(layer_done, 1)
                g.wait_ge(layer_done, layer * ENGINES + ENGINES)
                g.sem_inc(layer_over, 1)
                for s in layer_sems:
                    g.sem_clear(s)
                g.sem_inc(layer_go, 1)

        @block.scalar
        def _(a):
            a.wait_ge(angle_done, 1)
            a.activation(sin[:, :, :], sin[:, :, :], ACT.Sin)
            a.activation(cos[:, :, :], cos[:, :, :], ACT.Sin)
            a.drain().then_inc(consts_act, 1)
            a.wait_ge(in_dma, 3 * 16)

            def norm_squares():
                for t in range(NT):
                    a.activation(junk, x[:, t, :], ACT.Square, accum_out=ss[:, t:t + 1])
                    a.drain()
                a.drain().then_inc(squares, 1)

            def norm_hT(m, b0, gain):
                for j in range(4):
                    a.wait_ge(xT_ps, 4 * m + j + 1)
                    for k in (2 * j, 2 * j + 1):
                        src = bank(b0 + j, (k % 2) * SEQ, (k % 2 + 1) * SEQ)
                        ins = a.activation(hT[:, k, :], src, ACT.Copy,
                                           scale=1.0 if gain is None else par[:, gain + k:gain + k + 1])
                    ins.then_inc(hT_ready, 1)

            with a.Fori(0, DEPTH) as layer:
                mine = params[bass.ds(layer, 1)].rearrange("o p c -> p (o c)")
                a.dma_start(par, mine[:, 0:Q_END]).then_inc(params_in, 16)
                a.dma_start(pT[:, :], mine[:, Q_PT:Q_PLEN]).then_inc(params_in, 16)
                norm_squares()
                a.wait_ge(params_in, 32)
                norm_hT(0, 4, Q_GA)

                for n, (c0, w) in enumerate([(c0, w) for c0, w in ROW_BLOCKS for t in range(NT)]):
                    a.wait_ge(row_ps, n + 1)
                    a.activation(rows[:, n % NT, c0:c0 + w], bank(n % 4, 0, w), ACT.Copy).then_inc(row_ready, 1)
                a.drain()
                for t in range(NT):
                    ins = a.activation(cdup[:, t, :, :].rearrange("p s (e d) -> p s e d", e=2),
                                       rows[:, t, C_CK:C_CK + 4 * HD].rearrange("p (s d) -> p s d", d=HD).unsqueeze(2)
                                       .broadcast_to([P, 4, 2, HD]), ACT.Copy)
                ins.then_inc(cdup_ready, 1)
                a.activation(sg[:, :, :], rows[:, :, C_NG:C_NG + 24], ACT.Sigmoid).then_inc(sg_ready, 1)

                for n in range(8):
                    a.wait_ge(mg_ps, n + 1)
                    a.activation(gateT[:, 2 * n:2 * n + 2, :], bank(4 + n % 2).rearrange("p (m t) -> p m t", m=2),
                                 ACT.Sigmoid).then_inc(mg_ready, 1)

                a.wait_ge(cmp_ps, 2)
                a.activation(hidT[:, :, :], bank(2, 0, 64).rearrange("p (f c) -> p f c", f=2),
                             ACT.Gelu_apprx_tanh).then_inc(hid_ready, 1)
                a.wait_ge(cmp_ps, 3)
                for half in range(2):
                    ins = a.activation(hidv[:, half, :].rearrange("p (g r n) -> p g r n", g=2, r=4),
                                       bank(3, 32 * half, 32 * half + 32).rearrange("p (g n) -> p g n", g=2)
                                       .unsqueeze(2).broadcast_to([P, 2, 4, CP]), ACT.Gelu_apprx_tanh)
                ins.then_inc(hid_ready, 1)
                for n in range(9):
                    a.wait_ge(qk_ps, n + 1)
                    a.activation(qkT[:, 2 * n:2 * n + 2, :], bank(4 + n % 4).rearrange("p (s t) -> p s t", s=2),
                                 ACT.Copy).then_inc(qk_ready, 1)
                for t in range(NT):
                    keys = (t + 1) * P
                    a.wait_ge(idx_ps, t + 1)
                    if t:
                        a.wait_ge(relu_used, t)
                    per = 512 // keys
                    for j in range(HEADS // per):
                        ins = a.activation(relu[:, j * per:(j + 1) * per, 0:keys],
                                           bank(2 * t + j).rearrange("p (h s) -> p h s", h=per), ACT.Relu, scale=SCALE)
                    ins.then_inc(relu_ready, 1)
                for t in range(NT):
                    a.wait_ge(cs_sub, t + 1)
                    a.activation(pc[:, t, :], pc[:, t, :], ACT.Exp, scale=SCALE).then_inc(cs_exp, 1)
                a.wait_ge(pcT_ps, 1)
                a.activation(relu[:, 0:1, :], bank(6, 0, 256).rearrange("p (h s) -> p h s", h=1),
                             ACT.Copy).then_inc(pcT_ready, 1)
                def exps(i):
                    _, t, _ = ITEMS[i]
                    a.wait_ge(sm_ready, i + 1)
                    if i >= 2:
                        a.wait_ge(pT_ps, i - 1)
                    for h in range(4):
                        ins = a.activation(prob[:, i % 2, h, 0:(t + 1) * P], sm[:, i % 2, h, 0:(t + 1) * P], ACT.Exp,
                                           scale=SCALE, bias=nmax[:, i, h:h + 1], accum_out=sums[:, i, h:h + 1])
                    a.drain().then_inc(prob_ready, 1)

                def copies(i):
                    _, t, _ = ITEMS[i]
                    a.wait_ge(pT_ps, i + 1)
                    if i >= 2:
                        a.wait_ge(o_ps, i - 1)
                    for b in range(t + 1):
                        ins = a.activation(probT[:, i % 2, b, :], bank(4 + b), ACT.Copy)
                    ins.then_inc(pT_ready, 1)

                for i in range(len(ITEMS)):
                    exps(i)
                    if i:
                        copies(i - 1)
                copies(len(ITEMS) - 1)
                for n in range(4):
                    a.wait_ge(yT_ps, n + 1)
                    a.activation(yT[:, n // 2, 2 * (n % 2):2 * (n % 2) + 2, :],
                                 bank(n).rearrange("p (k t) -> p k t", k=2), ACT.Copy).then_inc(yT_ready, 1)

                a.wait_ge(xn_ready, 2)
                norm_squares()
                norm_hT(1, 4, Q_GF)
                a.drain()
                a.activation(hs[:, 0, :], hT[:, :, :].rearrange("p k t -> p (k t)"), ACT.Copy).then_inc(hs_ready, 1)
                for n in range(8):
                    a.wait_ge(q_ps, n + 1)
                    a.activation(qPT[:, 2 * n:2 * n + 2, :], bank(n % 2).rearrange("p (c t) -> p c t", c=2),
                                 ACT.Copy).then_inc(q_ready, 1)
                    if n % 2:
                        for t in range(NT):
                            a.wait_ge(ks_ps, (n // 2) * 2 + t + 1)
                            a.activation(keyscore[:, t, 2 * n - 2:2 * n + 2, :],
                                         bank(2 + t).rearrange("p (c n) -> p c n", c=4), ACT.Copy).then_inc(ks_ready, 1)
                a.wait_ge(gexp_in, 1)
                a.activation(expo[:, :, :, :], expo[:, :, :, :], ACT.Exp).then_inc(gexp_out, 1)
                a.wait_ge(pickT_ps, 1)
                a.activation(pickT[:, 0:2, :], bank(6).rearrange("p (v t) -> p v t", v=2), ACT.Copy).then_inc(pickT_ready, 1)
                a.activation(neg2[:, :], bank(6, SEQ, 2 * SEQ), ACT.Copy, scale=-1.0)
                a.activation(pickT[:, 2, :], bank(7, 0, SEQ), ACT.Copy).then_inc(pickT_ready, 1)
                a.drain()
                a.sem_inc(g_ready, 2)

                def hots(b, step, token):
                    a.wait_ge(g_ps, step + 1)
                    for j in range(4 - ACT_HOTS[b], 4):
                        a.activation(onehot2[:, b, j, :], iota[:, :], ACT.Abs, bias=neg2[:, token(j)])
                    a.drain()
                    for j in range(4 - ACT_HOTS[b], 4):
                        ins = a.activation(onehot2[:, b, j, :], onehot2[:, b, j, :], ACT.Relu, scale=-2.0,
                                           bias=pickT[:, 2, token(j)])
                    ins.then_inc(act_hot_ready, 1)

                def table(b, step, at):
                    a.wait_ge(g_ps, step + 3)
                    a.activation(big[:, at], bank(4 + b), ACT.Copy).then_inc(g_ready, 1)

                hots(0, 0, lambda j: slice(j, j + 1))
                with a.Fori(0, SEQ // 8 - 1) as i:
                    for b in range(2):
                        hots((b + 1) % 2, i * 2 + (b + 1), lambda j: bass.ds(i * 8 + (4 * b + 4 + j), 1))
                        table(b, i * 2 + b, bass.ds(i * (8 * P) + b * 4 * P, 4 * P))
                steps = SEQ // 4
                hots(1, steps - 1, lambda j: slice(SEQ - 4 + j, SEQ - 3 + j))
                for b in range(2):
                    at = (steps - 2 + b) * 4 * P
                    table(b, steps - 2 + b, slice(at, at + 4 * P))
                first_pair = B_EXP // 2
                turns = PAIRS // RING * 16

                def round_block(slot, blk):
                    a.activation(split[:, slot, blk, 0, :], ring[:, slot, blk, :], ACT.Copy).then_inc(hi_ready, 1)

                def gelu(j, acts, weights):
                    a.wait_ge(act_ps, acts)
                    a.wait_ge(wgt_ready, weights)
                    a.activation(act[:, j % 2, :], bank(4 + j % 2, 0, SEQ), ACT.Gelu_apprx_tanh).then_inc(act_ready, 1)

                a.wait_ge(pair_full[first_pair % RING], layer * turns + 16 * (first_pair // RING + 1))
                for c in range(2):
                    round_block(first_pair % RING, c)
                a.activation(small[:, 464:465], zero16[:, 0:1], ACT.Gelu_apprx_tanh)
                with a.Fori(0, NCHUNK // BODY - 1) as i:
                    for j in range(BODY):
                        slot, step = (first_pair + 1 + j) % RING, (first_pair + 1 + j) // RING
                        a.wait_ge(pair_full[slot], layer * turns + (i * 16 + 16 * (step + 1)))
                        a.wait_ge(wgt_used, i * BODY + (j + 2))
                        round_block(slot, 0)
                        gelu(j, i * BODY + (j + 1), i * BODY + (j + 1))
                        round_block(slot, 1)
                last_pair = first_pair + NCHUNK - 1
                a.wait_ge(pair_full[last_pair % RING], layer * turns + 16 * (last_pair // RING + 1))
                a.wait_ge(wgt_used, NCHUNK)
                for j in range(BODY):
                    round_block(last_pair % RING, j)
                    gelu(j, NCHUNK - 1 + j, NCHUNK - 1 + j)

                a.wait_ge(pw_ps, 1)
                a.dma_start(plen, mine[:, Q_PLEN:NPARAM]).then_inc(plen_in, 16)
                for n in range(4):
                    a.activation(pw[:, n // 2, (n % 2) * 512:(n % 2) * 512 + 512], bank(4 + n), ACT.Copy)
                a.drain()
                for t in range(NT):
                    a.activation(junk, pw[:, t, :], ACT.Square, accum_out=psq[:, t:t + 1])
                    a.drain()
                a.drain().then_inc(pw_ready, 1)
                a.wait_ge(xn_ready, 4)
                norm_squares()
                norm_hT(2, 0, None)
                a.wait_ge(pg_ps, 1)
                for n in range(4):
                    a.activation(gate[:, n // 2, (n % 2) * 512:(n % 2) * 512 + 512], bank(4 + n),
                                 ACT.Sigmoid).then_inc(pg_ready, 1)
                a.drain().then_inc(layer_done, 1)
                a.wait_ge(layer_go, layer + 1)

        @block.vector
        def _(v):
            v.memset(zero16[:, :], 0.0)
            v.memset(sin[:, :, :], 0.0)
            v.drain().then_inc(consts_dve, 1)
            v.wait_ge(in_dma, 3 * 16)
            v.tensor_copy(small[:, 16:19], small[:, 8:11].bitcast(I32))
            v.drain()
            ang = small[:, 32:56].rearrange("p (t f) -> p t f", f=ROT2)
            v.tensor_tensor(ang, small[:, 16:19].unsqueeze(2).broadcast_to([P, 3, ROT2]),
                            small[:, 0:8].unsqueeze(1).broadcast_to([P, 3, ROT2]), ALU.mult)
            v.drain()
            v.tensor_scalar(small[:, 64:88], small[:, 32:56], 0.15915494309189535, None, ALU.mult)
            v.drain()
            v.tensor_copy(small[:, 96:120].bitcast(I32), small[:, 64:88])
            v.drain()
            v.tensor_copy(small[:, 64:88], small[:, 96:120].bitcast(I32))
            v.drain()
            v.scalar_tensor_tensor(small[:, 128:152], small[:, 64:88], -6.28125, small[:, 32:56], ALU.mult, ALU.add)
            v.drain()
            v.scalar_tensor_tensor(small[:, 160:184], small[:, 64:88], -0.0019353071795864769, small[:, 128:152],
                                   ALU.mult, ALU.add)
            v.drain()
            v.tensor_scalar(sin[:, :, :], small[:, 160:184].rearrange("p (t f) -> p t f", f=ROT2),
                            3.141592, -3.141592, ALU.min, ALU.max)
            v.drain()
            v.scalar_tensor_tensor(cos[:, :, :], sin[:, :, :], -1.0, sin[:, :, :], ALU.mult, ALU.max)
            v.drain()
            v.tensor_scalar(cos[:, :, :], cos[:, :, :], -1.0, 1.5707963267948966, ALU.mult, ALU.add)
            v.drain().then_inc(angle_done, 1)
            v.wait_ge(consts_act, 1)
            v.wait_ge(consts_pool, 1)

            def rsqrt_mean(step, src, n):
                v.tensor_scalar(rms_steps[step], src, 1.0 / n, EPS, ALU.mult, ALU.add).then_inc(rms_in, 1)
                v.wait_ge(rms_out, step + 1)

            def norm_x(m):
                v.wait_ge(squares, m + 1)
                rsqrt_mean((0, 3, 5)[m], ss[:, :], D)
                for t in range(NT):
                    ins = v.tensor_scalar(xn[:, t, :], x[:, t, :], rstd[:, t:t + 1], None, ALU.mult)
                ins.then_inc(xn_ready, 1)

            def rope(lo, hi, c, s, shape):
                n = 1
                for d in shape[1:]:
                    n *= d
                np_ = shape[0]
                parts = []
                for j in range(4):
                    a = tmp[0:np_, j * n:(j + 1) * n]
                    if len(shape) == 4:
                        a = a.rearrange("p (t s f) -> p t s f", t=shape[1], s=shape[2])
                    parts.append(a)
                v.tensor_tensor(parts[0], lo, c, ALU.mult)
                v.tensor_tensor(parts[1], hi, s, ALU.mult)
                v.tensor_tensor(parts[2], hi, c, ALU.mult)
                v.tensor_tensor(parts[3], lo, s, ALU.mult)
                v.drain()
                v.tensor_tensor(lo, parts[0], parts[1], ALU.subtract)
                return v.tensor_tensor(hi, parts[2], parts[3], ALU.add)

            with v.Fori(0, DEPTH) as layer:
                norm_x(0)

                v.wait_ge(row_ready, 2 * len(ROW_BLOCKS))
                v.wait_ge(params_in, 32)
                nrows = rows[:, :, 0:NORM_SLOTS * HD]
                nslots = nrows.rearrange("p t (s d) -> p t s d", d=HD)
                tslots = tmp.rearrange("p (t s d) -> p t s d", t=NT, d=HD)
                v.tensor_tensor(tmp.rearrange("p (t c) -> p t c", t=NT), nrows, nrows, ALU.mult)
                v.drain()
                v.tensor_reduce(ms[:, :, :], tslots, AX.X, ALU.add)
                v.drain()
                rsqrt_mean(1, ms[:, :, :], HD)
                v.tensor_tensor(nslots, nslots, msr[:, :, :].unsqueeze(3).broadcast_to([P, NT, NORM_SLOTS, HD]), ALU.mult)
                v.drain()
                v.tensor_tensor(nrows, nrows, par[:, Q_GAIN:Q_GAIN + NORM_SLOTS * HD].unsqueeze(1)
                                .broadcast_to([P, NT, NORM_SLOTS * HD]), ALU.mult)
                v.drain()
                rslots = rows[:, :, 0:ROPE_SLOTS * HD].rearrange("p t (s d) -> p t s d", d=HD)
                shape = [P, NT, ROPE_SLOTS, ROT2]
                rope(rslots[:, :, :, 0:ROT2], rslots[:, :, :, ROT2:2 * ROT2],
                     cos[:, 0:NT, :].unsqueeze(2).broadcast_to(shape), sin[:, 0:NT, :].unsqueeze(2).broadcast_to(shape),
                     shape)
                v.drain()
                for t in range(NT):
                    v.tensor_copy(kdup[:, t, 0:4, :].rearrange("p s (e d) -> p s e d", e=2),
                                  rows[:, t, C_KS:C_KS + 4 * HD].rearrange("p (s d) -> p s d", d=HD).unsqueeze(2)
                                  .broadcast_to([P, 4, 2, HD]))
                    for s, col in ((4, C_KB), (5, C_IK)):
                        ins = v.tensor_copy(kdup[:, t, s, :].rearrange("p (e d) -> p e d", e=2),
                                            rows[:, t, col:col + HD].unsqueeze(1).broadcast_to([P, 2, HD]))
                ins.then_inc(rope_done, 1)
                v.tensor_scalar(iwb[:, :, :], rows[:, :, C_IW:C_IW + 8], HEADS ** -0.5, None, ALU.mult)
                v.memset(Z[:, :, :, :, :], 0.0)
                v.drain()

                v.wait_ge(cmp_ps, 1)
                for kv in range(2):
                    for gr in range(2):
                        for par_ in range(2):
                            lo = par_ * HD
                            src = ps[lo:lo + HD, kv, gr * SEQ:(gr + 1) * SEQ].rearrange(
                                "p (n j e) -> p e j n", j=8, e=2)[:, par_]
                            for half in range(2):
                                ins = v.tensor_tensor(
                                    Z[lo:lo + HD, kv, 8 * half:8 * half + 8, gr, 0:NCMP],
                                    src[:, :, half:half + NCMP],
                                    par[lo:lo + HD, Q_POS + 16 * kv + 8 * half:Q_POS + 16 * kv + 8 * half + 8]
                                    .unsqueeze(2).broadcast_to([HD, 8, NCMP]), ALU.add)
                v.drain().then_inc(z_ready, 1)
                v.wait_ge(cmp_ps, 4)
                kcp = ps[0:2 * CP, 3, 0:HD]
                kcs = kc[0:2 * CP, :]
                v.tensor_copy(kcs, kcp)
                v.drain()
                v.tensor_tensor(tmp[0:2 * CP, 0:HD], kcs, kcs, ALU.mult)
                v.drain()
                v.tensor_reduce(cms[0:2 * CP, 0:1], tmp[0:2 * CP, 0:HD], AX.X, ALU.add)
                v.drain()
                rsqrt_mean(2, cms[0:2 * CP, 0:1], HD)
                v.scalar_tensor_tensor(kcs, kcs, cms[0:2 * CP, 1:2], par[0:2 * CP, Q_CGAIN:Q_CGAIN + HD],
                                       ALU.mult, ALU.mult)
                v.drain()
                rope(kc[0:2 * CP, 0:ROT2], kc[0:2 * CP, ROT2:2 * ROT2], cos[0:2 * CP, NT, :], sin[0:2 * CP, NT, :],
                     [2 * CP, ROT2])
                v.drain()
                v.tensor_copy(kcdup[0:2 * CP, :].rearrange("p (e d) -> p e d", e=2),
                              kcs.unsqueeze(1).broadcast_to([2 * CP, 2, HD]))
                v.tensor_tensor(vcblk[:, :, :], bank(3, 64, 128).unsqueeze(1).broadcast_to([P, HEADS, HD]),
                                headmask[:, :].unsqueeze(2).broadcast_to([P, HEADS, HD]), ALU.mult)
                v.drain().then_inc(kc_ready, 1)
                v.wait_ge(cmp_ps, 5)
                v.tensor_copy(kcT, bank(3, 128, 128 + 2 * CP)).then_inc(kcT_ready, 1)

                for t in range(NT):
                    keys = (t + 1) * P
                    sc = score[:, t, 0:keys]
                    cm = causal[:, SEQ - keys:SEQ]
                    v.wait_ge(relu_ready, t + 1)
                    for h in range(HEADS):
                        v.scalar_tensor_tensor(sc, relu[:, h % 2 * 4 + h // 2, 0:keys], iwb[:, t, h:h + 1], cm if h == 0 else sc,
                                               ALU.mult, ALU.add)
                        v.drain()
                    v.drain().then_inc(relu_used, 1)
                for r in range(TOPK_ROUNDS):
                    for t in range(NT):
                        v.max(top8[:, t, :], score[:, t, 0:(t + 1) * P])
                    v.drain()
                    for t in range(NT):
                        v.match_replace(score[:, t, 0:(t + 1) * P], top8[:, t, :], score[:, t, 0:(t + 1) * P], GONE)
                    v.drain()
                for t in range(NT):
                    keys = (t + 1) * P
                    v.tensor_scalar(dmask[:, t, 0:keys], score[:, t, 0:keys], 0.5 * GONE, NEG, ALU.is_gt, ALU.mult)
                v.drain()
                for t in range(NT):
                    keys = (t + 1) * P
                    v.tensor_tensor(dmask[:, t, 0:keys], dmask[:, t, 0:keys], causal[:, SEQ - keys:SEQ], ALU.add)
                v.drain()

                v.wait_ge(cs_ps, 1)
                for t in range(NT):
                    pcv = pc[:, t, :].rearrange("p (h n) -> p h n", h=HEADS)
                    for e in range(2):
                        v.tensor_tensor(pcv.rearrange("p (h e) n -> p e h n", e=2)[:, e],
                                        bank(6 + e, t * HD, (t + 1) * HD).rearrange("p (h n) -> p h n", h=4),
                                        cneg[:, t, :].unsqueeze(1).broadcast_to([P, 4, CP]), ALU.add)
                    v.drain()
                    v.tensor_reduce(cmax[:, t, :], pcv, AX.X, ALU.max)
                    v.drain()
                    v.tensor_tensor(pcv, pcv, cmax[:, t, :].unsqueeze(2).broadcast_to([P, HEADS, CP]), ALU.subtract)
                    v.drain().then_inc(cs_sub, 1)
                for t in range(NT):
                    pcv = pc[:, t, :].rearrange("p (h n) -> p h n", h=HEADS)
                    v.wait_ge(cs_exp, t + 1)
                    v.tensor_reduce(csum[:, t, :], pcv, AX.X, ALU.add)
                    v.drain()
                    v.reciprocal(ccoef[:, t, :], csum[:, t, :])
                    v.tensor_tensor(pcv, pcv, cmask[:, t, :].unsqueeze(1).broadcast_to([P, HEADS, CP]), ALU.mult)
                    v.drain()
                v.wait_ge(sg_ready, 1)
                v.tensor_tensor(ccoef[:, :, :], ccoef[:, :, :], sg[:, :, 0:8], ALU.mult)
                v.drain().then_inc(pc_ready, 1)
                for t in range(NT):
                    v.wait_ge(oc_ps, t + 1)
                    v.tensor_tensor(y[:, 0, t, :].rearrange("p (h d) -> p h d", h=HEADS),
                                    bank(t).rearrange("p (h d) -> p h d", h=HEADS),
                                    ccoef[:, t, :].unsqueeze(2).broadcast_to([P, HEADS, HD]), ALU.mult)
                v.drain().then_inc(y_added, 1)

                def masked(i):
                    b, t, _ = ITEMS[i]
                    keys = (t + 1) * P
                    mk = dmask[:, t, 0:keys] if b == 2 else causal[:, SEQ - keys:SEQ]
                    v.wait_ge(s_ps, i + 1)
                    if i >= 2:
                        v.wait_ge(prob_ready, i - 1)
                    for h in range(4):
                        src = bank(2 * (i % 2) + h % 2, (h // 2) * keys, (h // 2 + 1) * keys)
                        v.tensor_tensor_reduce(out=sm[:, i % 2, h, 0:keys], in0=src, in1=mk, scale=1.0, scalar=GONE,
                                               op0=ALU.add, op1=ALU.max, accum_out=maxes[:, i, h:h + 1])
                    v.drain()
                    v.tensor_scalar(nmax[:, i, :], maxes[:, i, :], -SCALE, None, ALU.mult)
                    v.drain().then_inc(sm_ready, 1)

                def weighted(i):
                    b, t, hf = ITEMS[i]
                    v.wait_ge(prob_ready, i + 1)
                    v.reciprocal(coef[:, i, :], sums[:, i, :])
                    v.drain()
                    if b < 2:
                        v.tensor_tensor(coef[:, i, :], coef[:, i, :],
                                        sg[:, t, 8 * (b + 1) + 4 * hf:8 * (b + 1) + 4 * hf + 4], ALU.mult)
                        v.drain()
                    v.wait_ge(o_ps, i + 1)
                    cf = coef[:, i, :].unsqueeze(2).broadcast_to([P, 4, HD])
                    src = bank(6 + i % 2, 0, 256).rearrange("p (h d) -> p h d", h=4)
                    if b == 2:
                        v.tensor_tensor(y[:, 1, t, 256 * hf:256 * hf + 256].rearrange("p (h d) -> p h d", h=4),
                                        src, cf, ALU.mult)
                    else:
                        v.tensor_tensor(o_tmp[:, 0:256].rearrange("p (h d) -> p h d", h=4), src, cf, ALU.mult)
                        v.drain()
                        v.tensor_tensor(y[:, 0, t, 256 * hf:256 * hf + 256], y[:, 0, t, 256 * hf:256 * hf + 256],
                                        o_tmp[:, 0:256], ALU.add)
                    v.drain().then_inc(y_added, 1)

                for i in range(len(ITEMS)):
                    masked(i)
                    if i >= 2:
                        weighted(i - 2)
                weighted(len(ITEMS) - 2)
                weighted(len(ITEMS) - 1)

                v.wait_ge(mg_ready, 8)
                for m in range(NK):
                    v.wait_ge(br_ps, m + 1)
                    v.tensor_tensor(gate_prod[:, 0:SEQ], bank(4 + m % 4, 0, SEQ), gateT[:, m, :], ALU.mult)
                    v.tensor_tensor(gate_prod[:, SEQ:2 * SEQ], bank(4 + m % 4, SEQ, 2 * SEQ), gateT[:, NK + m, :], ALU.mult)
                    v.drain()
                    v.tensor_tensor(mergedT[:, m, :], gate_prod[:, 0:SEQ], gate_prod[:, SEQ:2 * SEQ],
                                    ALU.add)
                    v.drain().then_inc(br_ready, 1)
                v.wait_ge(wo_ps, 1)
                for n in range(4):
                    xs = x[:, n // 2, (n % 2) * 512:(n % 2) * 512 + 512]
                    v.tensor_tensor(xs, bank(n), xs, ALU.add)
                v.drain().then_inc(xn_ready, 1)

                norm_x(1)
                v.wait_ge(hs_ready, 1)
                v.tensor_tensor(hs[:, 1, :], hT[:, :, :].rearrange("p k t -> p (k t)"), hs[:, 0, :].bitcast(F32),
                                ALU.subtract).then_inc(hs_ready, 1)
                shape = [P, 2, PICKS, PICKS]
                for g in range(HEADS // 2):
                    v.wait_ge(ks_ready, NT * (g + 1))
                    both = [(t, c) for t in range(NT) for c in range(4 * g, 4 * g + 4)]
                    heads = [(t, h) for t in range(NT) for h in range(2 * g, 2 * g + 2)]
                    hs_ = slice(2 * g, 2 * g + 2)
                    cs_ = slice(4 * g, 4 * g + 4)
                    for t, c in both:
                        v.max(top1[:, t, c, 0:8], keyscore[:, t, c, :])
                    v.drain()
                    for t, c in both:
                        v.max_index(idx1u[:, t, c, 0:8], top1[:, t, c, 0:8], keyscore[:, t, c, :])
                        v.match_replace(keyrest[:, t, c, :], top1[:, t, c, 0:8], keyscore[:, t, c, :], GONE)
                    v.drain()
                    for t, c in both:
                        v.max(top1[:, t, c, 8:16], keyrest[:, t, c, :])
                    v.drain()
                    for t, c in both:
                        v.max_index(idx1u[:, t, c, 8:16], top1[:, t, c, 8:16], keyrest[:, t, c, :])
                    for t in range(NT):
                        tv = top1[:, t, cs_, :].rearrange("p (h s) k -> p h s k", s=2)
                        v.tensor_tensor(cand[:, t, hs_, :].rearrange("p h (a b) -> p h a b", a=PICKS),
                                        tv[:, :, 0, :].unsqueeze(3).broadcast_to(shape),
                                        tv[:, :, 1, :].unsqueeze(2).broadcast_to(shape), ALU.add)
                    v.drain()
                    for t, h in heads:
                        v.max(top2[:, t, h, 0:8], cand[:, t, h, :])
                    v.drain()
                    for t, h in heads:
                        v.max_index(pos2u[:, t, h, 0:8], top2[:, t, h, 0:8], cand[:, t, h, :])
                        v.match_replace(candrest[:, t, h, :], top2[:, t, h, 0:8], cand[:, t, h, :], GONE)
                    v.drain()
                    for t, h in heads:
                        v.max(top2[:, t, h, 8:16], candrest[:, t, h, :])
                    v.drain()
                    ins = v.tensor_tensor(expo[:, :, hs_, :], top2[:, :, hs_, :],
                                          top2[:, :, hs_, 0:1].broadcast_to([P, NT, 2, PICKS]), ALU.subtract)
                    if g == HEADS // 2 - 1:
                        ins.then_inc(gexp_in, 1)
                    for t, h in heads:
                        v.max_index(pos2u[:, t, h, 8:16], top2[:, t, h, 8:16], candrest[:, t, h, :])
                    v.drain()
                    v.tensor_scalar(whichu[:, 0, :, hs_, :], pos2u[:, :, hs_, :], 4, None, ALU.logical_shift_right)
                    v.tensor_scalar(whichu[:, 1, :, hs_, :], pos2u[:, :, hs_, :], PICKS - 1, None, ALU.bitwise_and)
                    v.tensor_copy(top1[:, :, cs_, :], idx1u[:, :, cs_, :])
                    v.drain()
                    for s in range(2):
                        v.tensor_copy(whichf[:, s, :, hs_, :], whichu[:, s, :, hs_, :])
                    v.drain()
                    for t in range(NT):
                        for s in range(2):
                            eq = (cand if s == 0 else candrest)[:, t, hs_, :].rearrange("p h (k j) -> p h k j", k=PICKS)
                            v.tensor_tensor(eq, iota[:, 0:PICKS].unsqueeze(1).unsqueeze(1).broadcast_to(shape),
                                            whichf[:, s, t, hs_, :].unsqueeze(3).broadcast_to(shape), ALU.is_equal)
                    v.drain()
                    for t in range(NT):
                        for s in range(2):
                            eq = (cand if s == 0 else candrest)[:, t, hs_, :].rearrange("p h (k j) -> p h k j", k=PICKS)
                            tv = top1[:, t, cs_, :].rearrange("p (h s) k -> p h s k", s=2)
                            v.tensor_tensor(eq, eq, tv[:, :, s, :].unsqueeze(2).broadcast_to(shape), ALU.mult)
                    v.drain()
                    for t in range(NT):
                        for s in range(2):
                            eq = (cand if s == 0 else candrest)[:, t, hs_, :].rearrange("p h (k j) -> p h k j", k=PICKS)
                            v.tensor_reduce(picks[:, s, t, hs_, :], eq, AX.X, ALU.add)
                v.wait_ge(gexp_out, 1)
                v.tensor_reduce(gsum[:, :, :], expo[:, :, :, :], AX.X, ALU.add)
                v.drain()
                v.reciprocal(grec[:, :, :], gsum[:, :, :])
                v.drain()
                v.tensor_tensor(picks[:, 2], expo[:, :, :, :],
                                grec[:, :, :].unsqueeze(3).broadcast_to([P, NT, HEADS, PICKS]), ALU.mult)
                v.drain().then_inc(picks_ready, 1)

                v.wait_ge(pickT_ready, 2)
                with v.Fori(0, SEQ // 8) as i:
                    for b in range(2):
                        v.wait_ge(g_ps, i * 2 + (b + 1))
                        four = pickT[:, 0, bass.ds(i * 8 + 4 * b, 4)]
                        v.tensor_tensor(onehot1[:, b, :, :], iota[:, :].unsqueeze(1).broadcast_to([P, 4, P]),
                                        four.unsqueeze(2).broadcast_to([P, 4, P]), ALU.is_equal)
                        for j in range(4 - ACT_HOTS[b]):
                            tok = bass.ds(i * 8 + (4 * b + j), 1)
                            ins = v.tensor_scalar(onehot2[:, b, j, :], iota[:, :], pickT[:, 1, tok], pickT[:, 2, tok],
                                                  ALU.is_equal, ALU.mult)
                        ins.then_inc(hot_ready, 1)
                v.wait_ge(g_ready, SEQ // 4 + 2)
                v.sem_inc(wgt_ready, 2)
                first_pair = B_EXP // 2

                def rest_of(slot, block):
                    return v.tensor_tensor(split[:, slot, block, 1, :], ring[:, slot, block, :],
                                           split[:, slot, block, 0, :].bitcast(F32), ALU.subtract)

                def weights(j, chunk, acts, used):
                    v.wait_ge(act_ready, acts)
                    v.tensor_tensor(act[:, j % 2, :], act[:, j % 2, :], G[:, :, chunk].squeeze(2), ALU.mult)
                    v.drain()
                    v.wait_ge(wgt_used, used)
                    v.tensor_copy(wgt[:, j % 2, 0, :], act[:, j % 2, :])
                    v.drain()
                    v.tensor_tensor(wgt[:, j % 2, 1, :], act[:, j % 2, :], wgt[:, j % 2, 0, :].bitcast(F32),
                                    ALU.subtract).then_inc(wgt_ready, 1)

                v.wait_ge(hi_ready, 2)
                rest_of(first_pair % RING, 0)
                rest_of(first_pair % RING, 1).then_inc(pair_free, 1)
                with v.Fori(0, NCHUNK // BODY - 1) as i:
                    for j in range(BODY):
                        slot = (first_pair + 1 + j) % RING
                        v.wait_ge(hi_ready, i * (2 * BODY) + (2 * j + 3))
                        rest_of(slot, 0).then_inc(lo_ready, 1)
                        weights(j, bass.ds(i * BODY + j, 1), i * BODY + (j + 1), i * BODY + (j + 2))
                        v.wait_ge(hi_ready, i * (2 * BODY) + (2 * j + 4))
                        rest_of(slot, 1).then_inc(pair_free, 1)
                for j in range(BODY):
                    c = NCHUNK - BODY + j
                    v.wait_ge(hi_ready, NCHUNK * 2 - 1 + j)
                    rest_of((first_pair + NCHUNK - 1) % RING, j).then_inc((lo_ready, pair_free)[j], 1)
                    weights(j, bass.ds(c, 1), c + 1, c + 2)
                v.wait_ge(wgt_used, NCHUNK + 3)
                for n in range(4):
                    xs = x[:, n // 2, (n % 2) * 512:(n % 2) * 512 + 512]
                    v.tensor_tensor(xs, bank(n), xs, ALU.add)
                v.drain().then_inc(xn_ready, 1)

                v.wait_ge(pw_ready, 1)
                rsqrt_mean(4, psq[:, :], D)
                norm_x(2)
                v.wait_ge(plen_in, 16)
                for t in range(NT):
                    v.scalar_tensor_tensor(pw[:, t, :], pw[:, t, :], prstd[:, t:t + 1], plen,
                                           ALU.mult, ALU.mult)
                v.drain()
                v.wait_ge(pg_ready, 4)
                for t in range(NT):
                    v.tensor_tensor(pw[:, t, :], pw[:, t, :], gate[:, t, :], ALU.mult)
                v.drain()
                for t in range(NT):
                    v.tensor_tensor(x[:, t, :], x[:, t, :], pw[:, t, :], ALU.add)
                v.drain().then_inc(layer_done, 1)
                v.wait_ge(layer_go, layer + 1)

        @block.tensor
        def _(pe):
            pe.wait_ge(consts_pool, 1)
            pe.wait_ge(consts_dve, 1)
            with pe.Fori(0, DEPTH) as layer:
                turns = PAIRS // RING * 16

                def block_of(n):
                    return ring[:, (n // 2) % RING, n % 2, :]

                def arrive(n):
                    if n % 2 == 0:
                        p = n // 2
                        pe.wait_ge(pair_full[p % RING], layer * turns + 16 * (p // RING + 1))

                owed = [0]

                def settle(ins):
                    if owed[0]:
                        ins.then_inc(pair_free, owed[0])
                        owed[0] = 0

                def norm_T(m, b0):
                    pe.wait_ge(xn_ready, [1, 3, 5][m])
                    for j in range(4):
                        for k in (2 * j, 2 * j + 1):
                            for t in range(NT):
                                ins = pe.transpose(bank(b0 + j, (k % 2) * SEQ + t * P, (k % 2) * SEQ + t * P + P),
                                                   xn[:, t, k * P:(k + 1) * P], ident[:, :])
                                settle(ins)
                        ins.then_inc(xT_ps, 1)
                    pe.wait_ge(hT_ready, 4 * (m + 1))

                norm_T(0, 4)
                for cb, (c0, w) in enumerate(ROW_BLOCKS):
                    for t in range(NT):
                        n = cb * NT + t
                        if n >= 4:
                            pe.wait_ge(row_ready, n - 3)
                        for k in range(NK):
                            blk = B_ROW + 4 * cb + k // 2
                            if t == 0 and k % 2 == 0:
                                arrive(blk)
                            wv = block_of(blk).rearrange("p (k c) -> p k c", k=2)
                            ins = pe.matmul(bank(n % 4, 0, w), hT[:, k, t * P:(t + 1) * P], wv[:, k % 2, 0:w],
                                            start=(k == 0), stop=(k == NK - 1))
                            settle(ins)
                            if t == NT - 1 and k == 3:
                                ins.then_inc(pair_free, 1)
                        owed[0] += t == NT - 1
                        ins.then_inc(row_ps, 1)
                for c in range(16):
                    blk = B_GATE + c
                    arrive(blk)
                    if c % 2 == 0 and c >= 4:
                        pe.wait_ge(mg_ready, c // 2 - 1)
                    wv = block_of(blk).rearrange("p (k c) -> p k c", k=NK)
                    for k in range(NK):
                        ins = pe.matmul(bank(4 + (c // 2) % 2, (c % 2) * SEQ, (c % 2 + 1) * SEQ), wv[:, k, :],
                                        hT[:, k, :], start=(k == 0), stop=(k == NK - 1))
                        settle(ins)
                    if c % 2:
                        ins.then_inc(mg_ps, 1)
                        owed[0] += 1

                pe.wait_ge(cdup_ready, 1)
                for kv in range(2):
                    for gr in range(2):
                        for t in range(NT):
                            ins = pe.transpose(bank(kv, gr * SEQ + t * P, gr * SEQ + t * P + P),
                                               cdup[:, t, 2 * kv + gr, :], ident[:, :])
                            settle(ins)
                ins.then_inc(cmp_ps, 1)
                pe.wait_ge(rope_done, 1)

                def transposes(n):
                    if n >= 4:
                        pe.wait_ge(qk_ready, n - 3)
                    for s in (2 * n, 2 * n + 1):
                        for t in range(NT):
                            src = rows[:, t, T_SRC[s]:T_SRC[s] + P] if s < T_KS else kdup[:, t, s - T_KS, :]
                            ins = pe.transpose(bank(4 + n % 4, (s % 2) * SEQ + t * P, (s % 2) * SEQ + t * P + P),
                                               src, ident[:, :])
                            settle(ins)
                    ins.then_inc(qk_ps, 1)

                pe.wait_ge(mg_ready, 8)
                pe.wait_ge(z_ready, 1)
                for kv in range(2):
                    for half in range(2):
                        for j in range(16):
                            if half == 0 and j % 4 == 0:
                                arrive(B_W1 + 4 * kv + j // 4)
                            wv = block_of(B_W1 + 4 * kv + j // 4).rearrange("p (j c) -> p j c", j=4)
                            ins = pe.matmul(bank(2 + kv, half * 32, half * 32 + 32),
                                            wv[:, j % 4, half * P:(half + 1) * P],
                                            Z[:, kv, j, :, :].rearrange("p g n -> p (g n)"),
                                            start=(j == 0), stop=(j == 15))
                            settle(ins)
                            if half == 1 and j == 7:
                                ins.then_inc(pair_free, 1)
                    owed[0] += 1
                    ins.then_inc(cmp_ps, 1)
                for n in range(9):
                    transposes(n)
                pe.wait_ge(hid_ready, 2)
                w2 = par[:, Q_W2:Q_W2 + 4 * HD].rearrange("p (v f d) -> p v f d", v=2, f=2)
                for half in range(2):
                    pe.matmul(ps[0:2 * CP, 3, 0:HD], hidT[:, half, :], w2[:, 0, half, :],
                              start=(half == 0), stop=(half == 1))
                for half in range(2):
                    ins = pe.matmul(bank(3, 64, 128), hidv[:, half, :], w2[:, 1, half, :], start=(half == 0), stop=(half == 1))
                ins.then_inc(cmp_ps, 1)
                pe.wait_ge(kc_ready, 1)
                pe.transpose(bank(3, 128, 128 + 2 * CP), kcdup[0:2 * CP, :],
                             ident[0:2 * CP, 0:2 * CP]).then_inc(cmp_ps, 1)

                def side(h):
                    return (h % 2) * HD

                pe.wait_ge(qk_ready, 9)
                pe.wait_ge(kcT_ready, 1)
                for t in range(NT):
                    keys = (t + 1) * P
                    per = 512 // keys
                    for h in range(HEADS):
                        lo = side(h)
                        at = h % 2 * 4 + h // 2
                        ins = pe.matmul(bank(2 * t + at // per, (at % per) * keys, (at % per + 1) * keys),
                                        qkT[lo:lo + HD, T_IQ + h // 2, t * P:(t + 1) * P],
                                        qkT[lo:lo + HD, T_IK, 0:keys], start=True, stop=True)
                    ins.then_inc(idx_ps, 1)
                for t in range(NT):
                    for h in range(HEADS):
                        lo = side(h)
                        gr = h // 4
                        ins = pe.matmul(bank(6 + h % 2, t * HD + h // 2 * CP, t * HD + (h // 2 + 1) * CP),
                                        qkT[lo:lo + HD, T_NQ + h // 2, t * P:(t + 1) * P],
                                        kcT[lo:lo + HD, gr * CP:(gr + 1) * CP], start=True, stop=True)
                ins.then_inc(cs_ps, 1)
                pe.wait_ge(pc_ready, 1)
                for t in range(NT):
                    ins = pe.transpose(bank(6, t * P, t * P + P), pc[:, t, :], ident[:, :])
                ins.then_inc(pcT_ps, 1)
                pe.wait_ge(pcT_ready, 1)
                pe.wait_ge(relu_ready, 2)
                for t in range(NT):
                    pe.matmul(bank(t), relu[:, 0, t * P:(t + 1) * P], vcblk[:, :, :].rearrange("p h d -> p (h d)"),
                              start=True, stop=True).then_inc(oc_ps, 1)
                pe.wait_ge(y_added, 1)

                def scores(i):
                    b, t, hf = ITEMS[i]
                    keys = (t + 1) * P
                    if i >= 2:
                        pe.wait_ge(sm_ready, i - 1)
                    for j in range(4):
                        h = 4 * hf + j
                        lo = side(h)
                        q = (T_DQ if b == 2 else T_NQ) + h // 2
                        k = (T_KS + h // 4, T_KW + h // 4, T_KB)[b]
                        ins = pe.matmul(bank(2 * (i % 2) + j % 2, (j // 2) * keys, (j // 2 + 1) * keys),
                                        qkT[lo:lo + HD, q, t * P:(t + 1) * P], qkT[lo:lo + HD, k, 0:keys],
                                        start=True, stop=True)
                    ins.then_inc(s_ps, 1)

                def prob_T(i):
                    _, t, _ = ITEMS[i]
                    pe.wait_ge(prob_ready, i + 1)
                    if i >= 1:
                        pe.wait_ge(pT_ready, i)
                    for b in range(t + 1):
                        for j in range(4):
                            ins = pe.transpose(bank(4 + b, j * P, (j + 1) * P), prob[:, i % 2, j, b * P:(b + 1) * P],
                                               ident[:, :])
                    ins.then_inc(pT_ps, 1)

                def outputs(i):
                    b, t, hf = ITEMS[i]
                    pe.wait_ge(pT_ready, i + 1)
                    if i >= 2:
                        pe.wait_ge(y_added, i)
                    for j in range(4):
                        col = (C_VS + (4 * hf + j) // 4 * HD, C_VW + (4 * hf + j) // 4 * HD, C_VB)[b]
                        for kb in range(t + 1):
                            ins = pe.matmul(bank(6 + i % 2, j * HD, (j + 1) * HD),
                                            probT[:, i % 2, kb, j * P:(j + 1) * P], rows[:, kb, col:col + HD],
                                            start=(kb == 0), stop=(kb == t))
                    ins.then_inc(o_ps, 1)

                n_items = len(ITEMS)
                scores(0)
                for i in range(n_items):
                    if i + 1 < n_items:
                        scores(i + 1)
                    prob_T(i)
                    if i:
                        outputs(i - 1)
                outputs(n_items - 1)
                pe.wait_ge(y_added, n_items + 1)
                for n in range(4):
                    m = n // 2
                    for k in (2 * (n % 2), 2 * (n % 2) + 1):
                        for t in range(NT):
                            ins = pe.transpose(bank(n, (k % 2) * SEQ + t * P, (k % 2) * SEQ + t * P + P),
                                               y[:, m, t, k * P:(k + 1) * P], ident[:, :])
                    ins.then_inc(yT_ps, 1)
                pe.wait_ge(yT_ready, 4)
                for m in range(NK):
                    if m >= 4:
                        pe.wait_ge(br_ready, m - 3)
                    for br in range(2):
                        blk = B_BR + 2 * (m // 2) + br
                        if m % 2 == 0:
                            arrive(blk)
                        wv = block_of(blk).rearrange("p (k c) -> p k c", k=4)
                        for k in range(4):
                            ins = pe.matmul(bank(4 + m % 4, br * SEQ, (br + 1) * SEQ),
                                            wv[:, k, (m % 2) * P:(m % 2 + 1) * P], yT[:, br, k, :],
                                            start=(k == 0), stop=(k == 3))
                            settle(ins)
                    ins.then_inc(br_ps, 1)
                    owed[0] += m % 2

                def streamed(blk, b0, left, nk):
                    for k in range(nk):
                        arrive(blk + k)
                        for n in range(4):
                            t = n // 2
                            ins = pe.matmul(bank(b0 + n), left[:, k, t * P:(t + 1) * P],
                                            block_of(blk + k)[:, (n % 2) * 512:(n % 2) * 512 + 512],
                                            start=(k == 0), stop=(k == nk - 1))
                            settle(ins)
                        if k % 2 and k < nk - 1:
                            ins.then_inc(pair_free, 1)
                    owed[0] += 1
                    return ins

                pe.wait_ge(br_ready, NK)
                streamed(B_OUT, 0, mergedT, NK).then_inc(wo_ps, 1)

                norm_T(1, 4)
                sub = par[:, Q_SUB:Q_SUB + 2 * NKEYS].rearrange("p (s n) -> p s n", s=2)
                for c in range(16):
                    blk = B_WQ + c
                    arrive(blk)
                    if c % 2 == 0 and c >= 4:
                        pe.wait_ge(q_ready, c // 2 - 1)
                    wv = block_of(blk).rearrange("p (k c) -> p k c", k=NK)
                    for k in range(NK):
                        ins = pe.matmul(bank((c // 2) % 2, (c % 2) * SEQ, (c % 2 + 1) * SEQ), wv[:, k, :],
                                        hT[:, k, :], start=(k == 0), stop=(k == NK - 1))
                        settle(ins)
                    if c % 2:
                        ins.then_inc(q_ps, 1)
                        owed[0] += 1
                    if c % 4 == 3:
                        pe.wait_ge(q_ready, (c + 1) // 2)
                        for t in range(NT):
                            if c >= 7:
                                pe.wait_ge(ks_ready, (c // 4 - 1) * 2 + t + 1)
                            for j in range(4):
                                cc = c - 3 + j
                                ins = pe.matmul(bank(2 + t, j * P, (j + 1) * P), qPT[:, cc, t * P:(t + 1) * P],
                                                sub[:, cc % 2, :], start=True, stop=True)
                                settle(ins)
                            ins.then_inc(ks_ps, 1)
                pe.wait_ge(picks_ready, 1)
                for w in range(3):
                    for t in range(NT):
                        ins = pe.transpose(bank(6 + w // 2, (w % 2) * SEQ + t * P, (w % 2) * SEQ + t * P + P),
                                           picks[:, w, t, :, :].rearrange("p h k -> p (h k)"), ident[:, :])
                ins.then_inc(pickT_ps, 1)
                pe.wait_ge(pickT_ready, 2)
                pe.sem_inc(g_ps, 2)
                with pe.Fori(0, SEQ // 8) as i:
                    for b in range(2):
                        pe.wait_ge(hot_ready, i * 2 + (b + 1))
                        pe.wait_ge(act_hot_ready, i * 2 + (b + 1))
                        pe.wait_ge(g_ready, i * 2 + (b + 1))
                        for j in range(4):
                            ins = pe.matmul(bank(4 + b, j * P, (j + 1) * P), onehot2[:, b, j, :], onehot1[:, b, j, :],
                                            start=True, stop=True)
                        ins.then_inc(g_ps, 1)

                for n in range(4):
                    pe.matmul(bank(n), zero16[:, 0:P], zero16[:, :], start=True, stop=False, skip_group_check=True)
                pe.wait_ge(g_ready, SEQ // 4 + 2)
                pe.sem_inc(wgt_used, 3)

                first_pair = B_EXP // 2
                pe.wait_ge(hs_ready, 2)
                PASSES = ((0, 0), (0, 1), (1, 0))

                def pre_act(b, slot, block):
                    for k in range(NK):
                        for n, (s_, m) in enumerate(PASSES):
                            ins = pe.matmul(bank(4 + b, 0, SEQ), split[:, slot, block, s_, k * P:(k + 1) * P],
                                            hs[:, m, k * SEQ:(k + 1) * SEQ], start=(k == 0 and n == 0),
                                            stop=(k == NK - 1 and n == 2))
                    return ins

                def product(b, slot, block, last=False):
                    for n in range(4):
                        t = n // 2
                        for s_, m in PASSES:
                            ins = pe.matmul(bank(n), wgt[:, b, s_, t * P:(t + 1) * P],
                                            split[:, slot, block, m, (n % 2) * 512:(n % 2) * 512 + 512],
                                            start=False, stop=last and s_ == 1, skip_group_check=True)
                    return ins

                pe.wait_ge(pair_free, layer * PAIRS + (first_pair + 1))
                for c in range(2):
                    pre_act(c, first_pair % RING, c).then_inc(act_ps, 1)

                def chunk(i, j):
                    slot = (first_pair + 1 + j) % RING
                    pe.wait_ge(lo_ready, i * BODY + (j + 1))
                    pe.wait_ge(wgt_ready, i * BODY + (j + 3))
                    product(j % 2, slot, 0).then_inc(wgt_used, 1)
                    pe.wait_ge(pair_free, layer * PAIRS + (i * BODY + (first_pair + j + 2)))
                    return slot

                with pe.Fori(0, NCHUNK // BODY - 1) as i:
                    for j in range(BODY):
                        pre_act(j % 2, chunk(i, j), 1).then_inc(act_ps, 1)
                pe.wait_ge(lo_ready, NCHUNK - 1)
                pe.wait_ge(wgt_ready, NCHUNK + 1)
                product(0, (first_pair + NCHUNK - 1) % RING, 0).then_inc(wgt_used, 1)
                pe.wait_ge(pair_free, layer * PAIRS + (first_pair + NCHUNK))
                pe.wait_ge(wgt_ready, NCHUNK + 2)
                product(1, (first_pair + NCHUNK - 1) % RING, 1, True).then_inc(wgt_used, 1)
                streamed(B_PLEW, 4, pT[:, :].rearrange("p (k t) -> p k t", k=2), 2).then_inc(pw_ps, 1)
                norm_T(2, 0)
                pe.wait_ge(pw_ready, 1)
                streamed(B_PLEG, 4, hT, NK).then_inc(pg_ps, 1)
                for p in range((B_PLEG + 8) // 2, PAIRS):
                    pe.wait_ge(pair_full[p % RING], layer * turns + 16 * (p // RING + 1))
                    owed[0] += 1
                pe.drain().then_inc(pair_free, owed[0])
                pe.drain().then_inc(layer_done, 1)
                pe.wait_ge(layer_go, layer + 1)


def _stream(i):
    import numpy as np

    blocks = np.zeros((DEPTH, PAIRS * 2, P, BLK), np.float32)
    w_in = i["w_in"]
    cuts = [(0, 512), (512 + 256, 512 + 384), (512 + 512, 512 + 640), (1304, 1816), (1816, 1880), (1944, 2456),
            (2456, 2520), (512 + 384, 512 + 512), (512 + 640, 512 + 768), (512, 640), (640, 768), (1880, 1944),
            (1280, 1304), (2520, 2528)]
    for l in range(DEPTH):
        b = blocks[l]
        rows = np.concatenate([w_in[l][:, lo:hi] for lo, hi in cuts], axis=1).reshape(4, 2, P, ROW)
        for cb, (c0, w) in enumerate(ROW_BLOCKS):
            v = b[B_ROW + 4 * cb:B_ROW + 4 * cb + 4].reshape(4, P, 2, 512)
            v[:, :, :, :w] = rows[:, :, :, c0:c0 + w].transpose(0, 2, 1, 3)

        def columns(w):
            return w.reshape(NK, P, -1, P).transpose(2, 1, 0, 3).reshape(-1, P, BLK)

        b[B_GATE:B_GATE + 16] = columns(w_in[l][:, 2528:])
        for v in range(2):
            b[B_W1 + 4 * v:B_W1 + 4 * v + 4] = i["cmp_w1"][l][v].reshape(4, 4, P, 256).transpose(0, 2, 1, 3).reshape(4, P, BLK)
        for m, name in enumerate(("w_branch_a", "w_branch_b")):
            b[B_BR + m:B_BR + 8:2] = i[name][l].reshape(4, P, 4, 256).transpose(2, 1, 0, 3).reshape(4, P, BLK)
        b[B_OUT:B_OUT + 8] = i["w_out"][l].reshape(8, P, D)
        b[B_WQ:B_WQ + 16] = columns(i["peer_wq"][l])
        u = i["peer_u"][l].reshape(NCHUNK, P, NK, P).transpose(0, 3, 2, 1).reshape(NCHUNK, P, BLK)
        v = i["peer_v"][l].reshape(NCHUNK, P, D)
        e = b[B_EXP:B_EXP + 2 * NCHUNK]
        e[0:2] = u[0:2]
        e[2:254:2], e[3:254:2] = v[0:126], u[2:128]
        e[254:256] = v[126:128]
        b[B_PLEW:B_PLEW + 2] = i["ple_w"][l].reshape(2, P, D)
        b[B_PLEG:B_PLEG + 8] = i["ple_gate_w"][l].reshape(8, P, D)
    return np.ascontiguousarray(blocks.reshape(DEPTH * PAIRS, 2, P, BLK).transpose(0, 2, 1, 3))


def _params(i):
    import numpy as np

    par = np.zeros((DEPTH, P, NPARAM), np.float32)
    for l in range(DEPTH):
        q = par[l]
        q[:, Q_GA:Q_GA + NK] = i["attn_norm"][l].reshape(NK, P).T
        q[:, Q_GF:Q_GF + NK] = i["ffn_norm"][l].reshape(NK, P).T
        ga, gd = i["nsa_qk_gain"][l], i["dsa_qk_gain"][l]
        gains = [ga[0]] * 8 + [ga[2]] * 2 + [ga[3]] * 2 + [gd[0]] * 8 + [gd[1]]
        q[:, Q_GAIN:Q_GAIN + NORM_SLOTS * HD] = np.concatenate(gains)[None]
        q[:, Q_CGAIN:Q_CGAIN + HD] = ga[1][None]
        q[:, Q_POS:Q_POS + 32] = i["cmp_pos"][l].reshape(2, 16, 2, HD).transpose(2, 3, 0, 1).reshape(P, 32)
        q[:, Q_W2:Q_W2 + 4 * HD] = i["cmp_w2"][l].reshape(2, 2, P, HD).transpose(2, 0, 1, 3).reshape(P, 4 * HD)
        q[:, Q_SUB:Q_SUB + 2 * NKEYS] = i["peer_sub_keys"][l].transpose(2, 0, 1).reshape(P, 2 * NKEYS)
        q[:, Q_PT:Q_PT + 2 * SEQ] = i["p"][l, 0].T.reshape(2, P, SEQ).transpose(1, 0, 2).reshape(P, 2 * SEQ)
        q[:, Q_PLEN:Q_PLEN + D] = i["ple_norm"][l][None]
    return par


def kernel(**inputs):
    import numpy as np
    import concourse.bacc as bacc
    from concourse.bass_utils import run_bass_kernel_spmd as run

    i = {k: np.asarray(v) for k, v in inputs.items()}
    pos = np.ascontiguousarray(i["positions"])
    posl = np.zeros((P, 3), pos.dtype)
    posl[:, 0:2] = pos[0].reshape(2, P).T
    for gr in range(2):
        posl[gr * CP:gr * CP + NCMP, 2] = pos[0, CMP_LEN - 1::CMP_STRIDE][:NCMP]
    inv = (np.float32(500000.0) ** (-np.arange(ROT2, dtype=np.float32) / ROT2)).astype(np.float32)
    arrays = {
        "in_x": np.ascontiguousarray(i["x"]),
        "in_stream": _stream(i),
        "in_params": _params(i),
        "in_positions": posl,
        "in_inv_freq": np.ascontiguousarray(np.broadcast_to(inv, (P, ROT2))),
    }
    nc = bacc.Bacc("TRN2", target_bir_lowering=False, num_devices=1, dynamic_dma_scratch_size=256)
    args = [nc.dram_tensor(n, a.shape, mybir.dt.from_np(a.dtype), kind="ExternalInput").ap() for n, a in arrays.items()]
    o = nc.dram_tensor("out_0", (1, SEQ, D), F32, kind="ExternalOutput").ap()
    build(nc, *args, o)
    r = run(nc, [arrays], core_ids=[0])
    return r.results[0]["out_0"]
```

```python
from contextlib import ExitStack

import concourse.bass as bass
from concourse import mybir

F32 = mybir.dt.float32
F32R = mybir.dt.float32r
BF16 = mybir.dt.bfloat16
I32 = mybir.dt.int32
U32 = mybir.dt.uint32
ALU = mybir.AluOpType
ACT = mybir.ActivationFunctionType
AX = mybir.AxisListType

P = 128
DEPTH, SEQ, D = 2, 256, 1024
NT = SEQ // P
NK = D // P
HD = 64
HEADS = 8
ROT2 = HD // 8
EPS = 1e-6
NEG = -1e30
GONE = -3e38
SCALE = HD ** -0.5
CMP_STRIDE, CMP_LEN, NCMP = 16, 32, 15
CP = 16
TOPK_ROUNDS = 64 // 8
PICKS = 16
NKEYS = 128
PLE = 256

C_NQ, C_KS, C_KW, C_DQ, C_KB, C_IQ, C_IK = 0, 512, 640, 768, 1280, 1344, 1856
C_VS, C_VW, C_CK, C_CV, C_VB, C_NG, C_IW = 1920, 2048, 2176, 2304, 2432, 2496, 2520
ROW = 2528
ROPE_SLOTS, NORM_SLOTS = 30, 21
ROW_BLOCKS = [(b * 512, min(512, ROW - b * 512)) for b in range((ROW + 511) // 512)]

BLK = 1024
B_ROW = 0
B_GATE = B_ROW + 4 * len(ROW_BLOCKS)
B_W1 = B_GATE + 16
B_BR = B_W1 + 8
B_OUT = B_BR + 8
B_WQ = B_OUT + 8
B_EXP = B_WQ + 16
NCHUNK = 128
B_PLEW = B_EXP + 2 * NCHUNK
B_PLEG = B_PLEW + 2
RING = 2
PAIRS = -(-(B_PLEG + 8) // 2)
PAIRS += -PAIRS % RING
ACT_HOTS = (1, 1)
BODY = 2

Q_GA, Q_GF, Q_GAIN, Q_CGAIN = 0, 8, 16, 16 + NORM_SLOTS * HD
Q_POS = Q_CGAIN + HD
Q_W2 = Q_POS + 32
Q_SUB = Q_W2 + 4 * HD
Q_END = Q_SUB + 2 * NKEYS
Q_PT = Q_END
Q_PLEN = Q_PT + 2 * SEQ
NPARAM = Q_PLEN + D

T_NQ, T_DQ, T_IQ, T_KS, T_KW, T_KB, T_IK = 0, 4, 8, 12, 14, 16, 17
T_SRC = [c + 128 * j for c in (C_NQ, C_DQ, C_IQ) for j in range(4)]

ITEMS = [(b, t, hf) for b in range(3) for t in range(NT) for hf in range(2)]


def build(nc, x_in, stream, params, positions, inv_freq, out):
    ctx = ExitStack()
    with ctx:
        def sb(name, shape, dt=F32):
            return ctx.enter_context(nc.sbuf_tensor(name, shape, dt))

        layer_sems = []

        def sem(name, cleared=True):
            s = ctx.enter_context(nc.semaphore(name))
            if cleared:
                layer_sems.append(s)
            return s

        ps = ctx.enter_context(nc.psum_tensor("ps", [P, 8, 512], F32))

        x = sb("x", [P, NT, D])
        hT = sb("hT", [P, NK, SEQ])
        hs = sb("hs", [P, 2, NK * SEQ], F32R)
        split = sb("split", [P, 2, 2, 2, BLK], F32R)
        wgt = sb("wgt", [P, 2, 2, SEQ], F32R)
        ring = sb("ring", [P, RING, 2, BLK])
        pT = sb("pT", [P, 2 * SEQ])
        ident = sb("ident", [P, P])
        iota = sb("iota", [P, P])
        causal = sb("causal", [P, SEQ])
        cmask = sb("cmask", [P, NT, CP])
        cneg = sb("cneg", [P, NT, CP])
        headmask = sb("headmask", [P, HEADS])
        minus_half = sb("minus_half", [P, NT * NORM_SLOTS])
        zero16 = sb("zero16", [P, 512], BF16)
        cos = sb("cos", [P, NT + 1, ROT2])
        sin = sb("sin", [P, NT + 1, ROT2])
        small = sb("small", [P, 480])
        pickT = sb("pickT", [P, 3, SEQ])
        neg2 = sb("neg2", [P, SEQ])
        rest = hT[:, :, :].rearrange("p k t -> p (k t)")
        onehot1 = rest[:, 0:1024].rearrange("p (b j i) -> p b j i", b=2, j=4)
        onehot2 = rest[:, 1024:2048].rearrange("p (b j i) -> p b j i", b=2, j=4)
        act = rest[:, 0:2 * SEQ].rearrange("p (b t) -> p b t", b=2)

        big = sb("big", [P, SEQ * NKEYS])
        G = big[:, :].rearrange("p (t i) -> p t i", t=SEQ)
        used = [0]

        def carve(n, *dims, **kw):
            a = big[:, used[0]:used[0] + n]
            used[0] += n
            assert used[0] <= SEQ * NKEYS
            return a.rearrange(*dims, **kw) if dims else a

        xn = carve(NT * D, "p (t d) -> p t d", t=NT)
        par = carve(Q_END)
        rows = carve(NT * ROW, "p (t c) -> p t c", t=NT)
        tmp = carve(NT * NORM_SLOTS * HD)
        qkT = carve(18 * SEQ, "p (s t) -> p s t", s=18)
        gateT = carve(16 * SEQ, "p (m t) -> p m t", m=16)
        Z = carve(2 * 16 * 2 * CP, "p (v j g n) -> p v j g n", v=2, j=16, g=2)
        hidT = carve(2 * 2 * CP, "p (f c) -> p f c", f=2)
        hidv = carve(2 * P, "p (f c) -> p f c", f=2)
        kcdup = carve(P)
        vcblk = carve(HEADS * HD, "p (h d) -> p h d", h=HEADS)
        kc = carve(HD)
        kcT = carve(4 * CP)
        hrow = big[:, NT * D - 512:NT * D].rearrange("p (v f) -> p v f", v=2)
        relu = carve(HEADS * SEQ, "p (h s) -> p h s", h=HEADS)
        score = carve(NT * SEQ, "p (t s) -> p t s", t=NT)
        dmask = carve(NT * SEQ, "p (t s) -> p t s", t=NT)
        over = used[0]
        cdup = carve(NT * 4 * P, "p (t s c) -> p t s c", t=NT, s=4)
        kdup = carve(NT * 6 * P, "p (t s c) -> p t s c", t=NT, s=6)
        used[0] = over
        sm = carve(2 * 4 * SEQ, "p (i h s) -> p i h s", i=2, h=4)
        prob = carve(2 * 4 * SEQ, "p (i h s) -> p i h s", i=2, h=4)
        probT = carve(2 * 2 * 512, "p (i b c) -> p i b c", i=2, b=2)
        pc = carve(NT * P, "p (t c) -> p t c", t=NT)
        y = big[:, 0:NT * D].rearrange("p (m t c) -> p m t c", m=2, t=NT)
        o_tmp = carve(512)
        used[0] = NT * D + Q_END
        yT = carve(2 * 4 * SEQ, "p (m k t) -> p m k t", m=2, k=4)
        mergedT = carve(NK * SEQ, "p (k t) -> p k t", k=NK)
        gate_prod = carve(2 * SEQ)
        assert used[0] <= NT * D + Q_END + NT * ROW + NT * NORM_SLOTS * HD
        used[0] = NT * D + Q_END
        qPT = carve(16 * SEQ, "p (c t) -> p c t", c=16)
        keyscore = carve(NT * 16 * NKEYS, "p (t c n) -> p t c n", t=NT, c=16)
        keyrest = carve(NT * 16 * NKEYS, "p (t c n) -> p t c n", t=NT, c=16)
        top1 = carve(NT * 16 * PICKS, "p (t c k) -> p t c k", t=NT, c=16)
        idx1 = carve(NT * 16 * PICKS, "p (t c k) -> p t c k", t=NT, c=16)
        cand = carve(NT * HEADS * 256, "p (t h c) -> p t h c", t=NT, h=HEADS)
        candrest = carve(NT * HEADS * 256, "p (t h c) -> p t h c", t=NT, h=HEADS)
        top2 = carve(NT * 128, "p (t h k) -> p t h k", t=NT, h=HEADS)
        pos2 = carve(NT * 128, "p (t h k) -> p t h k", t=NT, h=HEADS)
        which = carve(2 * NT * 128, "p (v t h k) -> p v t h k", v=2, t=NT, h=HEADS)
        whichf = carve(2 * NT * 128, "p (v t h k) -> p v t h k", v=2, t=NT, h=HEADS)
        picks = carve(3 * NT * 128, "p (v t h k) -> p v t h k", v=3, t=NT, h=HEADS)
        expo = carve(NT * 128, "p (t h k) -> p t h k", t=NT, h=HEADS)
        used[0] = NT * D
        pw = carve(NT * D, "p (t d) -> p t d", t=NT)
        gate = carve(NT * D, "p (t d) -> p t d", t=NT)
        plen = carve(D)

        junk = big[:, SEQ * NKEYS - D:SEQ * NKEYS]
        idx1u = idx1.bitcast(U32)
        pos2u = pos2.bitcast(U32)
        whichu = which.bitcast(U32)

        ss = small[:, 0:2]
        rstd = small[:, 2:4]
        psq = small[:, 4:6]
        prstd = small[:, 6:8]
        ms = small[:, 8:50].rearrange("p (t s) -> p t s", t=NT)
        msr = small[:, 50:92].rearrange("p (t s) -> p t s", t=NT)
        sg = small[:, 92:140].rearrange("p (t s) -> p t s", t=NT)
        iwb = small[:, 140:156].rearrange("p (t s) -> p t s", t=NT)
        cms = small[:, 156:158]
        maxes = small[:, 160:208].rearrange("p (i h) -> p i h", h=4)
        nmax = small[:, 208:256].rearrange("p (i h) -> p i h", h=4)
        sums = small[:, 256:304].rearrange("p (i h) -> p i h", h=4)
        coef = small[:, 304:352].rearrange("p (i h) -> p i h", h=4)
        csum = small[:, 352:368].rearrange("p (t h) -> p t h", t=NT)
        ccoef = small[:, 368:384].rearrange("p (t h) -> p t h", t=NT)
        cmax = small[:, 384:400].rearrange("p (t h) -> p t h", t=NT)
        gsum = small[:, 400:416].rearrange("p (t h) -> p t h", t=NT)
        top8 = small[:, 416:432].rearrange("p (t k) -> p t k", t=NT)
        gmax = small[:, 432:448].rearrange("p (t h) -> p t h", t=NT)
        grec = small[:, 448:464].rearrange("p (t h) -> p t h", t=NT)

        rms_steps = [rstd, msr, cms[0:2 * CP, 1:2], rstd, prstd, rstd]

        def bank(b, lo=0, hi=512):
            return ps[:, b, lo:hi]

        in_dma = sem("in_dma", False)
        consts_pool = sem("consts_pool", False)
        consts_dve = sem("consts_dve", False)
        consts_act = sem("consts_act", False)
        angle_done = sem("angle_done", False)
        pair_full = [sem(f"pair_full{s}", False) for s in range(RING)]
        pair_free = sem("pair_free", False)
        out_dma = sem("out_dma", False)
        layer_done = sem("layer_done", False)
        layer_over = sem("layer_over", False)
        layer_go = sem("layer_go", False)
        params_in = sem("params_in")
        squares = sem("squares")
        rms_in = sem("rms_in")
        rms_out = sem("rms_out")
        xn_ready = sem("xn_ready")
        xT_ps = sem("xT_ps")
        hT_ready = sem("hT_ready")
        row_ps = sem("row_ps")
        row_ready = sem("row_ready")
        mg_ps = sem("mg_ps")
        mg_ready = sem("mg_ready")
        cdup_ready = sem("cdup_ready")
        sg_ready = sem("sg_ready")
        rope_done = sem("rope_done")
        qk_ps = sem("qk_ps")
        qk_ready = sem("qk_ready")
        cmp_ps = sem("cmp_ps")
        z_ready = sem("z_ready")
        hid_ready = sem("hid_ready")
        kc_ready = sem("kc_ready")
        kcT_ready = sem("kcT_ready")
        idx_ps = sem("idx_ps")
        relu_ready = sem("relu_ready")
        relu_used = sem("relu_used")
        cs_ps = sem("cs_ps")
        cs_sub = sem("cs_sub")
        cs_exp = sem("cs_exp")
        pc_ready = sem("pc_ready")
        pcT_ps = sem("pcT_ps")
        pcT_ready = sem("pcT_ready")
        oc_ps = sem("oc_ps")
        s_ps = sem("s_ps")
        sm_ready = sem("sm_ready")
        prob_ready = sem("prob_ready")
        pT_ps = sem("pT_ps")
        pT_ready = sem("pT_ready")
        o_ps = sem("o_ps")
        y_added = sem("y_added")
        yT_ps = sem("yT_ps")
        yT_ready = sem("yT_ready")
        br_ps = sem("br_ps")
        br_ready = sem("br_ready")
        wo_ps = sem("wo_ps")
        q_ps = sem("q_ps")
        q_ready = sem("q_ready")
        ks_ps = sem("ks_ps")
        ks_ready = sem("ks_ready")
        picks_ready = sem("picks_ready")
        gexp_in = sem("gexp_in")
        gexp_out = sem("gexp_out")
        pickT_ps = sem("pickT_ps")
        pickT_ready = sem("pickT_ready")
        hot_ready = sem("hot_ready")
        act_hot_ready = sem("act_hot_ready")
        g_ps = sem("g_ps")
        g_ready = sem("g_ready")
        hs_hi = sem("hs_hi")
        hs_lo = sem("hs_lo")
        w_hi = sem("w_hi")
        w_used = sem("w_used")
        hi_ready = sem("hi_ready")
        v0_rest = sem("v0_rest")
        lo_ready = sem("lo_ready")
        plen_in = sem("plen_in")
        act_ps = sem("act_ps")
        act_ready = sem("act_ready")
        wgt_ready = sem("wgt_ready")
        wgt_used = sem("wgt_used")
        pw_ps = sem("pw_ps")
        pw_ready = sem("pw_ready")
        pg_ps = sem("pg_ps")
        pg_ready = sem("pg_ready")
        ENGINES = 4

        block = ctx.enter_context(nc.Block())

        @block.sync
        def _(sp):
            sp.dma_start(x[:, :, :], x_in.rearrange("o (t p) d -> p (o t) d", p=P)).then_inc(in_dma, 16)
            sp.dma_start(small[:, 0:8], inv_freq).then_inc(in_dma, 16)
            sp.dma_start(small[:, 8:11].bitcast(I32), positions).then_inc(in_dma, 16)
            for s in range(RING):
                sp.dma_start(ring[:, s, :, :], stream[s]).then_inc(pair_full[s], 16)
            with sp.Fori(1, DEPTH * PAIRS // RING) as turn:
                for s in range(RING):
                    need = sp.snap(turn * RING + (s + 1 - RING))
                    src = sp.snap(turn * RING + s)
                    sp.wait_ge(pair_free, need)
                    sp.dma_start(ring[:, s, :, :],
                                 stream[bass.ds(src, 1)].rearrange("o p b c -> p (o b) c")).then_inc(pair_full[s], 16)
            sp.wait_ge(layer_go, DEPTH)
            sp.dma_start(out.rearrange("o (t p) d -> p (o t) d", p=P), x[:, :, :]).then_inc(out_dma, 16)
            sp.wait_ge(out_dma, 16)

        @block.gpsimd
        def _(g):
            g.memset(ident[:, :], 0.0)
            g.memset(causal[:, :], 0.0)
            g.memset(minus_half[:, :], -0.5)
            g.memset(cmask[:, :, :], 1.0)
            g.memset(cneg[:, :, :], 0.0)
            g.memset(headmask[:, :], 1.0)
            g.iota(iota[:, :], pattern=[[1, P]], base=0, channel_multiplier=0, allow_small_or_imprecise_dtypes=True)
            g.drain()
            g.affine_select(out=ident[:, :], in_=ident[:, :], compare_op=ALU.not_equal, fill=1.0,
                            base=0, pattern=[[-1, P]], channel_multiplier=1)
            g.affine_select(out=causal[:, :], in_=causal[:, :], compare_op=ALU.is_ge, fill=NEG,
                            base=P, pattern=[[-1, SEQ]], channel_multiplier=1)
            g.affine_select(out=cmask[:, :, :], in_=cmask[:, :, :], compare_op=ALU.is_ge, fill=0.0,
                            base=-(CMP_LEN - 1), pattern=[[P, NT], [-CMP_STRIDE, CP]], channel_multiplier=1)
            g.affine_select(out=cneg[:, :, :], in_=cneg[:, :, :], compare_op=ALU.is_ge, fill=NEG,
                            base=-(CMP_LEN - 1), pattern=[[P, NT], [-CMP_STRIDE, CP]], channel_multiplier=1)
            g.affine_select(out=headmask[:, :], in_=headmask[:, :], compare_op=ALU.is_ge, fill=0.0,
                            base=0, pattern=[[-CP, HEADS]], channel_multiplier=1)
            g.drain()
            g.affine_select(out=headmask[:, :], in_=headmask[:, :], compare_op=ALU.is_ge, fill=0.0,
                            base=CP - 1, pattern=[[CP, HEADS]], channel_multiplier=-1)
            g.drain().then_inc(consts_pool, 1)
            with g.Fori(0, DEPTH) as layer:
                for n, v in enumerate(rms_steps):
                    g.wait_ge(rms_in, n + 1)
                    flat = v if len(v.shape) == 2 else v.rearrange("p a b -> p (a b)")
                    g.tensor_tensor(flat, flat, minus_half[0:v.shape[0], 0:flat.shape[1]], ALU.pow).then_inc(rms_out, 1)
                    if n == 3:
                        first_pair = B_EXP // 2
                        g.wait_ge(hi_ready, 2)
                        for p, blk, done in ((0, 0, None), (0, 1, pair_free), (1, 0, v0_rest)):
                            slot = (first_pair + p) % RING
                            if p:
                                g.wait_ge(hi_ready, 3)
                            ins = g.tensor_tensor(split[:, slot, blk, 1, :], ring[:, slot, blk, :],
                                                  split[:, slot, blk, 0, :].bitcast(F32), ALU.subtract)
                            if done:
                                ins.then_inc(done, 1)
                g.drain().then_inc(layer_done, 1)
                g.wait_ge(layer_done, layer * ENGINES + ENGINES)
                g.sem_inc(layer_over, 1)
                for s in layer_sems:
                    g.sem_clear(s)
                g.sem_inc(layer_go, 1)

        @block.scalar
        def _(a):
            a.wait_ge(angle_done, 1)
            a.activation(sin[:, :, :], sin[:, :, :], ACT.Sin)
            a.activation(cos[:, :, :], cos[:, :, :], ACT.Sin)
            a.drain().then_inc(consts_act, 1)
            a.wait_ge(in_dma, 3 * 16)

            def norm_squares():
                for t in range(NT):
                    a.activation(junk, x[:, t, :], ACT.Square, accum_out=ss[:, t:t + 1])
                    a.drain()
                a.drain().then_inc(squares, 1)

            def norm_hT(m, b0, gain):
                for j in range(4):
                    a.wait_ge(xT_ps, 4 * m + j + 1)
                    for k in (2 * j, 2 * j + 1):
                        src = bank(b0 + j, (k % 2) * SEQ, (k % 2 + 1) * SEQ)
                        ins = a.activation(hT[:, k, :], src, ACT.Copy,
                                           scale=1.0 if gain is None else par[:, gain + k:gain + k + 1])
                    ins.then_inc(hT_ready, 1)
                    if gain is not None:
                        a.drain()
                        a.activation(hs[:, 0, 2 * j * SEQ:(2 * j + 2) * SEQ], rest[:, 2 * j * SEQ:(2 * j + 2) * SEQ],
                                     ACT.Copy).then_inc(hs_hi, 1)

            with a.Fori(0, DEPTH) as layer:
                mine = params[bass.ds(layer, 1)].rearrange("o p c -> p (o c)")
                a.dma_start(par, mine[:, 0:Q_END]).then_inc(params_in, 16)
                a.dma_start(pT[:, :], mine[:, Q_PT:Q_PLEN]).then_inc(params_in, 16)
                norm_squares()
                turns = PAIRS // RING * 16

                def round_pair(p):
                    a.wait_ge(pair_full[p % RING], layer * turns + 16 * (p // RING + 1))
                    if p >= 2:
                        a.wait_ge(w_used, p - 1)
                    for blk in range(2):
                        a.activation(split[:, p % 2, blk, 0, :], ring[:, p % RING, blk, :], ACT.Copy).then_inc(w_hi, 1)

                round_pair(0)
                round_pair(1)
                a.wait_ge(params_in, 32)
                norm_hT(0, 4, Q_GA)
                for cb, (c0, w) in enumerate(ROW_BLOCKS):
                    round_pair(2 * cb + 2)
                    for t in range(NT):
                        n = cb * NT + t
                        a.wait_ge(row_ps, n + 1)
                        a.activation(rows[:, t, c0:c0 + w], bank(n % 4, 0, w), ACT.Copy).then_inc(row_ready, 1)
                    round_pair(2 * cb + 3)
                a.drain()
                for t in range(NT):
                    ins = a.activation(cdup[:, t, :, :].rearrange("p s (e d) -> p s e d", e=2),
                                       rows[:, t, C_CK:C_CK + 4 * HD].rearrange("p (s d) -> p s d", d=HD).unsqueeze(2)
                                       .broadcast_to([P, 4, 2, HD]), ACT.Copy)
                ins.then_inc(cdup_ready, 1)
                a.activation(sg[:, :, :], rows[:, :, C_NG:C_NG + 24], ACT.Sigmoid).then_inc(sg_ready, 1)

                for n in range(8):
                    a.wait_ge(mg_ps, n + 1)
                    a.activation(gateT[:, 2 * n:2 * n + 2, :], bank(4 + n % 2).rearrange("p (m t) -> p m t", m=2),
                                 ACT.Sigmoid).then_inc(mg_ready, 1)
                    if B_GATE // 2 + n + 2 < B_W1 // 2:
                        round_pair(B_GATE // 2 + n + 2)

                a.wait_ge(cmp_ps, 2)
                a.activation(hrow[0:2 * CP, 0, :], ps[0:2 * CP, 0, 0:256], ACT.Gelu_apprx_tanh).then_inc(hid_ready, 1)
                for n in range(9):
                    if n == 4:
                        a.wait_ge(cmp_ps, 3)
                        a.activation(hidT[:, :, :], bank(0, 256, 320).rearrange("p (f c) -> p f c", f=2),
                                     ACT.Copy).then_inc(hid_ready, 1)
                    a.wait_ge(qk_ps, n + 1)
                    a.activation(qkT[:, 2 * n:2 * n + 2, :], bank(4 + n % 4).rearrange("p (s t) -> p s t", s=2),
                                 ACT.Copy).then_inc(qk_ready, 1)
                for t in range(NT):
                    keys = (t + 1) * P
                    a.wait_ge(idx_ps, t + 1)
                    if t:
                        a.wait_ge(relu_used, t)
                    per = 512 // keys
                    for j in range(HEADS // per):
                        ins = a.activation(relu[:, j * per:(j + 1) * per, 0:keys],
                                           bank(2 + 2 * t + j).rearrange("p (h s) -> p h s", h=per), ACT.Relu, scale=SCALE)
                    ins.then_inc(relu_ready, 1)
                a.wait_ge(cmp_ps, 6)
                a.activation(hrow[0:2 * CP, 1, :], ps[0:2 * CP, 6, 0:256], ACT.Gelu_apprx_tanh).then_inc(hid_ready, 1)
                a.wait_ge(cmp_ps, 7)
                for half in range(2):
                    ins = a.activation(hidv[:, half, :].rearrange("p (g r n) -> p g r n", g=2, r=4),
                                       bank(6, 256 + 32 * half, 288 + 32 * half).rearrange("p (g n) -> p g n", g=2)
                                       .unsqueeze(2).broadcast_to([P, 2, 4, CP]), ACT.Copy)
                ins.then_inc(hid_ready, 1)
                for t in range(NT):
                    a.wait_ge(cs_sub, t + 1)
                    a.activation(pc[:, t, :], pc[:, t, :], ACT.Exp, scale=SCALE).then_inc(cs_exp, 1)
                def exps(i):
                    _, t, _ = ITEMS[i]
                    a.wait_ge(sm_ready, i + 1)
                    if i >= 2:
                        a.wait_ge(pT_ps, i - 1)
                    for h in range(4):
                        ins = a.activation(prob[:, i % 2, h, 0:(t + 1) * P], sm[:, i % 2, h, 0:(t + 1) * P], ACT.Exp,
                                           scale=SCALE, bias=nmax[:, i, h:h + 1], accum_out=sums[:, i, h:h + 1])
                    a.drain().then_inc(prob_ready, 1)

                def copies(i):
                    _, t, _ = ITEMS[i]
                    a.wait_ge(pT_ps, i + 1)
                    if i >= 2:
                        a.wait_ge(o_ps, i - 1)
                    for b in range(t + 1):
                        ins = a.activation(probT[:, i % 2, b, :], bank(4 + b), ACT.Copy)
                    ins.then_inc(pT_ready, 1)

                for i in range(len(ITEMS)):
                    exps(i)
                    if i == 0:
                        a.wait_ge(pcT_ps, 1)
                        a.activation(relu[:, 0:1, :], bank(6, 0, 256).rearrange("p (h s) -> p h s", h=1),
                                     ACT.Copy).then_inc(pcT_ready, 1)
                    if i:
                        copies(i - 1)
                copies(len(ITEMS) - 1)
                for n in range(4):
                    a.wait_ge(yT_ps, n + 1)
                    a.activation(yT[:, n // 2, 2 * (n % 2):2 * (n % 2) + 2, :],
                                 bank(n).rearrange("p (k t) -> p k t", k=2), ACT.Copy).then_inc(yT_ready, 1)

                a.wait_ge(xn_ready, 2)
                norm_squares()
                norm_hT(1, 4, Q_GF)

                def key_copies(h):
                    for t in range(NT):
                        a.wait_ge(ks_ps, h * NT + t + 1)
                        a.activation(keyscore[:, t, 2 * h:2 * h + 2, :],
                                     bank(2 + t, 0, 2 * P).rearrange("p (c n) -> p c n", c=2), ACT.Copy).then_inc(ks_ready, 1)

                for n in range(HEADS):
                    a.wait_ge(q_ps, n + 1)
                    a.activation(qPT[:, 2 * n:2 * n + 2, :], bank(n % 2).rearrange("p (c t) -> p c t", c=2),
                                 ACT.Copy).then_inc(q_ready, 1)
                    if n:
                        key_copies(n - 1)
                key_copies(HEADS - 1)
                first_pair = B_EXP // 2

                def round_block(slot, blk):
                    a.activation(split[:, slot, blk, 0, :], ring[:, slot, blk, :], ACT.Copy).then_inc(hi_ready, 1)

                def gelu(j, acts, weights):
                    a.wait_ge(act_ps, acts)
                    a.wait_ge(wgt_ready, weights)
                    a.activation(act[:, j % 2, :], bank(4 + j % 2, 0, SEQ), ACT.Gelu_apprx_tanh).then_inc(act_ready, 1)

                for p, blks in ((first_pair, (0, 1)), (first_pair + 1, (0,))):
                    a.wait_ge(pair_full[p % RING], layer * turns + 16 * (p // RING + 1))
                    for blk in blks:
                        round_block(p % RING, blk)
                a.wait_ge(gexp_in, 1)
                a.activation(expo[:, :, :, :], expo[:, :, :, :], ACT.Exp).then_inc(gexp_out, 1)
                a.wait_ge(pickT_ps, 1)
                a.activation(pickT[:, 0:2, :], bank(6).rearrange("p (v t) -> p v t", v=2), ACT.Copy).then_inc(pickT_ready, 1)
                a.activation(neg2[:, :], bank(6, SEQ, 2 * SEQ), ACT.Copy, scale=-1.0)
                a.activation(pickT[:, 2, :], bank(7, 0, SEQ), ACT.Copy).then_inc(pickT_ready, 1)
                a.drain()
                a.sem_inc(g_ready, 2)

                def hots(b, step, token):
                    a.wait_ge(g_ps, step + 1)
                    for j in range(4 - ACT_HOTS[b], 4):
                        a.activation(onehot2[:, b, j, :], iota[:, :], ACT.Abs, bias=neg2[:, token(j)])
                    a.drain()
                    for j in range(4 - ACT_HOTS[b], 4):
                        ins = a.activation(onehot2[:, b, j, :], onehot2[:, b, j, :], ACT.Relu, scale=-2.0,
                                           bias=pickT[:, 2, token(j)])
                    ins.then_inc(act_hot_ready, 1)

                def table(b, step, at):
                    a.wait_ge(g_ps, step + 3)
                    a.activation(big[:, at], bank(6 + b), ACT.Copy).then_inc(g_ready, 1)

                hots(0, 0, lambda j: slice(j, j + 1))
                with a.Fori(0, SEQ // 8 - 1) as i:
                    for b in range(2):
                        hots((b + 1) % 2, i * 2 + (b + 1), lambda j: bass.ds(i * 8 + (4 * b + 4 + j), 1))
                        table(b, i * 2 + b, bass.ds(i * (8 * P) + b * 4 * P, 4 * P))
                steps = SEQ // 4
                hots(1, steps - 1, lambda j: slice(SEQ - 4 + j, SEQ - 3 + j))
                for b in range(2):
                    at = (steps - 2 + b) * 4 * P
                    table(b, steps - 2 + b, slice(at, at + 4 * P))
                a.activation(small[:, 464:465], zero16[:, 0:1], ACT.Gelu_apprx_tanh)
                with a.Fori(0, NCHUNK // BODY - 1) as i:
                    for j in range(BODY):
                        gelu(j, i * BODY + (j + 1), i * BODY + (j + 1))
                        round_block((first_pair + 1 + j) % RING, 1)
                        slot, step = (first_pair + 2 + j) % RING, (first_pair + 2 + j) // RING
                        a.wait_ge(pair_full[slot], layer * turns + (i * 16 + 16 * (step + 1)))
                        a.wait_ge(wgt_used, i * BODY + (j + 3))
                        round_block(slot, 0)
                gelu(0, NCHUNK - 1, NCHUNK - 1)
                round_block((first_pair + NCHUNK - 1) % RING, 1)
                gelu(1, NCHUNK, NCHUNK)

                a.wait_ge(pw_ps, 1)
                a.dma_start(plen, mine[:, Q_PLEN:NPARAM]).then_inc(plen_in, 16)
                for n in range(4):
                    a.activation(pw[:, n // 2, (n % 2) * 512:(n % 2) * 512 + 512], bank(4 + n), ACT.Copy)
                a.drain()
                for t in range(NT):
                    a.activation(junk, pw[:, t, :], ACT.Square, accum_out=psq[:, t:t + 1])
                    a.drain()
                a.drain().then_inc(pw_ready, 1)
                a.wait_ge(xn_ready, 4)
                norm_squares()
                norm_hT(2, 0, None)
                a.wait_ge(pg_ps, 1)
                for n in range(4):
                    a.activation(gate[:, n // 2, (n % 2) * 512:(n % 2) * 512 + 512], bank(4 + n),
                                 ACT.Sigmoid).then_inc(pg_ready, 1)
                a.drain().then_inc(layer_done, 1)
                a.wait_ge(layer_go, layer + 1)

        @block.vector
        def _(v):
            v.memset(zero16[:, :], 0.0)
            v.memset(sin[:, :, :], 0.0)
            v.drain().then_inc(consts_dve, 1)
            v.wait_ge(in_dma, 3 * 16)
            v.tensor_copy(small[:, 16:19], small[:, 8:11].bitcast(I32))
            v.drain()
            ang = small[:, 32:56].rearrange("p (t f) -> p t f", f=ROT2)
            v.tensor_tensor(ang, small[:, 16:19].unsqueeze(2).broadcast_to([P, 3, ROT2]),
                            small[:, 0:8].unsqueeze(1).broadcast_to([P, 3, ROT2]), ALU.mult)
            v.drain()
            v.tensor_scalar(small[:, 64:88], small[:, 32:56], 0.15915494309189535, None, ALU.mult)
            v.drain()
            v.tensor_copy(small[:, 96:120].bitcast(I32), small[:, 64:88])
            v.drain()
            v.tensor_copy(small[:, 64:88], small[:, 96:120].bitcast(I32))
            v.drain()
            v.scalar_tensor_tensor(small[:, 128:152], small[:, 64:88], -6.28125, small[:, 32:56], ALU.mult, ALU.add)
            v.drain()
            v.scalar_tensor_tensor(small[:, 160:184], small[:, 64:88], -0.0019353071795864769, small[:, 128:152],
                                   ALU.mult, ALU.add)
            v.drain()
            v.tensor_scalar(sin[:, :, :], small[:, 160:184].rearrange("p (t f) -> p t f", f=ROT2),
                            3.141592, -3.141592, ALU.min, ALU.max)
            v.drain()
            v.scalar_tensor_tensor(cos[:, :, :], sin[:, :, :], -1.0, sin[:, :, :], ALU.mult, ALU.max)
            v.drain()
            v.tensor_scalar(cos[:, :, :], cos[:, :, :], -1.0, 1.5707963267948966, ALU.mult, ALU.add)
            v.drain().then_inc(angle_done, 1)
            v.wait_ge(consts_act, 1)
            v.wait_ge(consts_pool, 1)

            def rsqrt_mean(step, src, n, meanwhile=()):
                v.tensor_scalar(rms_steps[step], src, 1.0 / n, EPS, ALU.mult, ALU.add).then_inc(rms_in, 1)
                for p in meanwhile:
                    rest_of_pair(p)
                v.wait_ge(rms_out, step + 1)

            def norm_x(m):
                v.wait_ge(squares, m + 1)
                rsqrt_mean((0, 3, 5)[m], ss[:, :], D)
                for t in range(NT):
                    ins = v.tensor_scalar(xn[:, t, :], x[:, t, :], rstd[:, t:t + 1], None, ALU.mult)
                ins.then_inc(xn_ready, 1)

            def rope(lo, hi, c, s, shape):
                n = 1
                for d in shape[1:]:
                    n *= d
                np_ = shape[0]
                parts = []
                for j in range(4):
                    a = tmp[0:np_, j * n:(j + 1) * n]
                    if len(shape) == 4:
                        a = a.rearrange("p (t s f) -> p t s f", t=shape[1], s=shape[2])
                    parts.append(a)
                v.tensor_tensor(parts[0], lo, c, ALU.mult)
                v.tensor_tensor(parts[1], hi, s, ALU.mult)
                v.tensor_tensor(parts[2], hi, c, ALU.mult)
                v.tensor_tensor(parts[3], lo, s, ALU.mult)
                v.drain()
                v.tensor_tensor(lo, parts[0], parts[1], ALU.subtract)
                return v.tensor_tensor(hi, parts[2], parts[3], ALU.add)

            def rest_of_hT(m):
                for j in range(4):
                    part = slice(2 * j * SEQ, (2 * j + 2) * SEQ)
                    v.wait_ge(hs_hi, 4 * m + j + 1)
                    v.tensor_tensor(hs[:, 1, part], rest[:, part], hs[:, 0, part].bitcast(F32),
                                    ALU.subtract).then_inc(hs_lo, 1)

            def rest_of(slot, block):
                return v.tensor_tensor(split[:, slot, block, 1, :], ring[:, slot, block, :],
                                       split[:, slot, block, 0, :].bitcast(F32), ALU.subtract)

            def rest_of_pair(p):
                for blk in range(2):
                    v.wait_ge(w_hi, 2 * p + blk + 1)
                    ins = rest_of(p % RING, blk)
                ins.then_inc(pair_free, 1)

            with v.Fori(0, DEPTH) as layer:
                norm_x(0)
                rest_of_pair(0)
                rest_of_hT(0)
                for p in range(1, B_GATE // 2 + 2):
                    rest_of_pair(p)

                v.wait_ge(row_ready, 2 * len(ROW_BLOCKS))
                v.wait_ge(params_in, 32)
                nrows = rows[:, :, 0:NORM_SLOTS * HD]
                nslots = nrows.rearrange("p t (s d) -> p t s d", d=HD)
                tslots = tmp.rearrange("p (t s d) -> p t s d", t=NT, d=HD)
                v.tensor_tensor(tmp.rearrange("p (t c) -> p t c", t=NT), nrows, nrows, ALU.mult)
                v.drain()
                v.tensor_reduce(ms[:, :, :], tslots, AX.X, ALU.add)
                v.drain()
                gate_pairs = iter(range(B_GATE // 2 + 2, B_W1 // 2))
                rsqrt_mean(1, ms[:, :, :], HD, (next(gate_pairs), next(gate_pairs)))
                v.tensor_tensor(nslots, nslots, msr[:, :, :].unsqueeze(3).broadcast_to([P, NT, NORM_SLOTS, HD]), ALU.mult)
                rest_of_pair(next(gate_pairs))
                v.drain()
                v.tensor_tensor(nrows, nrows, par[:, Q_GAIN:Q_GAIN + NORM_SLOTS * HD].unsqueeze(1)
                                .broadcast_to([P, NT, NORM_SLOTS * HD]), ALU.mult)
                v.drain()
                rslots = rows[:, :, 0:ROPE_SLOTS * HD].rearrange("p t (s d) -> p t s d", d=HD)
                shape = [P, NT, ROPE_SLOTS, ROT2]
                rope(rslots[:, :, :, 0:ROT2], rslots[:, :, :, ROT2:2 * ROT2],
                     cos[:, 0:NT, :].unsqueeze(2).broadcast_to(shape), sin[:, 0:NT, :].unsqueeze(2).broadcast_to(shape),
                     shape)
                rest_of_pair(next(gate_pairs))
                v.drain()
                for t in range(NT):
                    v.tensor_copy(kdup[:, t, 0:4, :].rearrange("p s (e d) -> p s e d", e=2),
                                  rows[:, t, C_KS:C_KS + 4 * HD].rearrange("p (s d) -> p s d", d=HD).unsqueeze(2)
                                  .broadcast_to([P, 4, 2, HD]))
                    for s, col in ((4, C_KB), (5, C_IK)):
                        ins = v.tensor_copy(kdup[:, t, s, :].rearrange("p (e d) -> p e d", e=2),
                                            rows[:, t, col:col + HD].unsqueeze(1).broadcast_to([P, 2, HD]))
                ins.then_inc(rope_done, 1)
                v.tensor_scalar(iwb[:, :, :], rows[:, :, C_IW:C_IW + 8], HEADS ** -0.5, None, ALU.mult)
                v.memset(Z[:, :, :, :, :], 0.0)
                v.memset(kcT, 0.0)
                rest_of_pair(next(gate_pairs))
                v.drain()

                v.wait_ge(cmp_ps, 1)
                for kv in range(2):
                    for gr in range(2):
                        for par_ in range(2):
                            lo = par_ * HD
                            src = ps[lo:lo + HD, kv, gr * SEQ:(gr + 1) * SEQ].rearrange(
                                "p (n j e) -> p e j n", j=8, e=2)[:, par_]
                            for half in range(2):
                                ins = v.tensor_tensor(
                                    Z[lo:lo + HD, kv, 8 * half:8 * half + 8, gr, 0:NCMP],
                                    src[:, :, half:half + NCMP],
                                    par[lo:lo + HD, Q_POS + 16 * kv + 8 * half:Q_POS + 16 * kv + 8 * half + 8]
                                    .unsqueeze(2).broadcast_to([HD, 8, NCMP]), ALU.add)
                v.drain().then_inc(z_ready, 1)
                for p in gate_pairs:
                    rest_of_pair(p)
                v.wait_ge(cmp_ps, 4)
                kcp = ps[0:2 * CP, 0, 320:320 + HD]
                kcs = kc[0:2 * CP, :]
                v.tensor_copy(kcs, kcp)
                v.drain()
                v.tensor_tensor(tmp[0:2 * CP, 0:HD], kcs, kcs, ALU.mult)
                v.drain()
                v.tensor_reduce(cms[0:2 * CP, 0:1], tmp[0:2 * CP, 0:HD], AX.X, ALU.add)
                v.drain()
                rsqrt_mean(2, cms[0:2 * CP, 0:1], HD)
                v.scalar_tensor_tensor(kcs, kcs, cms[0:2 * CP, 1:2], par[0:2 * CP, Q_CGAIN:Q_CGAIN + HD],
                                       ALU.mult, ALU.mult)
                v.drain()
                rope(kc[0:2 * CP, 0:ROT2], kc[0:2 * CP, ROT2:2 * ROT2], cos[0:2 * CP, NT, :], sin[0:2 * CP, NT, :],
                     [2 * CP, ROT2])
                v.drain()
                v.tensor_copy(kcdup[0:2 * CP, :].rearrange("p (e d) -> p e d", e=2),
                              kcs.unsqueeze(1).broadcast_to([2 * CP, 2, HD])).then_inc(kc_ready, 1)
                for t in range(NT):
                    keys = (t + 1) * P
                    sc = score[:, t, 0:keys]
                    cm = causal[:, SEQ - keys:SEQ]
                    v.wait_ge(relu_ready, t + 1)
                    for h in range(HEADS):
                        v.scalar_tensor_tensor(sc, relu[:, h % 2 * 4 + h // 2, 0:keys], iwb[:, t, h:h + 1], cm if h == 0 else sc,
                                               ALU.mult, ALU.add)
                        v.drain()
                    v.drain().then_inc(relu_used, 1)
                    if t == 0:
                        v.wait_ge(cmp_ps, 5)
                        for e in range(2):
                            ins = v.tensor_copy(kcT[e * HD:(e + 1) * HD, :].rearrange("p (g e n) -> p e g n", g=2, e=2)[:, e],
                                                ps[e * HD:(e + 1) * HD, 0, 384:384 + 2 * CP]
                                                .rearrange("p (g n) -> p g n", g=2))
                        ins.then_inc(kcT_ready, 1)

                def topk_round():
                    for t in range(NT):
                        v.max(top8[:, t, :], score[:, t, 0:(t + 1) * P])
                    v.drain()
                    for t in range(NT):
                        v.match_replace(score[:, t, 0:(t + 1) * P], top8[:, t, :], score[:, t, 0:(t + 1) * P], GONE)
                    v.drain()

                def dsa_mask():
                    for t in range(NT):
                        keys = (t + 1) * P
                        v.tensor_scalar(dmask[:, t, 0:keys], score[:, t, 0:keys], 0.5 * GONE, NEG, ALU.is_gt, ALU.mult)
                    v.drain()
                    for t in range(NT):
                        keys = (t + 1) * P
                        v.tensor_tensor(dmask[:, t, 0:keys], dmask[:, t, 0:keys], causal[:, SEQ - keys:SEQ], ALU.add)
                    v.drain()

                v.wait_ge(cs_ps, 1)
                for t in range(NT):
                    pcv = pc[:, t, :].rearrange("p (h n) -> p h n", h=HEADS)
                    v.tensor_tensor(pcv, bank(t, 0, P).rearrange("p (h n) -> p h n", h=HEADS),
                                    cneg[:, t, :].unsqueeze(1).broadcast_to([P, HEADS, CP]), ALU.add)
                    v.drain()
                    v.tensor_reduce(cmax[:, t, :], pcv, AX.X, ALU.max)
                    v.drain()
                    v.tensor_tensor(pcv, pcv, cmax[:, t, :].unsqueeze(2).broadcast_to([P, HEADS, CP]), ALU.subtract)
                    v.drain().then_inc(cs_sub, 1)
                def masked(i):
                    b, t, _ = ITEMS[i]
                    keys = (t + 1) * P
                    mk = dmask[:, t, 0:keys] if b == 2 else causal[:, SEQ - keys:SEQ]
                    v.wait_ge(s_ps, i + 1)
                    if i >= 2:
                        v.wait_ge(prob_ready, i - 1)
                    for h in range(4):
                        src = bank(2 * ((i + 1) % 2) + h % 2, (h // 2) * keys, (h // 2 + 1) * keys)
                        v.tensor_tensor_reduce(out=sm[:, i % 2, h, 0:keys], in0=src, in1=mk, scale=1.0, scalar=GONE,
                                               op0=ALU.add, op1=ALU.max, accum_out=maxes[:, i, h:h + 1])
                    v.drain()
                    v.tensor_scalar(nmax[:, i, :], maxes[:, i, :], -SCALE, None, ALU.mult)
                    v.drain().then_inc(sm_ready, 1)

                def weighted(i):
                    b, t, hf = ITEMS[i]
                    v.wait_ge(prob_ready, i + 1)
                    v.reciprocal(coef[:, i, :], sums[:, i, :])
                    v.drain()
                    if b < 2:
                        v.tensor_tensor(coef[:, i, :], coef[:, i, :],
                                        sg[:, t, 8 * (b + 1) + 4 * hf:8 * (b + 1) + 4 * hf + 4], ALU.mult)
                        v.drain()
                    v.wait_ge(o_ps, i + 1)
                    cf = coef[:, i, :].unsqueeze(2).broadcast_to([P, 4, HD])
                    src = bank(6 + i % 2, 0, 256).rearrange("p (h d) -> p h d", h=4)
                    if b == 2:
                        v.tensor_tensor(y[:, 1, t, 256 * hf:256 * hf + 256].rearrange("p (h d) -> p h d", h=4),
                                        src, cf, ALU.mult)
                    else:
                        v.tensor_tensor(o_tmp[:, 0:256].rearrange("p (h d) -> p h d", h=4), src, cf, ALU.mult)
                        v.drain()
                        v.tensor_tensor(y[:, 0, t, 256 * hf:256 * hf + 256], y[:, 0, t, 256 * hf:256 * hf + 256],
                                        o_tmp[:, 0:256], ALU.add)
                    v.drain().then_inc(y_added, 1)

                def compressed_probs():
                    for t in range(NT):
                        pcv = pc[:, t, :].rearrange("p (h n) -> p h n", h=HEADS)
                        v.wait_ge(cs_exp, t + 1)
                        v.tensor_reduce(csum[:, t, :], pcv, AX.X, ALU.add)
                        v.drain()
                        v.reciprocal(ccoef[:, t, :], csum[:, t, :])
                        v.tensor_tensor(pcv, pcv, cmask[:, t, :].unsqueeze(1).broadcast_to([P, HEADS, CP]), ALU.mult)
                        v.drain()
                    v.wait_ge(sg_ready, 1)
                    v.tensor_tensor(ccoef[:, :, :], ccoef[:, :, :], sg[:, :, 0:8], ALU.mult)
                    v.wait_ge(cmp_ps, 8)
                    v.tensor_tensor(vcblk[:, :, :], bank(6, 320, 384).unsqueeze(1).broadcast_to([P, HEADS, HD]),
                                    headmask[:, :].unsqueeze(2).broadcast_to([P, HEADS, HD]), ALU.mult)
                    v.drain().then_inc(pc_ready, 1)

                def compressed_out():
                    for t in range(NT):
                        v.wait_ge(oc_ps, t + 1)
                        v.tensor_tensor(y[:, 0, t, :].rearrange("p (h d) -> p h d", h=HEADS),
                                        bank(4 + t).rearrange("p (h d) -> p h d", h=HEADS),
                                        ccoef[:, t, :].unsqueeze(2).broadcast_to([P, HEADS, HD]), ALU.mult)
                    v.drain().then_inc(y_added, 1)

                for i in range(len(ITEMS)):
                    if i == TOPK_ROUNDS:
                        dsa_mask()
                    masked(i)
                    if i == 0:
                        compressed_probs()
                    if i == 1:
                        compressed_out()
                    if i >= 2:
                        weighted(i - 2)
                    if i < TOPK_ROUNDS:
                        topk_round()
                weighted(len(ITEMS) - 2)
                weighted(len(ITEMS) - 1)

                v.wait_ge(mg_ready, 8)
                for m in range(NK):
                    v.wait_ge(br_ps, m + 1)
                    v.tensor_tensor(gate_prod[:, 0:SEQ], bank(4 + m % 4, 0, SEQ), gateT[:, m, :], ALU.mult)
                    v.tensor_tensor(gate_prod[:, SEQ:2 * SEQ], bank(4 + m % 4, SEQ, 2 * SEQ), gateT[:, NK + m, :], ALU.mult)
                    v.drain()
                    v.tensor_tensor(mergedT[:, m, :], gate_prod[:, 0:SEQ], gate_prod[:, SEQ:2 * SEQ],
                                    ALU.add)
                    v.drain().then_inc(br_ready, 1)
                v.wait_ge(wo_ps, 1)
                for n in range(4):
                    xs = x[:, n // 2, (n % 2) * 512:(n % 2) * 512 + 512]
                    v.tensor_tensor(xs, bank(n), xs, ALU.add)
                v.drain().then_inc(xn_ready, 1)

                norm_x(1)
                rest_of_hT(1)
                first_pair = B_EXP // 2

                for first, last in ((0, 1), (1, 2), (2, 4), (4, 6), (6, 8)):
                    v.wait_ge(ks_ready, NT * last)
                    both = [(t, c) for t in range(NT) for c in range(2 * first, 2 * last)]
                    heads = [(t, h) for t in range(NT) for h in range(first, last)]
                    hs_ = slice(first, last)
                    cs_ = slice(2 * first, 2 * last)
                    shape = [P, last - first, PICKS, PICKS]
                    for t, c in both:
                        v.max(top1[:, t, c, 0:8], keyscore[:, t, c, :])
                    v.drain()
                    for t, c in both:
                        v.max_index(idx1u[:, t, c, 0:8], top1[:, t, c, 0:8], keyscore[:, t, c, :])
                        v.match_replace(keyrest[:, t, c, :], top1[:, t, c, 0:8], keyscore[:, t, c, :], GONE)
                    v.drain()
                    for t, c in both:
                        v.max(top1[:, t, c, 8:16], keyrest[:, t, c, :])
                    v.drain()
                    for t, c in both:
                        v.max_index(idx1u[:, t, c, 8:16], top1[:, t, c, 8:16], keyrest[:, t, c, :])
                    for t in range(NT):
                        tv = top1[:, t, cs_, :].rearrange("p (h s) k -> p h s k", s=2)
                        v.tensor_tensor(cand[:, t, hs_, :].rearrange("p h (a b) -> p h a b", a=PICKS),
                                        tv[:, :, 0, :].unsqueeze(3).broadcast_to(shape),
                                        tv[:, :, 1, :].unsqueeze(2).broadcast_to(shape), ALU.add)
                    v.drain()
                    for t, h in heads:
                        v.max(top2[:, t, h, 0:8], cand[:, t, h, :])
                    v.drain()
                    for t, h in heads:
                        v.max_index(pos2u[:, t, h, 0:8], top2[:, t, h, 0:8], cand[:, t, h, :])
                        v.match_replace(candrest[:, t, h, :], top2[:, t, h, 0:8], cand[:, t, h, :], GONE)
                    v.drain()
                    for t, h in heads:
                        v.max(top2[:, t, h, 8:16], candrest[:, t, h, :])
                    v.drain()
                    ins = v.tensor_tensor(expo[:, :, hs_, :], top2[:, :, hs_, :],
                                          top2[:, :, hs_, 0:1].broadcast_to([P, NT, last - first, PICKS]), ALU.subtract)
                    if last == HEADS:
                        ins.then_inc(gexp_in, 1)
                    for t, h in heads:
                        v.max_index(pos2u[:, t, h, 8:16], top2[:, t, h, 8:16], candrest[:, t, h, :])
                    v.drain()
                    v.tensor_scalar(whichu[:, 0, :, hs_, :], pos2u[:, :, hs_, :], 4, None, ALU.logical_shift_right)
                    v.tensor_scalar(whichu[:, 1, :, hs_, :], pos2u[:, :, hs_, :], PICKS - 1, None, ALU.bitwise_and)
                    v.tensor_copy(top1[:, :, cs_, :], idx1u[:, :, cs_, :])
                    v.drain()
                    for s in range(2):
                        v.tensor_copy(whichf[:, s, :, hs_, :], whichu[:, s, :, hs_, :])
                    v.drain()
                    for t in range(NT):
                        for s in range(2):
                            eq = (cand if s == 0 else candrest)[:, t, hs_, :].rearrange("p h (k j) -> p h k j", k=PICKS)
                            v.tensor_tensor(eq, iota[:, 0:PICKS].unsqueeze(1).unsqueeze(1).broadcast_to(shape),
                                            whichf[:, s, t, hs_, :].unsqueeze(3).broadcast_to(shape), ALU.is_equal)
                    v.drain()
                    for t in range(NT):
                        for s in range(2):
                            eq = (cand if s == 0 else candrest)[:, t, hs_, :].rearrange("p h (k j) -> p h k j", k=PICKS)
                            tv = top1[:, t, cs_, :].rearrange("p (h s) k -> p h s k", s=2)
                            v.tensor_tensor(eq, eq, tv[:, :, s, :].unsqueeze(2).broadcast_to(shape), ALU.mult)
                    v.drain()
                    for t in range(NT):
                        for s in range(2):
                            eq = (cand if s == 0 else candrest)[:, t, hs_, :].rearrange("p h (k j) -> p h k j", k=PICKS)
                            v.tensor_reduce(picks[:, s, t, hs_, :], eq, AX.X, ALU.add)
                v.wait_ge(gexp_out, 1)
                v.tensor_reduce(gsum[:, :, :], expo[:, :, :, :], AX.X, ALU.add)
                v.drain()
                v.reciprocal(grec[:, :, :], gsum[:, :, :])
                v.drain()
                v.tensor_tensor(picks[:, 2], expo[:, :, :, :],
                                grec[:, :, :].unsqueeze(3).broadcast_to([P, NT, HEADS, PICKS]), ALU.mult)
                v.drain().then_inc(picks_ready, 1)

                v.sem_inc(wgt_ready, 2)
                v.wait_ge(v0_rest, 1)
                v.sem_inc(lo_ready, 1)

                v.wait_ge(pickT_ready, 2)
                with v.Fori(0, SEQ // 8) as i:
                    for b in range(2):
                        v.wait_ge(g_ps, i * 2 + (b + 1))
                        four = pickT[:, 0, bass.ds(i * 8 + 4 * b, 4)]
                        v.tensor_tensor(onehot1[:, b, :, :], iota[:, :].unsqueeze(1).broadcast_to([P, 4, P]),
                                        four.unsqueeze(2).broadcast_to([P, 4, P]), ALU.is_equal)
                        for j in range(4 - ACT_HOTS[b]):
                            tok = bass.ds(i * 8 + (4 * b + j), 1)
                            ins = v.tensor_scalar(onehot2[:, b, j, :], iota[:, :], pickT[:, 1, tok], pickT[:, 2, tok],
                                                  ALU.is_equal, ALU.mult)
                        ins.then_inc(hot_ready, 1)
                v.wait_ge(g_ready, SEQ // 4 + 2)

                def weights(j, chunk, acts, used):
                    v.wait_ge(act_ready, acts)
                    v.tensor_tensor(act[:, j % 2, :], act[:, j % 2, :], G[:, :, chunk].squeeze(2), ALU.mult)
                    v.drain()
                    v.wait_ge(wgt_used, used)
                    v.tensor_copy(wgt[:, j % 2, 0, :], act[:, j % 2, :])
                    v.drain()
                    v.tensor_tensor(wgt[:, j % 2, 1, :], act[:, j % 2, :], wgt[:, j % 2, 0, :].bitcast(F32),
                                    ALU.subtract).then_inc(wgt_ready, 1)

                with v.Fori(0, NCHUNK // BODY - 1) as i:
                    for j in range(BODY):
                        weights(j, bass.ds(i * BODY + j, 1), i * BODY + (j + 1), i * BODY + (j + 2))
                        v.wait_ge(hi_ready, i * (2 * BODY) + (2 * j + 4))
                        rest_of((first_pair + 1 + j) % RING, 1).then_inc(pair_free, 1)
                        v.wait_ge(hi_ready, i * (2 * BODY) + (2 * j + 5))
                        rest_of((first_pair + 2 + j) % RING, 0).then_inc(lo_ready, 1)
                weights(0, bass.ds(NCHUNK - 2, 1), NCHUNK - 1, NCHUNK)
                v.wait_ge(hi_ready, 2 * NCHUNK)
                rest_of((first_pair + NCHUNK - 1) % RING, 1).then_inc(pair_free, 1)
                weights(1, bass.ds(NCHUNK - 1, 1), NCHUNK, NCHUNK + 1)
                v.wait_ge(wgt_used, NCHUNK + 3)
                for n in range(4):
                    xs = x[:, n // 2, (n % 2) * 512:(n % 2) * 512 + 512]
                    v.tensor_tensor(xs, bank(n), xs, ALU.add)
                v.drain().then_inc(xn_ready, 1)

                v.wait_ge(pw_ready, 1)
                rsqrt_mean(4, psq[:, :], D)
                norm_x(2)
                v.wait_ge(plen_in, 16)
                for t in range(NT):
                    v.scalar_tensor_tensor(pw[:, t, :], pw[:, t, :], prstd[:, t:t + 1], plen,
                                           ALU.mult, ALU.mult)
                v.drain()
                v.wait_ge(pg_ready, 4)
                for t in range(NT):
                    v.tensor_tensor(pw[:, t, :], pw[:, t, :], gate[:, t, :], ALU.mult)
                v.drain()
                for t in range(NT):
                    v.tensor_tensor(x[:, t, :], x[:, t, :], pw[:, t, :], ALU.add)
                v.drain().then_inc(layer_done, 1)
                v.wait_ge(layer_go, layer + 1)

        @block.tensor
        def _(pe):
            pe.wait_ge(consts_pool, 1)
            pe.wait_ge(consts_dve, 1)
            with pe.Fori(0, DEPTH) as layer:
                turns = PAIRS // RING * 16

                def block_of(n):
                    return ring[:, (n // 2) % RING, n % 2, :]

                def arrive(n):
                    if n % 2 == 0:
                        p = n // 2
                        pe.wait_ge(pair_full[p % RING], layer * turns + 16 * (p // RING + 1))

                owed = [0]
                split_read = [0]

                def settle(ins):
                    if owed[0]:
                        ins.then_inc(pair_free, owed[0])
                        owed[0] = 0
                    elif split_read[0]:
                        ins.then_inc(w_used, split_read[0])
                        split_read[0] = 0

                def norm_T(m, b0):
                    pe.wait_ge(xn_ready, [1, 3, 5][m])
                    for j in range(4):
                        for k in (2 * j, 2 * j + 1):
                            for t in range(NT):
                                ins = pe.transpose(bank(b0 + j, (k % 2) * SEQ + t * P, (k % 2) * SEQ + t * P + P),
                                                   xn[:, t, k * P:(k + 1) * P], ident[:, :])
                                settle(ins)
                        ins.then_inc(xT_ps, 1)
                    pe.wait_ge(hT_ready, 4 * (m + 1))

                PASSES = ((0, 0), (0, 1), (1, 0))

                def columns(out, slot, block):
                    for k in range(NK):
                        for n, (s_, m) in enumerate(PASSES):
                            ins = pe.matmul(out, split[:, slot, block, s_, k * P:(k + 1) * P],
                                            hs[:, m, k * SEQ:(k + 1) * SEQ], start=(k == 0 and n == 0),
                                            stop=(k == NK - 1 and n == 2))
                            settle(ins)
                    return ins

                norm_T(0, 4)
                pe.wait_ge(hs_lo, 4)
                for cb, (c0, w) in enumerate(ROW_BLOCKS):
                    for half in range(2):
                        pe.wait_ge(pair_free, layer * PAIRS + (2 * cb + half + 1))
                        for t in range(NT):
                            n = cb * NT + t
                            if n >= 4 and half == 0:
                                pe.wait_ge(row_ready, n - 3)
                            for k in range(4 * half, 4 * half + 4):
                                for q, (s_, m) in enumerate(PASSES):
                                    at = (k % 2) * 512
                                    ins = pe.matmul(bank(n % 4, 0, w),
                                                    hs[:, s_, k * SEQ + t * P:k * SEQ + (t + 1) * P],
                                                    split[:, half, k // 2 % 2, m, at:at + w],
                                                    start=(k == 0 and q == 0), stop=(k == NK - 1 and q == 2))
                                    settle(ins)
                            if half == 1:
                                ins.then_inc(row_ps, 1)
                        split_read[0] += 1
                def raw_T():
                    pe.wait_ge(cdup_ready, 1)
                    for kv in range(2):
                        for gr in range(2):
                            for t in range(NT):
                                ins = pe.transpose(bank(kv, gr * SEQ + t * P, gr * SEQ + t * P + P),
                                                   cdup[:, t, 2 * kv + gr, :], ident[:, :])
                                settle(ins)
                    ins.then_inc(cmp_ps, 1)

                for c in range(16):
                    blk = B_GATE + c
                    if c == 2:
                        raw_T()
                    if c % 2 == 0:
                        pe.wait_ge(pair_free, layer * PAIRS + (blk // 2 + 1))
                    if c % 2 == 0 and c >= 4:
                        pe.wait_ge(mg_ready, c // 2 - 1)
                    ins = columns(bank(4 + (c // 2) % 2, (c % 2) * SEQ, (c % 2 + 1) * SEQ), blk // 2 % 2, c % 2)
                    if c % 2:
                        ins.then_inc(mg_ps, 1)
                        split_read[0] += 1

                def transposes(n):
                    if n >= 4:
                        pe.wait_ge(qk_ready, n - 3)
                    for s in (2 * n, 2 * n + 1):
                        for t in range(NT):
                            src = rows[:, t, T_SRC[s]:T_SRC[s] + P] if s < T_KS else kdup[:, t, s - T_KS, :]
                            ins = pe.transpose(bank(4 + n % 4, (s % 2) * SEQ + t * P, (s % 2) * SEQ + t * P + P),
                                               src, ident[:, :])
                            settle(ins)
                    ins.then_inc(qk_ps, 1)

                def hidden(kv, b):
                    for j in range(16):
                        if j % 4 == 0:
                            arrive(B_W1 + 4 * kv + j // 4)
                        ins = pe.matmul(ps[0:2 * CP, b, 0:256], Z[:, kv, j, :, :].rearrange("p g n -> p (g n)"),
                                        block_of(B_W1 + 4 * kv + j // 4).rearrange("p (j c) -> p j c", j=4)[:, j % 4, :],
                                        start=(j == 0), stop=(j == 15))
                        settle(ins)
                        if j == 7:
                            ins.then_inc(pair_free, 1)
                    owed[0] += 1
                    ins.then_inc(cmp_ps, 1)

                def hidden_T(kv, b):
                    pe.wait_ge(hid_ready, 2 * kv + 1)
                    for half in range(2):
                        ins = pe.transpose(bank(b, 256 + 32 * half, 288 + 32 * half),
                                           hrow[0:2 * CP, kv, half * P:(half + 1) * P], ident[0:2 * CP, 0:2 * CP])
                        settle(ins)
                    ins.then_inc(cmp_ps, 1)

                w2 = par[:, Q_W2:Q_W2 + 4 * HD].rearrange("p (v f d) -> p v f d", v=2, f=2)
                pe.wait_ge(z_ready, 1)
                hidden(0, 0)
                pe.wait_ge(mg_ready, 8)
                pe.wait_ge(rope_done, 1)
                for n in range(9):
                    if n == 4:
                        hidden_T(0, 0)
                    transposes(n)
                pe.wait_ge(hid_ready, 2)
                for half in range(2):
                    ins = pe.matmul(ps[0:2 * CP, 0, 320:320 + HD], hidT[:, half, :], w2[:, 0, half, :],
                                    start=(half == 0), stop=(half == 1))
                ins.then_inc(cmp_ps, 1)
                def side(h):
                    return (h % 2) * HD

                pe.wait_ge(qk_ready, 9)
                for t in range(NT):
                    keys = (t + 1) * P
                    per = 512 // keys
                    for h in range(HEADS):
                        lo = side(h)
                        at = h % 2 * 4 + h // 2
                        ins = pe.matmul(bank(2 + 2 * t + at // per, (at % per) * keys, (at % per + 1) * keys),
                                        qkT[lo:lo + HD, T_IQ + h // 2, t * P:(t + 1) * P],
                                        qkT[lo:lo + HD, T_IK, 0:keys], start=True, stop=True)
                    ins.then_inc(idx_ps, 1)
                pe.wait_ge(kc_ready, 1)
                pe.transpose(bank(0, 384, 384 + 2 * CP), kcdup[0:2 * CP, :],
                             ident[0:2 * CP, 0:2 * CP]).then_inc(cmp_ps, 1)
                pe.wait_ge(relu_ready, 2)
                hidden(1, 6)
                pe.wait_ge(kcT_ready, 1)
                for t in range(NT):
                    for hp in range(HEADS // 2):
                        ins = pe.matmul(bank(t, hp * 2 * CP, (hp + 1) * 2 * CP), qkT[:, T_NQ + hp, t * P:(t + 1) * P],
                                        kcT[:, hp // 2 * 2 * CP:(hp // 2 + 1) * 2 * CP], start=True, stop=True)
                        settle(ins)
                ins.then_inc(cs_ps, 1)
                hidden_T(1, 6)

                def scores(i):
                    b, t, hf = ITEMS[i]
                    keys = (t + 1) * P
                    if i >= 2:
                        pe.wait_ge(sm_ready, i - 1)
                    for j in range(4):
                        h = 4 * hf + j
                        lo = side(h)
                        q = (T_DQ if b == 2 else T_NQ) + h // 2
                        k = (T_KS + h // 4, T_KW + h // 4, T_KB)[b]
                        ins = pe.matmul(bank(2 * ((i + 1) % 2) + j % 2, (j // 2) * keys, (j // 2 + 1) * keys),
                                        qkT[lo:lo + HD, q, t * P:(t + 1) * P], qkT[lo:lo + HD, k, 0:keys],
                                        start=True, stop=True)
                    ins.then_inc(s_ps, 1)

                def prob_T(i):
                    _, t, _ = ITEMS[i]
                    pe.wait_ge(prob_ready, i + 1)
                    if i == 0:
                        pe.wait_ge(y_added, 1)
                    if i >= 1:
                        pe.wait_ge(pT_ready, i)
                    for b in range(t + 1):
                        for j in range(4):
                            ins = pe.transpose(bank(4 + b, j * P, (j + 1) * P), prob[:, i % 2, j, b * P:(b + 1) * P],
                                               ident[:, :])
                    ins.then_inc(pT_ps, 1)

                def outputs(i):
                    b, t, hf = ITEMS[i]
                    pe.wait_ge(pT_ready, i + 1)
                    if i >= 2:
                        pe.wait_ge(y_added, i)
                    for j in range(4):
                        col = (C_VS + (4 * hf + j) // 4 * HD, C_VW + (4 * hf + j) // 4 * HD, C_VB)[b]
                        for kb in range(t + 1):
                            ins = pe.matmul(bank(6 + i % 2, j * HD, (j + 1) * HD),
                                            probT[:, i % 2, kb, j * P:(j + 1) * P], rows[:, kb, col:col + HD],
                                            start=(kb == 0), stop=(kb == t))
                    ins.then_inc(o_ps, 1)

                n_items = len(ITEMS)
                scores(0)
                pe.wait_ge(hid_ready, 4)
                for half in range(2):
                    ins = pe.matmul(bank(6, 320, 384), hidv[:, half, :], w2[:, 1, half, :], start=(half == 0), stop=(half == 1))
                ins.then_inc(cmp_ps, 1)
                pe.wait_ge(pc_ready, 1)
                for t in range(NT):
                    ins = pe.transpose(bank(6, t * P, t * P + P), pc[:, t, :], ident[:, :])
                ins.then_inc(pcT_ps, 1)
                pe.wait_ge(pcT_ready, 1)
                for t in range(NT):
                    pe.matmul(bank(4 + t), relu[:, 0, t * P:(t + 1) * P], vcblk[:, :, :].rearrange("p h d -> p (h d)"),
                              start=True, stop=True).then_inc(oc_ps, 1)
                for i in range(n_items):
                    if i + 1 < n_items:
                        scores(i + 1)
                    prob_T(i)
                    if i:
                        outputs(i - 1)
                outputs(n_items - 1)
                pe.wait_ge(y_added, n_items + 1)
                for n in range(4):
                    m = n // 2
                    for k in (2 * (n % 2), 2 * (n % 2) + 1):
                        for t in range(NT):
                            ins = pe.transpose(bank(n, (k % 2) * SEQ + t * P, (k % 2) * SEQ + t * P + P),
                                               y[:, m, t, k * P:(k + 1) * P], ident[:, :])
                    ins.then_inc(yT_ps, 1)
                pe.wait_ge(yT_ready, 4)
                for m in range(NK):
                    if m >= 4:
                        pe.wait_ge(br_ready, m - 3)
                    for br in range(2):
                        blk = B_BR + 2 * (m // 2) + br
                        if m % 2 == 0:
                            arrive(blk)
                        wv = block_of(blk).rearrange("p (k c) -> p k c", k=4)
                        for k in range(4):
                            ins = pe.matmul(bank(4 + m % 4, br * SEQ, (br + 1) * SEQ),
                                            wv[:, k, (m % 2) * P:(m % 2 + 1) * P], yT[:, br, k, :],
                                            start=(k == 0), stop=(k == 3))
                            settle(ins)
                    ins.then_inc(br_ps, 1)
                    owed[0] += m % 2

                def streamed(blk, b0, left, nk):
                    for k in range(nk):
                        arrive(blk + k)
                        for n in range(4):
                            t = n // 2
                            ins = pe.matmul(bank(b0 + n), left[:, k, t * P:(t + 1) * P],
                                            block_of(blk + k)[:, (n % 2) * 512:(n % 2) * 512 + 512],
                                            start=(k == 0), stop=(k == nk - 1))
                            settle(ins)
                        if k % 2 and k < nk - 1:
                            ins.then_inc(pair_free, 1)
                    owed[0] += 1
                    return ins

                pe.wait_ge(br_ready, NK)
                streamed(B_OUT, 0, mergedT, NK).then_inc(wo_ps, 1)

                norm_T(1, 4)
                sub = par[:, Q_SUB:Q_SUB + 2 * NKEYS].rearrange("p (s n) -> p s n", s=2)

                def key_scores(h):
                    pe.wait_ge(q_ready, h + 1)
                    for t in range(NT):
                        if h:
                            pe.wait_ge(ks_ready, (h - 1) * NT + t + 1)
                        for s in range(2):
                            ins = pe.matmul(bank(2 + t, s * P, (s + 1) * P), qPT[:, 2 * h + s, t * P:(t + 1) * P],
                                            sub[:, s, :], start=True, stop=True)
                            settle(ins)
                        ins.then_inc(ks_ps, 1)

                for c in range(16):
                    blk = B_WQ + c
                    arrive(blk)
                    if c % 2 == 0 and c >= 4:
                        pe.wait_ge(q_ready, c // 2 - 1)
                    wv = block_of(blk).rearrange("p (k c) -> p k c", k=NK)
                    for k in range(NK):
                        ins = pe.matmul(bank((c // 2) % 2, (c % 2) * SEQ, (c % 2 + 1) * SEQ), wv[:, k, :],
                                        hT[:, k, :], start=(k == 0), stop=(k == NK - 1))
                        settle(ins)
                    if c % 2:
                        ins.then_inc(q_ps, 1)
                        owed[0] += 1
                    if c % 2 and c >= 3:
                        key_scores(c // 2 - 1)
                key_scores(HEADS - 1)
                pe.wait_ge(ks_ready, 2 * HEADS)
                for n in range(4):
                    ins = pe.matmul(bank(n), zero16[:, 0:P], zero16[:, :], start=True, stop=False,
                                    skip_group_check=True)
                    settle(ins)
                first_pair = B_EXP // 2

                def pre_act(b, slot, block):
                    return columns(bank(4 + b, 0, SEQ), slot, block)

                pe.sem_inc(wgt_used, 3)
                pe.wait_ge(hs_lo, 8)
                pe.wait_ge(pair_free, layer * PAIRS + (first_pair + 1))
                for c in range(2):
                    pre_act(c, first_pair % RING, c).then_inc(act_ps, 1)
                pe.wait_ge(picks_ready, 1)
                for w in range(3):
                    for t in range(NT):
                        ins = pe.transpose(bank(6 + w // 2, (w % 2) * SEQ + t * P, (w % 2) * SEQ + t * P + P),
                                           picks[:, w, t, :, :].rearrange("p h k -> p (h k)"), ident[:, :])
                ins.then_inc(pickT_ps, 1)
                pe.wait_ge(pickT_ready, 2)
                pe.sem_inc(g_ps, 2)
                with pe.Fori(0, SEQ // 8) as i:
                    for b in range(2):
                        pe.wait_ge(hot_ready, i * 2 + (b + 1))
                        pe.wait_ge(act_hot_ready, i * 2 + (b + 1))
                        pe.wait_ge(g_ready, i * 2 + (b + 1))
                        for j in range(4):
                            ins = pe.matmul(bank(6 + b, j * P, (j + 1) * P), onehot2[:, b, j, :], onehot1[:, b, j, :],
                                            start=True, stop=True)
                        ins.then_inc(g_ps, 1)

                def product(b, slot, block, last=False):
                    for n in range(4):
                        t = n // 2
                        for s_, m in PASSES:
                            ins = pe.matmul(bank(n), wgt[:, b, s_, t * P:(t + 1) * P],
                                            split[:, slot, block, m, (n % 2) * 512:(n % 2) * 512 + 512],
                                            start=False, stop=last and s_ == 1, skip_group_check=True)
                    return ins

                def chunk(i, j):
                    slot = (first_pair + 1 + j) % RING
                    pe.wait_ge(lo_ready, i * BODY + (j + 1))
                    pe.wait_ge(wgt_ready, i * BODY + (j + 3))
                    product(j % 2, slot, 0).then_inc(wgt_used, 1)
                    pe.wait_ge(pair_free, layer * PAIRS + (i * BODY + (first_pair + j + 2)))
                    return slot

                with pe.Fori(0, NCHUNK // BODY - 1) as i:
                    for j in range(BODY):
                        pre_act(j % 2, chunk(i, j), 1).then_inc(act_ps, 1)
                pe.wait_ge(lo_ready, NCHUNK - 1)
                pe.wait_ge(wgt_ready, NCHUNK + 1)
                product(0, (first_pair + NCHUNK - 1) % RING, 0).then_inc(wgt_used, 1)
                pe.wait_ge(pair_free, layer * PAIRS + (first_pair + NCHUNK))
                pe.wait_ge(wgt_ready, NCHUNK + 2)
                product(1, (first_pair + NCHUNK - 1) % RING, 1, True).then_inc(wgt_used, 1)
                streamed(B_PLEW, 4, pT[:, :].rearrange("p (k t) -> p k t", k=2), 2).then_inc(pw_ps, 1)
                norm_T(2, 0)
                pe.wait_ge(pw_ready, 1)
                streamed(B_PLEG, 4, hT, NK).then_inc(pg_ps, 1)
                for p in range((B_PLEG + 8) // 2, PAIRS):
                    pe.wait_ge(pair_full[p % RING], layer * turns + 16 * (p // RING + 1))
                    owed[0] += 1
                pe.drain().then_inc(pair_free, owed[0])
                pe.drain().then_inc(layer_done, 1)
                pe.wait_ge(layer_go, layer + 1)


def _stream(i):
    import numpy as np

    blocks = np.zeros((DEPTH, PAIRS * 2, P, BLK), np.float32)
    w_in = i["w_in"]
    cuts = [(0, 512), (512 + 256, 512 + 384), (512 + 512, 512 + 640), (1304, 1816), (1816, 1880), (1944, 2456),
            (2456, 2520), (512 + 384, 512 + 512), (512 + 640, 512 + 768), (512, 640), (640, 768), (1880, 1944),
            (1280, 1304), (2520, 2528)]
    for l in range(DEPTH):
        b = blocks[l]
        rows = np.concatenate([w_in[l][:, lo:hi] for lo, hi in cuts], axis=1).reshape(4, 2, P, ROW)
        for cb, (c0, w) in enumerate(ROW_BLOCKS):
            v = b[B_ROW + 4 * cb:B_ROW + 4 * cb + 4].reshape(4, P, 2, 512)
            v[:, :, :, :w] = rows[:, :, :, c0:c0 + w].transpose(0, 2, 1, 3)

        def columns(w):
            return w.reshape(NK, P, -1, P).transpose(2, 1, 0, 3).reshape(-1, P, BLK)

        b[B_GATE:B_GATE + 16] = columns(w_in[l][:, 2528:])
        for v in range(2):
            b[B_W1 + 4 * v:B_W1 + 4 * v + 4] = i["cmp_w1"][l][v].reshape(4, 4, P, 256).transpose(0, 2, 1, 3).reshape(4, P, BLK)
        for m, name in enumerate(("w_branch_a", "w_branch_b")):
            b[B_BR + m:B_BR + 8:2] = i[name][l].reshape(4, P, 4, 256).transpose(2, 1, 0, 3).reshape(4, P, BLK)
        b[B_OUT:B_OUT + 8] = i["w_out"][l].reshape(8, P, D)
        b[B_WQ:B_WQ + 16] = columns(i["peer_wq"][l])
        u = i["peer_u"][l].reshape(NCHUNK, P, NK, P).transpose(0, 3, 2, 1).reshape(NCHUNK, P, BLK)
        v = i["peer_v"][l].reshape(NCHUNK, P, D)
        e = b[B_EXP:B_EXP + 2 * NCHUNK]
        e[0:2] = u[0:2]
        e[2:254:2], e[3:254:2] = v[0:126], u[2:128]
        e[254:256] = v[126:128]
        b[B_PLEW:B_PLEW + 2] = i["ple_w"][l].reshape(2, P, D)
        b[B_PLEG:B_PLEG + 8] = i["ple_gate_w"][l].reshape(8, P, D)
    return np.ascontiguousarray(blocks.reshape(DEPTH * PAIRS, 2, P, BLK).transpose(0, 2, 1, 3))


def _params(i):
    import numpy as np

    par = np.zeros((DEPTH, P, NPARAM), np.float32)
    for l in range(DEPTH):
        q = par[l]
        q[:, Q_GA:Q_GA + NK] = i["attn_norm"][l].reshape(NK, P).T
        q[:, Q_GF:Q_GF + NK] = i["ffn_norm"][l].reshape(NK, P).T
        ga, gd = i["nsa_qk_gain"][l], i["dsa_qk_gain"][l]
        gains = [ga[0]] * 8 + [ga[2]] * 2 + [ga[3]] * 2 + [gd[0]] * 8 + [gd[1]]
        q[:, Q_GAIN:Q_GAIN + NORM_SLOTS * HD] = np.concatenate(gains)[None]
        q[:, Q_CGAIN:Q_CGAIN + HD] = ga[1][None]
        q[:, Q_POS:Q_POS + 32] = i["cmp_pos"][l].reshape(2, 16, 2, HD).transpose(2, 3, 0, 1).reshape(P, 32)
        q[:, Q_W2:Q_W2 + 4 * HD] = i["cmp_w2"][l].reshape(2, 2, P, HD).transpose(2, 0, 1, 3).reshape(P, 4 * HD)
        q[:, Q_SUB:Q_SUB + 2 * NKEYS] = i["peer_sub_keys"][l].transpose(2, 0, 1).reshape(P, 2 * NKEYS)
        q[:, Q_PT:Q_PT + 2 * SEQ] = i["p"][l, 0].T.reshape(2, P, SEQ).transpose(1, 0, 2).reshape(P, 2 * SEQ)
        q[:, Q_PLEN:Q_PLEN + D] = i["ple_norm"][l][None]
    return par


def kernel(**inputs):
    import numpy as np
    import concourse.bacc as bacc
    from concourse.bass_utils import run_bass_kernel_spmd as run

    i = {k: np.asarray(v) for k, v in inputs.items()}
    pos = np.ascontiguousarray(i["positions"])
    posl = np.zeros((P, 3), pos.dtype)
    posl[:, 0:2] = pos[0].reshape(2, P).T
    for gr in range(2):
        posl[gr * CP:gr * CP + NCMP, 2] = pos[0, CMP_LEN - 1::CMP_STRIDE][:NCMP]
    inv = (np.float32(500000.0) ** (-np.arange(ROT2, dtype=np.float32) / ROT2)).astype(np.float32)
    arrays = {
        "in_x": np.ascontiguousarray(i["x"]),
        "in_stream": _stream(i),
        "in_params": _params(i),
        "in_positions": posl,
        "in_inv_freq": np.ascontiguousarray(np.broadcast_to(inv, (P, ROT2))),
    }
    nc = bacc.Bacc("TRN2", target_bir_lowering=False, num_devices=1, dynamic_dma_scratch_size=256)
    args = [nc.dram_tensor(n, a.shape, mybir.dt.from_np(a.dtype), kind="ExternalInput").ap() for n, a in arrays.items()]
    o = nc.dram_tensor("out_0", (1, SEQ, D), F32, kind="ExternalOutput").ap()
    build(nc, *args, o)
    r = run(nc, [arrays], core_ids=[0])
    return r.results[0]["out_0"]
```
